# Optimizing a Trainium2 kernel written in Bass

```python
import math
import jax, jax.numpy as jnp
from jax import lax
import numpy as np
import jax
import jax.numpy as jnp

D_MODEL = 1024
BATCH = 1
SEQ = 512
DEPTH = 1

MEM_LEN = 256
ATTN_HEADS = 16
ATTN_KV_HEADS = 4
HEAD_DIM = 64
WINDOW = 128
BLOCK = 128
SSD_EXPAND = 2
D_INNER = SSD_EXPAND * D_MODEL
SSD_HEAD_DIM = 64
SSD_HEADS = D_INNER // SSD_HEAD_DIM
SSD_GROUPS = 8
D_STATE = 128
CONV_K = 5
CHUNK = 128
X_HEADS = 4
X_HEAD_DIM = 128
D_FF = 4 * D_MODEL
EPS = 1e-6

Q_W = ATTN_HEADS * HEAD_DIM
KV_W = ATTN_KV_HEADS * HEAD_DIM
BC_W = SSD_GROUPS * D_STATE
XBC_W = D_INNER + 2 * BC_W
DT_W = 2 * SSD_HEADS
GATE_W = 2 * D_MODEL
OFF_K = Q_W
OFF_V = OFF_K + KV_W
OFF_Z = OFF_V + KV_W
OFF_XBC = OFF_Z + D_INNER
OFF_DT = OFF_XBC + XBC_W
OFF_GATE = OFF_DT + DT_W
D_IN_PROJ = OFF_GATE + GATE_W


def rmsnorm(x, g):
    xf = x.astype(jnp.float32)
    y = xf * lax.rsqrt(jnp.mean(xf * xf, axis=-1, keepdims=True) + EPS)
    return (y * g.astype(jnp.float32)).astype(x.dtype)

def alibi_slopes(n_heads):
    return jnp.asarray(np.array([2.0 ** (-8.0 * (h + 1) / n_heads) for h in range(n_heads)], dtype=np.float32))

def windowed_gqa_sink(q, k, v, sink):
    b, l, H, d = q.shape
    kvh = k.shape[2]
    r = H // kvh
    nb = l // BLOCK
    qb = q.reshape(b, nb, BLOCK, kvh, r, d)
    pad = ((0, 0), (BLOCK, BLOCK), (0, 0), (0, 0))
    kp = jnp.pad(k, pad).reshape(b, nb + 2, BLOCK, kvh, d)
    vp = jnp.pad(v, pad).reshape(b, nb + 2, BLOCK, kvh, d)
    kw = jnp.concatenate([kp[:, :-2], kp[:, 1:-1], kp[:, 2:]], axis=2)
    vw = jnp.concatenate([vp[:, :-2], vp[:, 1:-1], vp[:, 2:]], axis=2)
    a_idx = np.arange(BLOCK)[:, None]
    w_idx = np.arange(3 * BLOCK)[None, :]
    rel = BLOCK + a_idx - w_idx
    in_band = np.abs(rel) <= WINDOW
    spos = (np.arange(nb)[:, None] - 1) * BLOCK + np.arange(3 * BLOCK)[None, :]
    valid = (spos >= 0) & (spos < l)
    mask = in_band[None] & valid[:, None, :]
    slopes = alibi_slopes(H).reshape(kvh, r, 1, 1)
    alibi = -slopes * jnp.asarray(np.abs(rel), jnp.float32)
    bias = jnp.where(jnp.asarray(mask)[:, None, None], alibi[None], -jnp.inf)
    s = jnp.einsum('bnqgrd,bnkgd->bngrqk', qb, kw).astype(jnp.float32) * (d ** -0.5) + bias[None]
    sink_f = sink.astype(jnp.float32).reshape(1, 1, kvh, r, 1, 1)
    m = jnp.maximum(jnp.max(s, axis=-1, keepdims=True), sink_f)
    p = jnp.exp(s - m)
    denom = jnp.sum(p, axis=-1, keepdims=True) + jnp.exp(sink_f - m)
    o = jnp.einsum('bngrqk,bnkgd->bnqgrd', (p / denom).astype(v.dtype), vw)
    return o.reshape(b, l, H * d)

def segsum_exp(a):
    T = a.shape[-1]
    cs = jnp.cumsum(a, axis=-1)
    diff = cs[..., :, None] - cs[..., None, :]
    tri = jnp.asarray(np.tril(np.ones((T, T), dtype=bool)))
    return jnp.where(tri, jnp.exp(jnp.where(tri, diff, 0.0)), 0.0)

def ssd_chunked(x, dt, A, Bm, Cm):
    b, l, H, P = x.shape
    G, N = Bm.shape[2], Bm.shape[3]
    r = H // G
    c = l // CHUNK
    xdt = (x * dt[..., None]).reshape(b, c, CHUNK, G, r, P)
    adt = jnp.moveaxis((dt * A).reshape(b, c, CHUNK, G, r), 2, -1)
    Bc = Bm.reshape(b, c, CHUNK, G, N)
    Cc = Cm.reshape(b, c, CHUNK, G, N)
    a_cs = jnp.cumsum(adt, axis=-1)
    CB = jnp.einsum('bclgn,bcsgn->bcgls', Cc, Bc)
    Wd = CB[:, :, :, None] * segsum_exp(adt)
    y_diag = jnp.einsum('bcgrls,bcsgrp->bclgrp', Wd, xdt)
    decay_states = jnp.exp(a_cs[..., -1:] - a_cs)
    states = jnp.einsum('bcsgn,bcgrs,bcsgrp->bcgrpn', Bc, decay_states, xdt)
    chunk_decay = jnp.exp(a_cs[..., -1])

    def step(carry, inp):
        st, dec = inp
        return carry * dec[..., None, None] + st, carry

    init = jnp.zeros((b, G, r, P, N), jnp.float32)
    _, prev = lax.scan(step, init, (jnp.moveaxis(states, 1, 0), jnp.moveaxis(chunk_decay, 1, 0)))
    prev = jnp.moveaxis(prev, 0, 1)
    y_off = jnp.einsum('bclgn,bcgrpn,bcgrl->bclgrp', Cc, prev, jnp.exp(a_cs))
    return (y_diag + y_off).reshape(b, l, H, P)

def depthwise_conv_centred(u, w, bias):
    out = lax.conv_general_dilated(u, w[:, None, :].astype(u.dtype), window_strides=(1,),
                                   padding=[(CONV_K // 2, CONV_K // 2)],
                                   dimension_numbers=('NWC', 'WIO', 'NWC'),
                                   feature_group_count=u.shape[-1])
    return out + bias.astype(u.dtype)

def ssd_branch(z, xbc, dt_raw, conv_w, conv_b, dt_bias, a_log, d_skip, norm_g):
    b, l, _ = z.shape
    f32 = jnp.float32
    xbc = jax.nn.silu(depthwise_conv_centred(xbc, conv_w, conv_b)).astype(f32)
    xs = xbc[..., :D_INNER].reshape(b, l, SSD_HEADS, SSD_HEAD_DIM)
    Bm = xbc[..., D_INNER:D_INNER + BC_W].reshape(b, l, SSD_GROUPS, D_STATE)
    Cm = xbc[..., D_INNER + BC_W:].reshape(b, l, SSD_GROUPS, D_STATE)
    A = -jnp.exp(a_log.astype(f32))
    dt = jax.nn.softplus(dt_raw.astype(f32).reshape(b, l, 2, SSD_HEADS) + dt_bias.astype(f32))
    y_fwd = ssd_chunked(xs, dt[:, :, 0], A[0], Bm, Cm)
    fl = lambda t: jnp.flip(t, axis=1)
    y_bwd = fl(ssd_chunked(fl(xs), fl(dt[:, :, 1]), A[1], fl(Bm), fl(Cm)))
    y = y_fwd + y_bwd + d_skip.astype(f32)[:, None] * xs
    y = y.reshape(b, l, D_INNER) * jax.nn.silu(z.astype(f32))
    yg = y.reshape(b, l, SSD_GROUPS, D_INNER // SSD_GROUPS)
    yg = yg * lax.rsqrt(jnp.mean(yg * yg, axis=-1, keepdims=True) + EPS)
    y = yg.reshape(b, l, D_INNER) * norm_g.astype(f32)
    return y.astype(z.dtype)

def cross_attention(h, mem_n, w_q, w_kv, w_o):
    b, l, _ = h.shape
    m = mem_n.shape[1]
    q = (h @ w_q).reshape(b, l, X_HEADS, X_HEAD_DIM)
    kv = mem_n @ w_kv
    k = kv[..., :X_HEADS * X_HEAD_DIM].reshape(b, m, X_HEADS, X_HEAD_DIM)
    v = kv[..., X_HEADS * X_HEAD_DIM:].reshape(b, m, X_HEADS, X_HEAD_DIM)
    s = jnp.einsum('blhd,bmhd->bhlm', q, k).astype(jnp.float32) * (X_HEAD_DIM ** -0.5)
    p = jax.nn.softmax(s, axis=-1)
    o = jnp.einsum('bhlm,bmhd->blhd', p.astype(v.dtype), v).reshape(b, l, X_HEADS * X_HEAD_DIM)
    return o @ w_o

def first_inputs(seed: int = 0) -> dict:
    key = jax.random.key(seed)
    ks = iter(jax.random.split(key, 32))
    f32 = jnp.float32

    def dense(shape, fan_in):
        return jax.random.normal(next(ks), shape, f32) * (fan_in ** -0.5)

    def gain(shape):
        return 1.0 + 0.02 * jax.random.normal(next(ks), shape, f32)

    x = jax.random.normal(next(ks), (BATCH, SEQ, D_MODEL), f32)
    mem = jax.random.normal(next(ks), (BATCH, MEM_LEN, D_MODEL), f32)
    norm_mix = gain((DEPTH, D_MODEL))
    w_in = dense((DEPTH, D_MODEL, D_IN_PROJ), D_MODEL)
    attn_sink = 0.1 * jax.random.normal(next(ks), (DEPTH, ATTN_HEADS), f32)
    conv_w = dense((DEPTH, CONV_K, XBC_W), CONV_K)
    conv_b = 0.01 * jax.random.normal(next(ks), (DEPTH, XBC_W), f32)
    dt0 = jnp.exp(jax.random.uniform(next(ks), (DEPTH, 2, SSD_HEADS), f32,
                                     minval=math.log(1e-3), maxval=math.log(1e-1)))
    dt_bias = dt0 + jnp.log(-jnp.expm1(-dt0))
    a_log = jnp.log(jax.random.uniform(next(ks), (DEPTH, 2, SSD_HEADS), f32, minval=1.0, maxval=16.0))
    d_skip = gain((DEPTH, SSD_HEADS))
    ssd_norm = gain((DEPTH, D_INNER))
    w_attn_branch = dense((DEPTH, Q_W, D_MODEL), Q_W)
    w_ssd_branch = dense((DEPTH, D_INNER, D_MODEL), D_INNER)
    w_out = dense((DEPTH, D_MODEL, D_MODEL), D_MODEL)
    norm_cross = gain((DEPTH, D_MODEL))
    norm_mem = gain((DEPTH, D_MODEL))
    w_xq = dense((DEPTH, D_MODEL, X_HEADS * X_HEAD_DIM), D_MODEL)
    w_xkv = dense((DEPTH, D_MODEL, 2 * X_HEADS * X_HEAD_DIM), D_MODEL)
    w_xo = dense((DEPTH, X_HEADS * X_HEAD_DIM, D_MODEL), X_HEADS * X_HEAD_DIM)
    norm_ffn = gain((DEPTH, D_MODEL))
    w_up = dense((DEPTH, D_MODEL, D_FF), D_MODEL)
    w_down = dense((DEPTH, D_FF, D_MODEL), D_FF)
    norm_final = gain((D_MODEL,))
    return {"x": x, "mem": mem, "norm_mix": norm_mix, "w_in": w_in, "attn_sink": attn_sink,
            "conv_w": conv_w, "conv_b": conv_b, "dt_bias": dt_bias, "a_log": a_log,
            "d_skip": d_skip, "ssd_norm": ssd_norm, "w_attn_branch": w_attn_branch,
            "w_ssd_branch": w_ssd_branch, "w_out": w_out, "norm_cross": norm_cross,
            "norm_mem": norm_mem, "w_xq": w_xq, "w_xkv": w_xkv, "w_xo": w_xo,
            "norm_ffn": norm_ffn, "w_up": w_up, "w_down": w_down, "norm_final": norm_final}

def first_block(x, mem, norm_mix, w_in, attn_sink, conv_w, conv_b, dt_bias, a_log, d_skip,
              ssd_norm, w_attn_branch, w_ssd_branch, w_out, norm_cross, norm_mem, w_xq,
              w_xkv, w_xo, norm_ffn, w_up, w_down, norm_final):
    b, l, _ = x.shape
    for i in range(DEPTH):
        h = rmsnorm(x, norm_mix[i])
        proj = h @ w_in[i]
        q = proj[..., :OFF_K].reshape(b, l, ATTN_HEADS, HEAD_DIM)
        k = proj[..., OFF_K:OFF_V].reshape(b, l, ATTN_KV_HEADS, HEAD_DIM)
        v = proj[..., OFF_V:OFF_Z].reshape(b, l, ATTN_KV_HEADS, HEAD_DIM)
        z = proj[..., OFF_Z:OFF_XBC]
        xbc = proj[..., OFF_XBC:OFF_DT]
        dt_raw = proj[..., OFF_DT:OFF_GATE]
        gate_a = proj[..., OFF_GATE:OFF_GATE + D_MODEL]
        gate_b = proj[..., OFF_GATE + D_MODEL:]
        attn = windowed_gqa_sink(q, k, v, attn_sink[i])
        ssd = ssd_branch(z, xbc, dt_raw, conv_w[i], conv_b[i], dt_bias[i], a_log[i],
                         d_skip[i], ssd_norm[i])
        merged = (jax.nn.sigmoid(gate_a) * (attn @ w_attn_branch[i])
                  + jax.nn.sigmoid(gate_b) * (ssd @ w_ssd_branch[i]))
        x = x + merged @ w_out[i]
        h = rmsnorm(x, norm_cross[i])
        x = x + cross_attention(h, rmsnorm(mem, norm_mem[i]), w_xq[i], w_xkv[i], w_xo[i])
        h = rmsnorm(x, norm_ffn[i])
        x = x + jnp.square(jax.nn.relu(h @ w_up[i])) @ w_down[i]
    return rmsnorm(x, norm_final)


CHUNK_2 = 64
ROPE_THETA = 10000.0
A_HEADS = 8
A_DK = 64
A_DV = 64
CONV_K_2 = 4
B_HEADS = 8
B_KV_HEADS = 2
B_HD = 64
IDX_HEADS = 8
IDX_HD = 64
TOPK_MAX = 256
N_GROUPS = 4
EXPERTS_PER_GROUP = 4
N_EXPERTS = N_GROUPS * EXPERTS_PER_GROUP
TOPK_IN_GROUP = 2
D_EXPERT = 256

A_QK_W = A_HEADS * A_DK
A_V_W = A_HEADS * A_DV
B_Q_W = B_HEADS * B_HD
B_KV_W = B_KV_HEADS * B_HD
CONV_W = 2 * A_QK_W + A_V_W
IN_SPLITS = (
    ("a_q", A_QK_W), ("a_k", A_QK_W), ("a_v", A_V_W), ("a_z", A_V_W),
    ("a_beta", A_HEADS), ("a_alpha", A_HEADS),
    ("b_q", B_Q_W), ("b_k", B_KV_W), ("b_v", B_KV_W),
    ("i_q", IDX_HEADS * IDX_HD), ("i_k", IDX_HD), ("i_w", IDX_HEADS),
    ("gate_a", D_MODEL), ("gate_b", D_MODEL),
)
D_IN = sum(n for _, n in IN_SPLITS)


def rmsnorm_2(x, g):
    xf = x.astype(jnp.float32)
    y = xf * lax.rsqrt(jnp.mean(xf * xf, axis=-1, keepdims=True) + EPS)
    return (y * g.astype(jnp.float32)).astype(x.dtype)

def l2norm(x):
    xf = x.astype(jnp.float32)
    return xf * lax.rsqrt(jnp.sum(xf * xf, axis=-1, keepdims=True) + EPS)

def split_cols(z):
    parts, off = {}, 0
    for name, n in IN_SPLITS:
        parts[name] = z[..., off:off + n]
        off += n
    return parts

def rope(x, pos):
    half = x.shape[-1] // 2
    inv = ROPE_THETA ** (-jnp.arange(half, dtype=jnp.float32) / half)
    ang = pos.astype(jnp.float32)[..., None] * inv
    cos = jnp.cos(ang)[:, :, None, :]
    sin = jnp.sin(ang)[:, :, None, :]
    xf = x.astype(jnp.float32)
    x1, x2 = xf[..., :half], xf[..., half:]
    return jnp.concatenate([x1 * cos - x2 * sin, x2 * cos + x1 * sin], axis=-1).astype(x.dtype)

def causal_dwconv(x, w):
    c = x.shape[-1]
    return lax.conv_general_dilated(
        x, w[:, None, :].astype(x.dtype), window_strides=(1,), padding=[(CONV_K_2 - 1, 0)],
        dimension_numbers=("NWC", "WIO", "NWC"), feature_group_count=c)

def gated_delta_rule(q, k, v, g, beta):
    b, s, h, dk = q.shape
    dv = v.shape[-1]
    n = s // CHUNK_2

    def chunks(t):
        return jnp.moveaxis(t.reshape((b, n, CHUNK_2, h) + t.shape[3:]), 3, 1)

    qc, kc, vc, gc, bc = chunks(q), chunks(k), chunks(v), chunks(g), chunks(beta)
    G = jnp.cumsum(gc, axis=-1)
    idx = jnp.arange(CHUNK_2)
    incl = idx[:, None] >= idx[None, :]
    strict = idx[:, None] > idx[None, :]
    decay = jnp.exp(jnp.where(incl, G[..., :, None] - G[..., None, :], -jnp.inf))
    kk = jnp.einsum("bhnid,bhnjd->bhnij", kc, kc)
    a_mat = jnp.where(strict, bc[..., :, None] * kk * decay, 0.0) + jnp.eye(CHUNK_2, dtype=jnp.float32)
    rhs = jnp.concatenate([vc * bc[..., None], kc * (bc * jnp.exp(G))[..., None]], axis=-1)
    sol = lax.linalg.triangular_solve(a_mat, rhs, left_side=True, lower=True, unit_diagonal=True)
    u, w = sol[..., :dv], sol[..., dv:]
    qk = jnp.einsum("bhnid,bhnjd->bhnij", qc, kc) * decay
    q_dec = qc * jnp.exp(G)[..., None]
    k_dec = kc * jnp.exp(G[..., -1:] - G)[..., None]
    g_last = jnp.exp(G[..., -1])

    def step(state, xs):
        u_n, w_n, q_n, qk_n, k_n, gl_n = xs
        v_new = u_n - jnp.einsum("bhck,bhkv->bhcv", w_n, state)
        o_n = jnp.einsum("bhck,bhkv->bhcv", q_n, state) + jnp.einsum("bhij,bhjv->bhiv", qk_n, v_new)
        state = state * gl_n[..., None, None] + jnp.einsum("bhck,bhcv->bhkv", k_n, v_new)
        return state, o_n

    xs = tuple(jnp.moveaxis(t, 2, 0) for t in (u, w, q_dec, qk, k_dec, g_last))
    s0 = jnp.zeros((b, h, dk, dv), jnp.float32)
    _, o = lax.scan(step, s0, xs)
    return jnp.transpose(o, (1, 0, 3, 2, 4)).reshape(b, s, h, dv)

def dsa_attention(q, k, v, qi, ki, wi):
    b, s, hq, d = q.shape
    hk = k.shape[2]
    grp = hq // hk
    n = s // CHUNK_2
    topk = min(TOPK_MAX, s // 4)
    kf = k.reshape(b, s, hk * d)
    vf = v.reshape(b, s, hk * d)
    kif = ki.astype(jnp.float32)
    key_pos = jnp.arange(s)
    gather = jax.vmap(lambda table, ids: table[ids])

    def to_blocks(t):
        return jnp.moveaxis(t.reshape((b, n, CHUNK_2) + t.shape[2:]), 1, 0)

    def block(args):
        q_b, qi_b, wi_b, blk = args
        limit = (blk + 1) * CHUNK_2
        rel = jax.nn.relu(jnp.einsum("bthd,bsd->bths", qi_b.astype(jnp.float32), kif))
        score = jnp.einsum("bth,bths->bts", wi_b.astype(jnp.float32), rel)
        score = jnp.where(key_pos < limit, score, -jnp.inf)
        _, sel = lax.top_k(score, topk)
        valid = sel < limit
        ks = gather(kf, sel).reshape(b, CHUNK_2, topk, hk, d)
        vs = gather(vf, sel).reshape(b, CHUNK_2, topk, hk, d)
        qg = q_b.reshape(b, CHUNK_2, hk, grp, d)
        logits = jnp.einsum("btkgd,btjkd->btkgj", qg, ks).astype(jnp.float32) * (d ** -0.5)
        logits = jnp.where(valid[:, :, None, None, :], logits, -jnp.inf)
        p = jax.nn.softmax(logits, axis=-1).astype(v.dtype)
        o = jnp.einsum("btkgj,btjkd->btkgd", p, vs)
        return o.reshape(b, CHUNK_2, hq * d)

    out = lax.map(block, (to_blocks(q), to_blocks(qi), to_blocks(wi), jnp.arange(n)))
    return jnp.moveaxis(out, 0, 1).reshape(b, s, hq * d)

def hier_moe(h, w_rg, b_rg, w_re, b_re, w1, w3, w2):
    bsz, s, d = h.shape
    xt = h.reshape(-1, d)
    glog = (xt @ w_rg + b_rg).astype(jnp.float32)
    gp = jax.nn.softmax(glog, axis=-1)
    gsel = jnp.argmax(glog, axis=-1)
    ggate = jnp.take_along_axis(gp, gsel[:, None], axis=-1)
    elog = (xt @ w_re + b_re).astype(jnp.float32).reshape(-1, N_GROUPS, EXPERTS_PER_GROUP)
    elog_g = jnp.take_along_axis(elog, gsel[:, None, None], axis=1)[:, 0]
    ep = jax.nn.softmax(elog_g, axis=-1)
    top_p, top_i = lax.top_k(ep, TOPK_IN_GROUP)
    top_p = top_p / jnp.sum(top_p, axis=-1, keepdims=True)
    wts = ggate * top_p
    eid = gsel[:, None] * EXPERTS_PER_GROUP + top_i
    comb = jnp.sum(jax.nn.one_hot(eid, N_EXPERTS, dtype=jnp.float32) * wts[..., None], axis=1)
    act = jax.nn.silu(jnp.einsum("nd,edf->nef", xt, w1)) * jnp.einsum("nd,edf->nef", xt, w3)
    act = act * comb[:, :, None].astype(act.dtype)
    y = jnp.einsum("nef,efd->nd", act, w2)
    return y.reshape(bsz, s, d)

def second_inputs(seed: int = 0) -> dict:
    key = jax.random.key(seed)
    ks = jax.random.split(key, 24)
    f32 = jnp.float32

    def nrm(k, shape, fan):
        return jax.random.normal(k, shape, f32) * (fan ** -0.5)

    def gain(k, shape):
        return 1.0 + 0.02 * jax.random.normal(k, shape, f32)

    x = jax.random.normal(ks[0], (BATCH, SEQ, D_MODEL), f32)
    offs = jax.random.randint(ks[1], (BATCH, 1), 0, 64) * CHUNK_2
    positions = (offs + jnp.arange(SEQ, dtype=jnp.int32)[None, :]).astype(jnp.int32)
    norm1_g = gain(ks[2], (DEPTH, D_MODEL))
    w_in = nrm(ks[3], (DEPTH, D_MODEL, D_IN), D_MODEL)
    b_gate = 0.02 * jax.random.normal(ks[4], (DEPTH, 2 * D_MODEL), f32)
    conv_w = nrm(ks[5], (DEPTH, CONV_K_2, CONV_W), CONV_K_2)
    a_log = jnp.log(jax.random.uniform(ks[6], (DEPTH, A_HEADS), f32, 1.0, 16.0))
    dt = jnp.exp(jax.random.uniform(ks[7], (DEPTH, A_HEADS), f32, math.log(1e-3), math.log(1e-1)))
    dt_bias = dt + jnp.log(-jnp.expm1(-dt))
    a_norm_g = gain(ks[8], (DEPTH, A_DV))
    w_proj_a = nrm(ks[9], (DEPTH, A_V_W, D_MODEL), A_V_W)
    w_proj_b = nrm(ks[10], (DEPTH, B_Q_W, D_MODEL), B_Q_W)
    w_out = nrm(ks[11], (DEPTH, D_MODEL, D_MODEL), D_MODEL)
    norm2_g = gain(ks[12], (DEPTH, D_MODEL))
    w_router_group = nrm(ks[13], (DEPTH, D_MODEL, N_GROUPS), D_MODEL)
    b_router_group = 0.01 * jax.random.normal(ks[14], (DEPTH, N_GROUPS), f32)
    w_router_expert = nrm(ks[15], (DEPTH, D_MODEL, N_EXPERTS), D_MODEL)
    b_router_expert = 0.01 * jax.random.normal(ks[16], (DEPTH, N_EXPERTS), f32)
    w_exp_gate = nrm(ks[17], (DEPTH, N_EXPERTS, D_MODEL, D_EXPERT), D_MODEL)
    w_exp_up = nrm(ks[18], (DEPTH, N_EXPERTS, D_MODEL, D_EXPERT), D_MODEL)
    w_exp_down = nrm(ks[19], (DEPTH, N_EXPERTS, D_EXPERT, D_MODEL), D_EXPERT)
    final_norm_g = gain(ks[20], (D_MODEL,))
    return {
        "x": x, "positions": positions, "norm1_g": norm1_g, "w_in": w_in, "b_gate": b_gate,
        "conv_w": conv_w, "a_log": a_log, "dt_bias": dt_bias, "a_norm_g": a_norm_g,
        "w_proj_a": w_proj_a, "w_proj_b": w_proj_b, "w_out": w_out, "norm2_g": norm2_g,
        "w_router_group": w_router_group, "b_router_group": b_router_group,
        "w_router_expert": w_router_expert, "b_router_expert": b_router_expert,
        "w_exp_gate": w_exp_gate, "w_exp_up": w_exp_up, "w_exp_down": w_exp_down,
        "final_norm_g": final_norm_g,
    }

def second_block(x, positions, norm1_g, w_in, b_gate, conv_w, a_log, dt_bias, a_norm_g,
              w_proj_a, w_proj_b, w_out, norm2_g, w_router_group, b_router_group,
              w_router_expert, b_router_expert, w_exp_gate, w_exp_up, w_exp_down, final_norm_g):
    b, s, _ = x.shape
    for l in range(DEPTH):
        h = rmsnorm_2(x, norm1_g[l])
        parts = split_cols(h @ w_in[l])

        qkv = jnp.concatenate([parts["a_q"], parts["a_k"], parts["a_v"]], axis=-1)
        qkv = jax.nn.silu(causal_dwconv(qkv, conv_w[l]))
        aq = l2norm(qkv[..., :A_QK_W].reshape(b, s, A_HEADS, A_DK)) * (A_DK ** -0.5)
        ak = l2norm(qkv[..., A_QK_W:2 * A_QK_W].reshape(b, s, A_HEADS, A_DK))
        av = qkv[..., 2 * A_QK_W:].reshape(b, s, A_HEADS, A_DV).astype(jnp.float32)
        beta = jax.nn.sigmoid(parts["a_beta"].astype(jnp.float32))
        g = -jnp.exp(a_log[l].astype(jnp.float32)) * jax.nn.softplus(
            parts["a_alpha"].astype(jnp.float32) + dt_bias[l].astype(jnp.float32))
        o_a = gated_delta_rule(aq, ak, av, g, beta)
        o_a = rmsnorm_2(o_a, a_norm_g[l]) * jax.nn.silu(
            parts["a_z"].reshape(b, s, A_HEADS, A_DV).astype(jnp.float32))
        o_a = o_a.reshape(b, s, A_V_W).astype(x.dtype)

        bq = rope(parts["b_q"].reshape(b, s, B_HEADS, B_HD), positions)
        bk = rope(parts["b_k"].reshape(b, s, B_KV_HEADS, B_HD), positions)
        bv = parts["b_v"].reshape(b, s, B_KV_HEADS, B_HD)
        iq = rope(parts["i_q"].reshape(b, s, IDX_HEADS, IDX_HD), positions)
        ik = rope(parts["i_k"][:, :, None, :], positions)[:, :, 0, :]
        iw = parts["i_w"] * ((IDX_HEADS ** -0.5) * (IDX_HD ** -0.5))
        o_b = dsa_attention(bq, bk, bv, iq, ik, iw)

        gate_a = jax.nn.sigmoid(parts["gate_a"] + b_gate[l][:D_MODEL])
        gate_b = jax.nn.sigmoid(parts["gate_b"] + b_gate[l][D_MODEL:])
        merged = gate_a * (o_a @ w_proj_a[l]) + gate_b * (o_b @ w_proj_b[l])
        x = x + merged @ w_out[l]

        x = x + hier_moe(rmsnorm_2(x, norm2_g[l]), w_router_group[l], b_router_group[l],
                         w_router_expert[l], b_router_expert[l],
                         w_exp_gate[l], w_exp_up[l], w_exp_down[l])
    return rmsnorm_2(x, final_norm_g)


def setup_inputs(seed=0):
    out = dict(first_inputs(seed))
    for name, value in second_inputs(seed + 1).items():
        if name != "x":
            out[name + "_2"] = value
    return out


def reference(
    x, mem, norm_mix, w_in, attn_sink, conv_w, conv_b, dt_bias, a_log, d_skip, ssd_norm,
    w_attn_branch, w_ssd_branch, w_out, norm_cross, norm_mem, w_xq, w_xkv, w_xo, norm_ffn, w_up,
    w_down, norm_final, positions_2, norm1_g_2, w_in_2, b_gate_2, conv_w_2, a_log_2, dt_bias_2,
    a_norm_g_2, w_proj_a_2, w_proj_b_2, w_out_2, norm2_g_2, w_router_group_2, b_router_group_2,
    w_router_expert_2, b_router_expert_2, w_exp_gate_2, w_exp_up_2, w_exp_down_2,
    final_norm_g_2,
):
    x = first_block(
        x, mem, norm_mix, w_in, attn_sink, conv_w, conv_b, dt_bias, a_log, d_skip, ssd_norm,
        w_attn_branch, w_ssd_branch, w_out, norm_cross, norm_mem, w_xq, w_xkv, w_xo, norm_ffn,
        w_up, w_down, norm_final,
    )
    return second_block(
        x, positions_2, norm1_g_2, w_in_2, b_gate_2, conv_w_2, a_log_2, dt_bias_2, a_norm_g_2,
        w_proj_a_2, w_proj_b_2, w_out_2, norm2_g_2, w_router_group_2, b_router_group_2,
        w_router_expert_2, b_router_expert_2, w_exp_gate_2, w_exp_up_2, w_exp_down_2,
        final_norm_g_2,
    )


_drawn_inputs = setup_inputs


def setup_inputs(seed=0):
    import zlib

    import numpy as np

    out = dict(_drawn_inputs(seed))
    spreads = {}
    factors = {'attn_sink': 7.432,
     'conv_b': 2.708,
     'd_skip': 3.666,
     'norm_cross': 5.583,
     'norm_mem': 5.48,
     'b_gate_2': 5.098,
     'a_norm_g_2': 3.445,
     'b_router_group_2': 27.217,
     'b_router_expert_2': 12.046,
     'final_norm_g_2': 8.0,
     'norm_ffn': 3.907,
     'norm2_g_2': 3.138}
    for name, (base, spread) in spreads.items():
        noise = np.random.default_rng([zlib.crc32(name.encode()), seed]).standard_normal(out[name].shape)
        drawn = base * np.exp(spread * noise) if base else spread * noise
        out[name] = jnp.asarray(drawn.astype(out[name].dtype))
    for name, factor in factors.items():
        out[name] = (out[name] * factor).astype(out[name].dtype)
    return out
```

```python
from contextlib import ExitStack

import numpy as np
import concourse.bass as bass
from concourse import mybir

ALU = mybir.AluOpType
ACT = mybir.ActivationFunctionType
F32 = mybir.dt.float32
I32 = mybir.dt.int32
AX = mybir.AxisListType

P = 128
T = 512
NT = T // P
D = 1024
DC = D // P
BANK = 512
EPS = 1e-6
NEG = -1e30

MEM = 256
HEADS, KV_HEADS, HD = 16, 4, 64
D_INNER, SSD_HEADS, GROUPS, D_STATE, TAPS = 2048, 32, 8, 128, 5
GH = SSD_HEADS // GROUPS
GW = D_INNER // GROUPS
X_HEADS, XD = 4, 128
D_FF = 4096
OFF_K = HEADS * HD
OFF_V = OFF_K + KV_HEADS * HD
OFF_Z = OFF_V + KV_HEADS * HD
OFF_XBC = OFF_Z + D_INNER
OFF_DT = OFF_XBC + D_INNER + 2 * GROUPS * D_STATE
OFF_GATE = OFF_DT + 2 * SSD_HEADS

AH, AD, TAPS_2 = 8, 64, 4
BH, BKV = 8, 2
IH = 8
TOPK = min(256, T // 4)
CAUSAL = 64
EXPERTS, EG, DE = 16, 4, 256
OFF2 = {}
_at = 0
for _name, _n in (("a_q", 512), ("a_k", 512), ("a_v", 512), ("a_z", 512), ("a_beta", 8), ("a_alpha", 8),
                  ("b_q", 512), ("b_k", 128), ("b_v", 128), ("i_q", 512), ("i_k", 64), ("i_w", 8),
                  ("gate_a", 1024), ("gate_b", 1024)):
    OFF2[_name] = _at
    _at += _n
ROPE_INV = (np.float32(10000.0) ** (-np.arange(32, dtype=np.float32) / np.float32(32))).astype(np.float32)


class Counter:

    def __init__(self, sem):
        self.sem, self.base = sem, 0

    def at(self, n):
        return self.base + n


class Core:

    def __init__(self, nc, ctx):
        self.nc, self.ctx = nc, ctx
        self.ps = ctx.enter_context(nc.psum_tensor("ps", [P, 8, BANK], F32))
        self.ring = ctx.enter_context(nc.sbuf_tensor("ring", [P, 2, 4096], F32))
        self.arena_size = 44800
        self.arena = ctx.enter_context(nc.sbuf_tensor("arena", [P, self.arena_size], F32))
        self.top = 0
        self.landed = [self.count(f"weights_landed_{s}") for s in range(2)]
        self.unit_ready = self.count("product_ready")
        self.unit_taken = {e: self.count(f"product_stored_{e}") for e in ("act", "dve")}
        self.slots = 0
        self.units = 0
        self.landed_count = [0, 0]
        self.taken_count = {"act": 0, "dve": 0}
        self.per_slot_before, self.on_before = (4, 4), "act"
        self.fence = {e: self.count(f"stage_done_{e}") for e in ("pe", "act", "dve", "pool")}
        self.fences = 0

    def count(self, name):
        return Counter(self.ctx.enter_context(self.nc.semaphore(name)))

    def take(self, *shape):
        n = int(np.prod(shape))
        assert self.top + n <= self.arena_size, (self.top, n)
        v = self.arena[:, self.top:self.top + n]
        self.top += n
        if len(shape) == 2:
            v = v.rearrange("p (a b) -> p a b", a=shape[0])
        elif len(shape) == 3:
            v = v.rearrange("p (a b c) -> p a b c", a=shape[0], b=shape[1])
        elif len(shape) == 4:
            v = v.rearrange("p (a b c d) -> p a b c d", a=shape[0], b=shape[1], c=shape[2])
        return v

    def finish(self, eng, name):
        eng.drain().then_inc(self.fence[name].sem, 1)

    def begin(self, eng, stage):
        if stage:
            for other in self.fence.values():
                eng.wait_ge(other.sem, stage)


class Job:

    def __init__(self, kind, weights, act, kc, cols, slots, store, on="act", nt=T, loop=False, needs=False):
        self.kind, self.weights, self.act, self.kc, self.cols = kind, weights, act, kc, cols
        self.slots, self.store, self.on, self.nt, self.loop = slots, store, on, nt, loop
        self.by_parity = None
        self.needs = needs
        self.per_slot = -(-cols // P) if kind == "features" else nt // P
        if not isinstance(on, str):
            self.share = {e: on.count(e) for e in ("act", "dve")}
        self.step = 1
        if loop:
            self.step = max(2, 4 // self.per_slot)
            assert slots % self.step == 0

    def engine(self, u):
        return self.on if isinstance(self.on, str) else self.on[u]

    def stored(self, i, u):
        if isinstance(self.on, str):
            return i * self.per_slot + (u + 1)
        e = self.on[u]
        return i * self.share[e] + self.on[:u + 1].count(e)


class Project:

    BANKS = 4

    def __init__(self, core, jobs):
        self.core, self.jobs, self.plan = core, jobs, []
        for j in jobs:
            assert not j.loop or (j.step * j.per_slot % self.BANKS == 0 and min(core.taken_count.values()) > 4)
            assert isinstance(j.on, str) or (j.per_slot == self.BANKS and j.loop)
            parts = len(j.weights(0))
            self.plan.append(dict(
                slot=core.slots, unit=core.units, landed=list(core.landed_count), parts=parts,
                taken=dict(core.taken_count), before=core.per_slot_before, settle=j.loop or j.needs or j.on != core.on_before))
            for n in range(core.slots, core.slots + j.slots):
                core.landed_count[n % 2] += 16 * parts
            core.slots += j.slots
            core.units += j.slots * j.per_slot
            for u in range(j.per_slot):
                core.taken_count[j.engine(u)] += j.slots
            core.per_slot_before, core.on_before = (j.per_slot, j.per_slot), j.on
            if j.slots == 1:
                core.per_slot_before = (self.plan[-1]["before"][1], j.per_slot)

    def sweep(self, eng, body):
        for j, p in zip(self.jobs, self.plan):
            if j.loop:
                with eng.Fori(0, j.slots // j.step) as n:
                    for s in range(j.step):
                        body(j, p, s, n * j.step + s)
            else:
                for i in range(j.slots):
                    body(j, p, i, i)

    def sync(self, sp):
        core = self.core

        def body(j, p, s, i):
            par = (p["slot"] + s) % 2
            if s < 2 and not j.loop:
                ended = p["unit"] - (p["before"][1] if s == 0 else 0)
            else:
                ended = p["unit"] + (i - 1) * j.per_slot
                if j.loop and s == 0:
                    ended = ended + max(0, j.per_slot - p["before"][1])
            if p["slot"] + s >= 2:
                sp.wait_ge(core.unit_ready.sem, ended)
            view = core.ring[:, par, 0:j.kc * j.cols].rearrange("p (k n) -> p k n", k=j.kc)
            for c, w in j.weights(i):
                sp.dma_start(view[:, :, c:c + w.shape[2]], w).then_inc(core.landed[par].sem, 16)
        self.sweep(sp, body)

    def tensor(self, pe):
        core, nc = self.core, self.core.nc

        def body(j, p, s, i):
            par = (p["slot"] + s) % 2
            if p["settle"] and s == 0 and not j.loop:
                settle(p)
            pe.wait_ge(core.landed[par].sem, p["landed"][par] + 16 * p["parts"] * (s // 2 + 1) + (i - s) * 8 * p["parts"])
            view = core.ring[:, par, 0:j.kc * j.cols].rearrange("p (k n) -> p k n", k=j.kc)
            for u in range(j.per_slot):
                n = s * j.per_slot + u
                bank = (p["unit"] + n) % self.BANKS
                if n >= self.BANKS or j.loop or not p["settle"]:
                    e = j.engine(u)
                    before = p["taken"][e] + j.stored(i, u) - (self.BANKS if isinstance(j.on, str) else j.share[e])
                    if j.loop or before > 0:
                        pe.wait_ge(core.unit_taken[e].sem, before)
                for k in range(j.kc):
                    if j.kind == "features":
                        m = min(P, j.cols - u * P)
                        mm = nc.tensor.matmul(core.ps[0:m, bank, 0:j.nt], view[:, k, u * P:u * P + m],
                                              j.act[:, k, 0:j.nt], start=k == 0, stop=k == j.kc - 1)
                    else:
                        mm = nc.tensor.matmul(core.ps[:, bank, 0:j.cols], j.act[:, k, u * P:(u + 1) * P],
                                              view[:, k, :], start=k == 0, stop=k == j.kc - 1)
                mm.then_inc(core.unit_ready.sem, 1)

        def settle(p):
            for on, n in p["taken"].items():
                if n:
                    pe.wait_ge(core.unit_taken[on].sem, n)

        for j, p in zip(self.jobs, self.plan):
            if j.loop:
                settle(p)
                with pe.Fori(0, j.slots // j.step) as n:
                    for s in range(j.step):
                        body(j, p, s, n * j.step + s)
            else:
                for i in range(j.slots):
                    body(j, p, i, i)

    def store(self, eng, name):
        core = self.core

        def body(j, p, s, i):
            for u in range(j.per_slot):
                if j.engine(u) != name:
                    continue
                eng.wait_ge(core.unit_ready.sem, p["unit"] + i * j.per_slot + (u + 1))
                bank = (p["unit"] + s * j.per_slot + u) % self.BANKS
                store = j.by_parity[s % 2] if j.by_parity else j.store
                store(eng, i, u, core.ps[:, bank, :]).then_inc(core.unit_taken[name].sem, 1)

        for j, p in zip(self.jobs, self.plan):
            if j.loop:
                with eng.Fori(0, j.slots // j.step) as n:
                    for s in range(j.step):
                        body(j, p, s, n * j.step + s)
            else:
                for i in range(j.slots):
                    body(j, p, i, i)


def columns_of(w, kc, width, base=0):
    view = w.rearrange("(k p) n -> p k n", p=P)
    return lambda i: [(0, view[:, 0:kc, bass.ds(base + i * width, width)])]


def feature_norm(core, stage, src, gain, dst, nt=T):
    nc, ps = core.nc, core.ps
    mark = core.top
    sq = core.take(DC, nt)
    v, r, a = core.take(nt), core.take(nt), core.take(nt)
    core.top = mark
    squares, summed, var_ready, root_ready = core.norm_sems
    k = core.norms
    core.norms += 1

    def scalar(act):
        for c in range(DC):
            act.activation(sq[:, c, :], src[:, c, :], ACT.Square).then_inc(squares.sem, 1)
        act.wait_ge(var_ready.sem, k + 1)
        act.activation(r, v, ACT.Sqrt).then_inc(root_ready.sem, 1)

    def tensor(pe):
        for c in range(DC):
            pe.wait_ge(squares.sem, DC * k + c + 1)
            mm = nc.tensor.matmul(ps[:, 4, 0:nt], core.ones, sq[:, c, :], start=c == 0, stop=c == DC - 1)
        mm.then_inc(summed.sem, 1)

    def vector(dve):
        dve.wait_ge(summed.sem, k + 1)
        dve.tensor_scalar(v, ps[:, 4, 0:nt], 1.0 / D, EPS, ALU.mult, ALU.add).then_inc(var_ready.sem, 1)
        dve.wait_ge(root_ready.sem, k + 1)
        newton_rsqrt(core, dve, v, r, a)
        for c in range(DC):
            dve.scalar_tensor_tensor(out=dst[:, c, :], in0=src[:, c, :], scalar=gain[:, c:c + 1], in1=r,
                                     op0=ALU.mult, op1=ALU.mult)

    return dict(act=scalar, pe=tensor, dve=vector)


def newton_rsqrt(core, dve, v, r, a):
    dve.reciprocal(r, r)
    dve.drain()
    dve.tensor_tensor(a, r, r, ALU.mult)
    dve.drain()
    dve.tensor_tensor(a, a, v, ALU.mult)
    dve.drain()
    dve.tensor_scalar(a, a, -0.5, 1.5, ALU.mult, ALU.add)
    dve.drain()
    dve.tensor_tensor(r, r, a, ALU.mult)
    dve.drain()


def mixer_kernel(nc, IN, out, debug):
    with ExitStack() as ctx:
        core = Core(nc, ctx)
        ps = core.ps
        sem = lambda name: core.count(name).sem
        core.norm_sems = [core.count(n) for n in ("squares_ready", "squares_summed", "variance_ready", "root_ready")]
        core.norms = 0

        core.ident = core.take(P)
        core.ones = core.take(P)
        LE, GT, LT, GE = (core.take(P) for _ in range(4))
        PROWS = 3
        rows = core.take(PROWS, P)
        cols = core.take(PROWS * P)
        col = {}
        pieces, at = [], 0
        for name, n in (("norm_mix", 8), ("norm_cross", 8), ("norm_mem", 8), ("norm_ffn", 8), ("norm_final", 8),
                        ("ssd_norm", 16), ("conv_b", 32), ("conv_w", 160), ("norm1_g_2", 8), ("norm2_g_2", 8),
                        ("b_gate_2", 16), ("conv_w_2", 48), ("final_norm_g_2", 8)):
            flat = IN[name]
            flat = {1: lambda a: a.rearrange("(r c) -> r c", c=P),
                    2: lambda a: a.rearrange("a (r c) -> (a r) c", c=P),
                    3: lambda a: a.rearrange("a t (r c) -> (a t r) c", c=P)}[len(flat.shape)](flat)
            col[name] = cols[:, at:at + n]
            done = 0
            while done < n:
                m = min(n - done, P - at % P)
                pieces.append((rows[at % P:at % P + m, at // P, :], flat[done:done + m, :]))
                done, at = done + m, at + m
        assert at <= PROWS * P
        xT = core.take(DC, T)
        hT = core.take(DC, T)
        floor = core.top

        s_small = sem("parameters_landed")
        s_x = sem("x_landed")
        s_made = sem("constants_made")
        s_prow = sem("parameter_rows_zeroed")
        s_turned = sem("chunks_turned")
        s_out = sem("output_stored")
        s_copied = sem("chunks_copied")

        def stage_load():
            mark = core.top
            xt = core.take(NT, D)
            core.top = mark

            def sync(sp):
                for t in range(NT):
                    sp.dma_start(xt[:, t, :], IN["x"][0, t * P:(t + 1) * P, :]).then_inc(s_x, 16)
                sp.wait_ge(s_prow, 1)
                for dst, src in pieces:
                    sp.dma_start(dst, src).then_inc(s_small, 16)

            def pool(gp):
                gp.memset(core.ident, 0.0)
                gp.memset(core.ones, 1.0)
                for m in (LE, GT, LT, GE):
                    gp.memset(m, 1.0)
                gp.drain()
                gp.affine_select(out=core.ident, in_=core.ident, compare_op=ALU.not_equal, fill=1.0, base=0,
                                 pattern=[[-1, P]], channel_multiplier=1)
                for m, cmp, mult in ((LE, ALU.is_ge, -1), (GT, ALU.is_gt, 1), (LT, ALU.is_gt, -1), (GE, ALU.is_ge, 1)):
                    gp.affine_select(out=m, in_=m, compare_op=cmp, fill=0.0, base=0,
                                     pattern=[[-mult, P]], channel_multiplier=mult)

            def vector(dve):
                dve.memset(rows, 0.0).then_inc(s_prow, 1)
                for c in range(DC // 2):
                    dve.wait_ge(s_turned, c + 1)
                    dve.tensor_copy(xT[:, c, :], ps[:, c, :]).then_inc(s_copied, 1)
                dve.wait_ge(s_turned, DC + 1)
                dve.tensor_copy(cols, ps[:, 0, 0:PROWS * P]).then_inc(s_made, 1)

            def scalar(act):
                for c in range(DC // 2, DC):
                    act.wait_ge(s_turned, c + 1)
                    act.activation(xT[:, c, :], ps[:, c, :], ACT.Copy)

            def tensor(pe):
                pe.wait_ge(core.fence["pool"].sem, 1)
                pe.wait_ge(s_x, 16 * NT)
                for c in range(DC):
                    for t in range(NT):
                        mm = nc.tensor.transpose(ps[:, c, t * P:(t + 1) * P], xt[:, t, c * P:(c + 1) * P], core.ident)
                    mm.then_inc(s_turned, 1)
                pe.wait_ge(s_small, 16 * len(pieces))
                pe.wait_ge(s_copied, 1)
                for t in range(PROWS):
                    mm = nc.tensor.transpose(ps[:, 0, t * P:(t + 1) * P], rows[:, t, :], core.ident)
                mm.then_inc(s_turned, 1)
            return dict(sp=sync, pool=pool, dve=vector, act=scalar, pe=tensor)


        def turn(src, dst, chunks, s_turned, base, gain=None, nt=T, on="dve", bank0=0):
            def tensor(pe):
                for c in range(chunks):
                    for t in range(nt // P):
                        mm = nc.tensor.transpose(ps[:, bank0 + c, t * P:(t + 1) * P], src[:, t, c * P:(c + 1) * P],
                                                 core.ident)
                    mm.then_inc(s_turned, 1)

            def evacuate(eng):
                for c in range(chunks):
                    eng.wait_ge(s_turned, base + c + 1)
                    if on == "act":
                        eng.activation(dst[:, c, :], ps[:, bank0 + c, 0:nt], ACT.Copy,
                                       scale=1.0 if gain is None else gain[:, c:c + 1])
                    elif gain is None:
                        eng.tensor_copy(dst[:, c, :], ps[:, bank0 + c, 0:nt])
                    else:
                        eng.tensor_scalar(dst[:, c, :], ps[:, bank0 + c, 0:nt], gain[:, c:c + 1], None, ALU.mult)
            return {"pe": tensor, on: evacuate}

        def project(jobs):
            p = Project(core, jobs)
            return dict(sp=p.sync, pe=p.tensor, act=lambda e: p.store(e, "act"), dve=lambda e: p.store(e, "dve"))

        def copy_store(dst, scale=1.0):
            return lambda eng, i, u, acc: eng.activation(dst[:, i * 4 + u, :], acc, ACT.Copy, scale=scale)

        def add_store(dst):
            return lambda eng, i, u, acc: eng.tensor_tensor(dst[:, i * 4 + u, :], acc, dst[:, i * 4 + u, :], ALU.add)

        def broadcast(src, n):
            return bass.AP(src.tensor, src.offset, [[0, P], [1, n]])

        def stage_attention():
            mark = core.top
            qT = core.take(DC, T)
            kd = core.take(KV_HEADS, T)
            v = core.take(NT, KV_HEADS * HD)
            attn = core.take(NT, D)
            W = 3 * P
            dist = core.take(W)
            dist2 = core.take(W)
            s, pr, pt = core.take(2, W), core.take(2, W), core.take(2, W)
            U = HEADS * NT
            top, shift, total, esink, den = (core.take(U) for _ in range(5))
            sink = core.take(HEADS)
            core.top = mark
            w = IN["w_in"][0]

            def k_store(eng, i, u, acc):
                for half in range(2):
                    for copy in range(2):
                        ins = eng.activation(kd[64 * copy:64 * copy + 64, 2 * u + half, :],
                                             acc[64 * half:64 * half + 64, :], ACT.Copy)
                return ins

            jobs = [Job("features", columns_of(w, DC, 512), hT, DC, 512, 2, copy_store(qT, HD ** -0.5)),
                    Job("features", columns_of(w, DC, 256, OFF_K), hT, DC, 256, 1, k_store),
                    Job("tokens", columns_of(w, DC, 256, OFF_V), hT, DC, 256, 1,
                        lambda eng, i, u, acc: eng.activation(v[:, u, :], acc[:, 0:256], ACT.Copy))]
            first = project(jobs)
            s_sink, s_dist, scores_ready, scores_read, shift_ready, probs_ready, sum_ready = (
                sem(n) for n in ("sink_landed", "distances_made", "scores_ready", "scores_read", "shift_ready",
                                 "probs_ready", "sums_ready"))
            probs_turned, turned_copied, out_ready, out_stored = (
                sem(n) for n in ("probs_turned", "turned_probs_copied", "mix_ready", "mix_stored"))
            first_sp = first["sp"]

            def sync(sp):
                sp.dma_start(sink, broadcast(IN["attn_sink"], HEADS)).then_inc(s_sink, 16)
                first_sp(sp)
            first["sp"] = sync

            def pool(gp):
                gp.iota(dist, pattern=[[-1, W]], base=P, channel_multiplier=1, allow_small_or_imprecise_dtypes=True)
                gp.drain()
                gp.tensor_scalar(dist2, dist, -1.0, None, ALU.mult)
                gp.drain()
                gp.affine_select(out=dist, in_=dist, compare_op=ALU.is_ge, fill=1e32, base=0,
                                 pattern=[[1, W]], channel_multiplier=-1)
                gp.affine_select(out=dist2, in_=dist2, compare_op=ALU.is_ge, fill=1e32, base=2 * P,
                                 pattern=[[-1, W]], channel_multiplier=1)
                gp.drain().then_inc(s_dist, 1)
            first["pool"] = pool

            units = [(h, b, max(0, b - 1), min(NT, b + 2)) for h in range(HEADS) for b in range(NT)]

            def tensor(pe):
                for u in range(U + 2):
                    if u < U:
                        h, b, k0, k1 = units[u]
                        r = 64 * (h % 2)
                        if u >= 2:
                            pe.wait_ge(scores_read, u - 1)
                        nc.tensor.matmul(ps[:, u % 2, 0:(k1 - k0) * P], qT[r:r + 64, h // 2, b * P:(b + 1) * P],
                                         kd[r:r + 64, h // 4, k0 * P:k1 * P], start=True, stop=True)\
                            .then_inc(scores_ready, 1)
                    if 1 <= u <= U:
                        n = u - 1
                        h, b, k0, k1 = units[n]
                        pe.wait_ge(probs_ready, n + 1)
                        if n >= 2:
                            pe.wait_ge(turned_copied, n - 1)
                        for k in range(k1 - k0):
                            mm = nc.tensor.transpose(ps[:, 2 + n % 2, k * P:(k + 1) * P],
                                                     pr[:, n % 2, k * P:(k + 1) * P], core.ident)
                        mm.then_inc(probs_turned, 1)
                    if u >= 2:
                        n = u - 2
                        h, b, k0, k1 = units[n]
                        pe.wait_ge(turned_copied, n + 1)
                        if n >= 2:
                            pe.wait_ge(out_stored, n - 1)
                        for k in range(k1 - k0):
                            mm = nc.tensor.matmul(ps[:, 4 + n % 2, 0:HD], pt[:, n % 2, k * P:(k + 1) * P],
                                                  v[:, k0 + k, (h // 4) * HD:(h // 4 + 1) * HD],
                                                  start=k == 0, stop=k == k1 - k0 - 1)
                        mm.then_inc(out_ready, 1)

            def vector(dve):
                dve.wait_ge(s_dist, 1)
                dve.tensor_tensor(dist, dist, dist2, ALU.max)
                dve.drain()
                dve.wait_ge(s_sink, 16)
                for u in range(U + 2):
                    if u < U:
                        h, b, k0, k1 = units[u]
                        n = (k1 - k0) * P
                        w0 = (k0 - b + 1) * P
                        dve.wait_ge(scores_ready, u + 1)
                        if u >= 2:
                            dve.wait_ge(probs_ready, u - 1)
                        dve.scalar_tensor_tensor(out=s[:, u % 2, 0:n], in0=dist[:, w0:w0 + n],
                                                 scalar=-(2.0 ** (-8.0 * (h + 1) / HEADS)),
                                                 in1=ps[:, u % 2, 0:n], op0=ALU.mult, op1=ALU.add)\
                            .then_inc(scores_read, 1)
                        dve.drain()
                        dve.tensor_reduce(top[:, u:u + 1], s[:, u % 2, 0:n], AX.X, ALU.max)
                        dve.drain()
                        dve.tensor_scalar(shift[:, u:u + 1], top[:, u:u + 1], sink[:, h:h + 1], -1.0,
                                          ALU.max, ALU.mult).then_inc(shift_ready, 1)
                    if u >= 2:
                        n = u - 2
                        h, b = units[n][:2]
                        dve.wait_ge(sum_ready, n + 1)
                        dve.tensor_tensor(den[:, n:n + 1], total[:, n:n + 1], esink[:, n:n + 1], ALU.add)
                        dve.drain()
                        dve.reciprocal(den[:, n:n + 1], den[:, n:n + 1])
                        dve.drain()
                        dve.wait_ge(out_ready, n + 1)
                        dve.tensor_scalar(attn[:, b, h * HD:(h + 1) * HD], ps[:, 4 + n % 2, 0:HD],
                                          den[:, n:n + 1], None, ALU.mult).then_inc(out_stored, 1)

            def scalar(act):
                act.wait_ge(s_sink, 16)
                for u in range(U + 1):
                    if u < U:
                        h, b, k0, k1 = units[u]
                        n = (k1 - k0) * P
                        act.wait_ge(shift_ready, u + 1)
                        if u >= 2:
                            act.wait_ge(probs_turned, u - 1)
                        act.activation(pr[:, u % 2, 0:n], s[:, u % 2, 0:n], ACT.Exp, bias=shift[:, u:u + 1],
                                       accum_out=total[:, u:u + 1]).then_inc(probs_ready, 1)
                        act.activation(esink[:, u:u + 1], sink[:, h:h + 1], ACT.Exp, bias=shift[:, u:u + 1])\
                            .then_inc(sum_ready, 1)
                    if u >= 1:
                        n = u - 1
                        h, b, k0, k1 = units[n]
                        act.wait_ge(probs_turned, n + 1)
                        if n >= 2:
                            act.wait_ge(out_ready, n - 1)
                        act.activation(pt[:, n % 2, 0:(k1 - k0) * P], ps[:, 2 + n % 2, 0:(k1 - k0) * P], ACT.Copy)\
                            .then_inc(turned_copied, 1)
            return first, dict(pe=tensor, dve=vector, act=scalar), attn

        def gate_store(dst, bias=None):
            def store(eng, i, u, acc):
                if bias is None:
                    return eng.activation(dst[:, i * 4 + u, :], acc, ACT.Sigmoid)
                return eng.activation(dst[:, i * 4 + u, :], acc, ACT.Sigmoid, bias=bias[:, i * 4 + u:i * 4 + u + 1])
            return store

        def times_store(dst, gate):
            return lambda eng, i, u, acc: eng.tensor_tensor(dst[:, i * 4 + u, :], acc, gate[:, i * 4 + u, :], ALU.mult)

        def add_times_store(dst, gate, per_slot):
            def store(eng, i, u, acc):
                m = i * per_slot + u
                eng.tensor_tensor(gate[:, m, :], acc, gate[:, m, :], ALU.mult)
                eng.drain()
                return eng.tensor_tensor(dst[:, m, :], dst[:, m, :], gate[:, m, :], ALU.add)
            return store

        def softplus(x, u, a, b, ready, base, act_too):
            r0, r1 = ready

            def vector(dve):
                dve.tensor_scalar(a, x, -1.0, None, ALU.mult)
                dve.drain()
                dve.tensor_tensor(u, a, x, ALU.min).then_inc(r0, 1)
                dve.wait_ge(r1, base + 1)
                dve.tensor_scalar(a, u, 2.0, None, ALU.add)
                dve.drain()
                dve.reciprocal(a, a)
                dve.drain()
                dve.tensor_tensor(u, u, a, ALU.mult)
                dve.drain()
                dve.tensor_tensor(a, u, u, ALU.mult)
                dve.drain()
                dve.tensor_scalar(b, a, 2.0 / 17, 2.0 / 15, ALU.mult, ALU.add)
                for k in (13, 11, 9, 7, 5, 3, 1):
                    dve.drain()
                    dve.tensor_tensor(b, b, a, ALU.mult)
                    dve.drain()
                    dve.tensor_scalar(b, b, 2.0 / k, None, ALU.add)
                dve.drain()
                dve.tensor_tensor(b, b, u, ALU.mult)
                dve.drain()
                dve.scalar_tensor_tensor(out=x, in0=x, scalar=0.0, in1=b, op0=ALU.max, op1=ALU.add)
                dve.drain()

            def scalar(act):
                act.wait_ge(r0, base + 1)
                act.activation(u, u, ACT.Exp).then_inc(r1, 1)
            return vector, scalar

        ssdT = None

        def stages_ssd():
            mark = core.top
            w = IN["w_in"][0]
            ssdT = core.take(2 * GROUPS, T)
            inner = core.top
            H = SSD_HEADS
            dt = core.take(2, NT, H)
            a = core.take(2, NT, H)
            into = core.take(2, NT, H)
            wst = core.take(2, NT, H)
            whole = core.take(2, NT, H)
            bias, alog = core.take(2, H), core.take(2, H)
            dskip = core.take(H)
            after_dt = core.top
            raw, u_, a_, b_ = (core.take(NT * 2 * H) for _ in range(4))
            core.top = after_dt
            raw4 = raw.rearrange("p (c d h) -> p c d h", c=NT, d=2)
            s_par, sp0, sp1, s_a, s_exp, s_a_ready, s_sums = (
                sem(n) for n in ("ssd_parameters_landed", "softplus_arg", "softplus_exp", "a_log_exp", "decay_exp",
                                 "log_decays_ready", "decay_sums_ready"))

            def raw_store(eng, i, u, acc):
                return eng.activation(raw[:, u * 2 * H:(u + 1) * 2 * H], acc[:, 0:2 * H], ACT.Copy)
            proj_dt = project([Job("tokens", columns_of(w, DC, 2 * H, OFF_DT), hT, DC, 2 * H, 1, raw_store)])
            dt_sp = proj_dt["sp"]

            def sync(sp):
                sp.dma_start(bias.rearrange("p d h -> p (d h)"), broadcast(IN["dt_bias"], 2 * H)).then_inc(s_par, 16)
                sp.dma_start(alog.rearrange("p d h -> p (d h)"), broadcast(IN["a_log"], 2 * H)).then_inc(s_par, 16)
                sp.dma_start(dskip, broadcast(IN["d_skip"], H)).then_inc(s_par, 16)
                dt_sp(sp)
            proj_dt["sp"] = sync
            soft_v, soft_a = softplus(raw, u_, a_, b_, (sp0, sp1), 0, None)

            def decay_vector(dve):
                dve.wait_ge(s_par, 48)
                for c in range(NT):
                    dve.tensor_tensor(raw4[:, c], raw4[:, c], bias, ALU.add)
                dve.drain()
                soft_v(dve)
                for d in range(2):
                    dve.tensor_copy(dt[:, d], raw4[:, :, d, :])
                dve.drain()
                dve.wait_ge(s_a, 1)
                for d in range(2):
                    for c in range(NT):
                        ins = dve.scalar_tensor_tensor(out=a[:, d, c, :], in0=dt[:, d, c, :], scalar=-1.0,
                                                       in1=alog[:, d, :], op0=ALU.mult, op1=ALU.mult)
                ins.then_inc(s_a_ready, 1)
                dve.wait_ge(s_exp, 1)
                dve.tensor_tensor(wst, wst, dt, ALU.mult)

            def decay_scalar(act):
                act.wait_ge(s_par, 48)
                act.activation(alog, alog, ACT.Exp).then_inc(s_a, 1)
                soft_a(act)
                act.wait_ge(s_sums, 1)
                flat = lambda t: t.rearrange("p d c h -> p (d c h)")
                act.activation(flat(into), ps[:, 0, 0:2 * NT * H], ACT.Exp)
                act.activation(flat(whole), ps[:, 1, 0:2 * NT * H], ACT.Exp)
                act.activation(flat(wst), ps[:, 2, 0:2 * NT * H], ACT.Exp).then_inc(s_exp, 1)

            def decay_tensor(pe):
                pe.wait_ge(s_a_ready, 1)
                n = NT * H
                for bank, masks in ((0, (LE, GE)), (1, (core.ones, core.ones)), (2, (GT, LT))):
                    for d in range(2):
                        mm = nc.tensor.matmul(ps[:, bank, d * n:(d + 1) * n], masks[d],
                                              a[:, d].rearrange("p c h -> p (c h)"), start=True, stop=True)
                mm.then_inc(s_sums, 1)

            PAD = TAPS // 2
            up = core.take(4, T + 2 * PAD)
            cv = core.take(4, T)
            fT = core.take(4, T)
            zt = core.take(NT, GW)
            xt = core.take(NT, GW)
            Bt = core.take(NT, D_STATE)
            xw = core.take(4, NT, GW)
            xd = core.take(NT, GW)
            prev = core.take(2, NT, GW)
            cb = core.take(2, NT, P)
            am = core.take(4, GH, P)
            ex = core.take(2, GH * P)
            M = xw[:, 2:4].rearrange("p a c n -> p (a c n)").rearrange("p (a n) -> p a n", a=4)
            y = cv.rearrange("p a b -> p (a b)")[:, 0:NT * GW].rearrange("p (c n) -> p c n", c=NT)
            off = core.take(2, GW)
            ss, vv, rr, aa = (core.take(NT) for _ in range(4))
            core.top = mark
            (w_landed0, w_landed1, u_ready, u_copied, z_ready, z_stored, conv_ready, feat_ready, turned,
             tok_ready, xw_ready, st_ready, prev_ready, cb_ready, am_ready, diff_ready, ex_ready, m_ready,
             y_ready, y_read, y_done, ss_ready, v_ready, root_ready, y_final, y_turned, y_stored, diag_done, pads_zeroed) = (
                sem(f"ssd_{n}") for n in (
                    "xbc_weights_landed", "z_weights_landed", "xbc_ready", "xbc_copied", "z_ready",
                    "z_stored", "conv_ready", "features_ready", "turned", "tokens_ready", "weighted_ready",
                    "chunk_states_ready", "states_ready", "cb_ready", "steps_ready", "sums_ready",
                    "decays_ready", "mixers_ready", "y_ready", "y_read", "y_gated", "squares_ready", "variance_ready",
                    "root_ready", "y_normed", "y_turned", "y_stored", "diagonal_made", "pads_zeroed"))
            units_before = core.units
            wv = w.rearrange("(k p) n -> p k n", p=P)
            slot0 = core.ring[:, 0, :].rearrange("p (k n) -> p k n", k=DC)
            slot1 = core.ring[:, 1, 0:DC * GW].rearrange("p (k n) -> p k n", k=DC)
            OFF_B = OFF_XBC + D_INNER
            OFF_C = OFF_B + GROUPS * D_STATE
            cw = col["conv_w"].rearrange("p (t c) -> p t c", t=TAPS)

            def chunk_of(g, j):
                return (2 * g, 2 * g + 1, g + 2 * GROUPS, g + 3 * GROUPS)[j]

            def ssd_sync(sp):
                sp.wait_ge(core.unit_ready.sem, units_before)
                with sp.Fori(0, GROUPS) as g:
                    sp.wait_ge(u_ready, g * 4 + 1)
                    for c, n, at in ((0, GW, OFF_XBC + g * GW), (GW, D_STATE, OFF_B + g * D_STATE),
                                     (GW + D_STATE, D_STATE, OFF_C + g * D_STATE)):
                        sp.dma_start(slot0[:, :, c:c + n], wv[:, :, bass.ds(at, n)]).then_inc(w_landed0, 16)
                    sp.wait_ge(z_ready, g * 4 + 1)
                    sp.dma_start(slot1, wv[:, :, bass.ds(OFF_Z + g * GW, GW)]).then_inc(w_landed1, 16)
                sp.wait_ge(z_ready, NT * GROUPS + 1)

            def begin_at_one(eng, *semaphores):
                for s in semaphores:
                    eng.drain().then_inc(s, 1)

            def ssd_tensor(pe):
                begin_at_one(pe, u_ready, z_ready, y_turned, diff_ready)
                with pe.Fori(0, GROUPS) as g:
                    pe.wait_ge(w_landed0, g * 48 + 48)
                    pe.wait_ge(y_stored, g * 2 + 1)
                    for j in range(4):
                        for k in range(DC):
                            mm = nc.tensor.matmul(ps[:, j, :], slot0[:, k, j * P:(j + 1) * P], hT[:, k, :],
                                                  start=k == 0, stop=k == DC - 1)
                        mm.then_inc(u_ready, 1)
                    pe.wait_ge(w_landed1, g * 16 + 16)
                    for t in range(NT):
                        for k in range(DC):
                            mm = nc.tensor.matmul(ps[:, 4 + t, 0:GW], hT[:, k, t * P:(t + 1) * P], slot1[:, k, :],
                                                  start=k == 0, stop=k == DC - 1)
                        mm.then_inc(z_ready, 1)
                    pe.wait_ge(feat_ready, g * 4 + 4)
                    pe.wait_ge(z_stored, g * 4 + 4)
                    for c in range(NT):
                        t = slice(c * P, (c + 1) * P)
                        mm = nc.tensor.matmul(ps[:, 6, t], fT[:, 2, t], fT[:, 3, t], start=True, stop=True)
                    mm.then_inc(cb_ready, 1)
                    pe.wait_ge(u_copied, g * 4 + 4)
                    for j in range(3):
                        for t in range(NT):
                            mm = nc.tensor.transpose(ps[:, j, t * P:(t + 1) * P], fT[:, j, t * P:(t + 1) * P],
                                                     core.ident)
                        mm.then_inc(turned, 1)
                    pe.wait_ge(xw_ready, g * 4 + 4)
                    pe.wait_ge(tok_ready, g * 3 + 3)
                    n = 0
                    for d, chunks in ((0, (0, 1, 2)), (1, (3, 2, 1))):
                        for c in chunks:
                            mm = nc.tensor.matmul(ps[:, 3 + n // 2, (n % 2) * GW:(n % 2 + 1) * GW], Bt[:, c, :],
                                                  xw[:, 2 + d, c, :], start=True, stop=True)
                            n += 1
                    mm.then_inc(st_ready, 1)

                    def sums(n):
                        c, d = n // 2, n % 2
                        pe.wait_ge(am_ready, g * 8 + (n + 1))
                        if n >= 2:
                            pe.wait_ge(ex_ready, g * 8 + (n - 1))
                        for r in range(GH):
                            mm = nc.tensor.matmul(ps[:, n % 2, r * P:(r + 1) * P], am[:, n % 4, r, :], (LE, GE)[d],
                                                  start=True, stop=True)
                        mm.then_inc(diff_ready, 1)

                    sums(0)
                    sums(1)
                    pe.wait_ge(prev_ready, g + 1)
                    for c in range(NT):
                        if c + 1 < NT:
                            sums(2 * c + 2)
                            sums(2 * c + 3)
                        t = slice(c * P, (c + 1) * P)
                        if c:
                            pe.wait_ge(y_read, g * 4 + c)
                        if c > 0:
                            nc.tensor.matmul(ps[:, 5, 0:GW], fT[:, 3, t], prev[:, 0, c, :], start=True, stop=True)
                        if c < NT - 1:
                            nc.tensor.matmul(ps[:, 5, GW:2 * GW], fT[:, 3, t], prev[:, 1, c, :], start=True, stop=True)
                        pe.wait_ge(m_ready, g * 8 + (2 * c + 2))
                        for r in range(GH):
                            for d in range(2):
                                mm = nc.tensor.matmul(ps[:, 7, r * 64:(r + 1) * 64],
                                                      M[:, (2 * c + d) % 4, r * P:(r + 1) * P],
                                                      xw[:, d, c, r * 64:(r + 1) * 64], start=d == 0, stop=d == 1)
                        mm.then_inc(y_ready, 1)
                    pe.wait_ge(y_final, g + 1)
                    for j in range(2):
                        for t in range(NT):
                            mm = nc.tensor.transpose(ps[:, j, t * P:(t + 1) * P], y[:, t, j * P:(j + 1) * P],
                                                     core.ident)
                        mm.then_inc(y_turned, 1)

            def ssd_scalar(act):
                begin_at_one(act, y_stored)
                act.wait_ge(pads_zeroed, 1)
                with act.Fori(0, GROUPS) as g:
                    for j in range(4):
                        act.wait_ge(u_ready, g * 4 + (j + 2))
                        act.wait_ge(conv_ready, g * 4 + 1)
                        ins = act.activation(up[:, j, PAD:PAD + T], ps[:, j, :], ACT.Copy)
                        ins.then_inc(u_copied, 1)
                    for t in range(NT):
                        act.wait_ge(z_ready, g * 4 + (t + 2))
                        act.activation(zt[:, t, :], ps[:, 4 + t, 0:GW], ACT.Silu).then_inc(z_stored, 1)
                    for j in (2, 3, 0, 1):
                        act.wait_ge(conv_ready, g * 4 + ((2, 3, 0, 1).index(j) + 2))
                        act.activation(fT[:, j, :], cv[:, j, :], ACT.Silu,
                                       bias=col["conv_b"][:, bass.ds(chunk_of(g, j), 1)]).then_inc(feat_ready, 1)
                    for j in range(3):
                        act.wait_ge(turned, g * 3 + (j + 1))
                        src = ps[:, j, :].rearrange("p (t n) -> p t n", t=NT)
                        dst = xt[:, :, j * P:(j + 1) * P] if j < 2 else Bt
                        act.activation(dst, src, ACT.Copy).then_inc(tok_ready, 1)
                    for n in range(8):
                        act.wait_ge(diff_ready, g * 8 + (n + 2))
                        if n >= 2:
                            act.wait_ge(m_ready, g * 8 + (n - 1))
                        act.activation(ex[:, n % 2, :], ps[:, n % 2, :], ACT.Exp).then_inc(ex_ready, 1)
                    for c in range(NT):
                        act.wait_ge(y_done, g * 4 + (c + 1))
                        act.activation(up[:, c, PAD:PAD + GW], y[:, c, :], ACT.Square,
                                       accum_out=ss[:, c:c + 1]).then_inc(ss_ready, 1)
                    act.wait_ge(v_ready, g + 1)
                    act.activation(rr, vv, ACT.Sqrt).then_inc(root_ready, 1)
                    for j in range(2):
                        act.wait_ge(y_turned, g * 2 + (j + 2))
                        act.activation(ssdT[:, bass.ds(2 * g + j, 1), :].rearrange("p a t -> p (a t)"),
                                       ps[:, j, :], ACT.Copy,
                                       scale=col["ssd_norm"][:, bass.ds(2 * g + j, 1)]).then_inc(y_stored, 1)

            def per_head(t, g, d, c=None):
                if c is None:
                    return t[:, d, :, bass.ds(g * GH, GH)].unsqueeze(3).to_broadcast([P, NT, GH, 64])
                return t[:, d, c, bass.ds(g * GH, GH)].unsqueeze(2).to_broadcast([P, GH, 64])

            heads = lambda t: t.rearrange("p (r n) -> p r n", r=GH)

            def ssd_vector(dve):
                dve.memset(up, 0.0).then_inc(pads_zeroed, 1)
                begin_at_one(dve, conv_ready)
                with dve.Fori(0, GROUPS) as g:
                    for n, j in enumerate((2, 3, 0, 1)):
                        dve.wait_ge(u_copied, g * 4 + 4)
                        m = chunk_of(g, j)
                        dve.wait_ge(y_turned, g * 2 + 1)
                        dve.tensor_scalar(cv[:, j, :], up[:, j, 0:T], cw[:, 0, bass.ds(m, 1)], None, ALU.mult)
                        for k in range(1, TAPS):
                            dve.drain()
                            ins = dve.scalar_tensor_tensor(out=cv[:, j, :], in0=up[:, j, k:k + T],
                                                           scalar=cw[:, k, bass.ds(m, 1)], in1=cv[:, j, :],
                                                           op0=ALU.mult, op1=ALU.add)
                        ins.then_inc(conv_ready, 1)
                    dve.wait_ge(cb_ready, g + 1)
                    for d, mask in enumerate((LE, GE)):
                        dve.tensor_tensor(cb[:, d], ps[:, 6, :].rearrange("p (c n) -> p c n", c=NT),
                                          mask.unsqueeze(1).to_broadcast([P, NT, P]), ALU.mult)
                    dve.drain()
                    dve.wait_ge(st_ready, g + 1)
                    n = 0
                    for d, chunks in ((0, (0, 1, 2)), (1, (3, 2, 1))):
                        for c in chunks:
                            to = c + 1 if d == 0 else c - 1
                            add = ps[:, 3 + n // 2, (n % 2) * GW:(n % 2 + 1) * GW]
                            if n % 3 == 0:
                                ins = dve.tensor_copy(prev[:, d, to, :], add)
                            else:
                                dve.tensor_tensor(heads(prev[:, d, to, :]), heads(prev[:, d, c, :]),
                                                  per_head(whole, g, d, c), ALU.mult)
                                dve.drain()
                                ins = dve.tensor_tensor(prev[:, d, to, :], add, prev[:, d, to, :], ALU.add)
                            dve.drain()
                            n += 1
                    ins = dve.drain()
                    ins.then_inc(prev_ready, 1)

                    def mixers(n):
                        c, d = n // 2, n % 2
                        dve.wait_ge(ex_ready, g * 8 + (n + 1))
                        if n >= 4:
                            dve.wait_ge(y_ready, g * 4 + (n // 2 - 1))
                        dve.tensor_tensor(heads(M[:, n % 4, :]), heads(ex[:, n % 2, :]),
                                          cb[:, d, c, :].unsqueeze(1).to_broadcast([P, GH, P]), ALU.mult)\
                            .then_inc(m_ready, 1)
                    mixers(0)
                    mixers(1)
                    for c in range(NT):
                        if c + 1 < NT:
                            mixers(2 * c + 2)
                            mixers(2 * c + 3)
                        dve.wait_ge(y_ready, g * 4 + (c + 1))
                        dve.wait_ge(diag_done, g + 1)
                        if c > 0:
                            dve.tensor_tensor(heads(off[:, 0, :]), heads(ps[:, 5, 0:GW]), per_head(into, g, 0, c),
                                              ALU.mult)
                        if c < NT - 1:
                            dve.tensor_tensor(heads(off[:, 1, :]), heads(ps[:, 5, GW:2 * GW]),
                                              per_head(into, g, 1, c), ALU.mult)
                        dve.tensor_tensor(y[:, c, :], ps[:, 7, 0:GW], xd[:, c, :], ALU.add).then_inc(y_read, 1)
                        dve.drain()
                        if c > 0:
                            dve.tensor_tensor(y[:, c, :], y[:, c, :], off[:, 0, :], ALU.add)
                            dve.drain()
                        if c < NT - 1:
                            dve.tensor_tensor(y[:, c, :], y[:, c, :], off[:, 1, :], ALU.add)
                            dve.drain()
                        dve.tensor_tensor(y[:, c, :], y[:, c, :], zt[:, c, :], ALU.mult).then_inc(y_done, 1)
                    dve.wait_ge(ss_ready, g * 4 + 4)
                    dve.tensor_scalar(vv, ss, 1.0 / GW, EPS, ALU.mult, ALU.add).then_inc(v_ready, 1)
                    dve.wait_ge(root_ready, g + 1)
                    newton_rsqrt(core, dve, vv, rr, aa)
                    for c in range(NT):
                        ins = dve.tensor_scalar(y[:, c, :], y[:, c, :], rr[:, c:c + 1], None, ALU.mult)
                    ins.then_inc(y_final, 1)

            def ssd_pool(gp):
                with gp.Fori(0, GROUPS) as g:
                    def steps(n):
                        c, d = n // 2, n % 2
                        if n >= 4:
                            gp.wait_ge(diff_ready, g * 8 + (n - 2))
                        gp.tensor_tensor(am[:, n % 4], (GT, LT)[d].unsqueeze(1).to_broadcast([P, GH, P]),
                                         a[:, d, c, bass.ds(g * GH, GH)].unsqueeze(2).to_broadcast([P, GH, P]),
                                         ALU.mult).then_inc(am_ready, 1)
                    gp.wait_ge(diff_ready, g * 8 + 1)
                    for n in range(4):
                        steps(n)
                    gp.wait_ge(tok_ready, g * 3 + 2)
                    x4 = xt.rearrange("p c (r n) -> p c r n", r=GH)
                    for n, t in ((2, wst), (3, wst), (0, dt), (1, dt)):
                        for c in range(NT):
                            ins = gp.tensor_tensor(heads(xw[:, n, c, :]), heads(xt[:, c, :]),
                                                   per_head(t, g, n % 2, c), ALU.mult)
                        ins.then_inc(xw_ready, 1)
                    for c in range(NT):
                        ins = gp.tensor_tensor(heads(xd[:, c, :]), heads(xt[:, c, :]),
                                               dskip[:, bass.ds(g * GH, GH)].unsqueeze(2).to_broadcast([P, GH, 64]),
                                               ALU.mult)
                    ins.then_inc(diag_done, 1)
                    for n in range(4, 8):
                        steps(n)

            ssd = dict(sp=ssd_sync, pe=ssd_tensor, act=ssd_scalar, dve=ssd_vector, pool=ssd_pool)
            gate = core.arena[:, inner:inner + DC * T].rearrange("p (a b) -> p a b", a=DC)
            join = project([
                Job("features", columns_of(w, DC, 512, OFF_GATE + D), hT, DC, 512, 2, gate_store(gate)),
                Job("features", columns_of(IN["w_ssd_branch"][0], 2 * DC, 256), ssdT, 2 * DC, 256, 4,
                    add_times_store(merged, gate, 2), on="dve"),
                Job("features", columns_of(IN["w_out"][0], DC, 512), merged, DC, 512, 2, add_store(xT), on="dve",
                    needs=True)])
            return proj_dt, dict(pe=decay_tensor, act=decay_scalar, dve=decay_vector), ssd, join

        def stages_cross():
            mark = core.top
            MT = MEM // P
            memT = core.take(DC, MEM)
            kx = core.take(X_HEADS, MEM)
            vx = core.take(MT, X_HEADS * XD)
            qx = core.take(X_HEADS, T)
            ox = core.take(X_HEADS, T)
            s, pr, pt = core.take(2, MEM), core.take(2, MEM), core.take(2, MEM)
            U = X_HEADS * NT
            shift, total, den = (core.take(U) for _ in range(3))
            mt = core.take(MT, D)
            (s_mem, s_mturned, scores_ready, scores_read, shift_ready, probs_ready, normed, probs_turned,
             turned_copied, out_ready, out_stored) = (
                sem(f"cross_{n}") for n in ("memory_landed", "memory_turned", "scores_ready", "scores_read",
                                            "shift_ready", "probs_ready", "probs_normed", "probs_turned",
                                            "turned_copied", "mix_ready", "mix_stored"))
            before = len(stages)
            load = turn(mt, memT, DC, s_mturned, 0, nt=MEM)
            turn_pe = load["pe"]

            def sync(sp):
                core.begin(sp, before)
                for t in range(MT):
                    sp.dma_start(mt[:, t, :], IN["mem"][0, t * P:(t + 1) * P, :]).then_inc(s_mem, 16)
            load["sp"] = sync

            def wait_turn(pe):
                pe.wait_ge(s_mem, 16 * MT)
                turn_pe(pe)
            load["pe"] = wait_turn
            yield load
            yield feature_norm(core, 0, memT, col["norm_mem"], memT, nt=MEM)
            yield feature_norm(core, 0, xT, col["norm_cross"], hT)
            core.top = mark
            wkv = IN["w_xkv"][0]
            yield project([
                Job("features", columns_of(IN["w_xq"][0], DC, 512), hT, DC, 512, 1, copy_store(qx, XD ** -0.5)),
                Job("features", columns_of(wkv, DC, 512), memT, DC, 512, 1,
                    lambda eng, i, u, acc: eng.activation(kx[:, u, :], acc[:, 0:MEM], ACT.Copy), nt=MEM),
                Job("tokens", columns_of(wkv, DC, 512, 512), memT, DC, 512, 1,
                    lambda eng, i, u, acc: eng.activation(vx[:, u, :], acc, ACT.Copy), nt=MEM)])
            units = [(h, b) for h in range(X_HEADS) for b in range(NT)]

            def tensor(pe):
                for u in range(U + 2):
                    if u < U:
                        h, b = units[u]
                        if u >= 2:
                            pe.wait_ge(scores_read, u - 1)
                        nc.tensor.matmul(ps[:, u % 2, 0:MEM], qx[:, h, b * P:(b + 1) * P], kx[:, h, :],
                                         start=True, stop=True).then_inc(scores_ready, 1)
                    if 1 <= u <= U:
                        n = u - 1
                        pe.wait_ge(normed, n + 1)
                        if n >= 2:
                            pe.wait_ge(turned_copied, n - 1)
                        for k in range(MT):
                            mm = nc.tensor.transpose(ps[:, 2 + n % 2, k * P:(k + 1) * P],
                                                     pr[:, n % 2, k * P:(k + 1) * P], core.ident)
                        mm.then_inc(probs_turned, 1)
                    if u >= 2:
                        n = u - 2
                        h, b = units[n]
                        pe.wait_ge(turned_copied, n + 1)
                        if n >= 2:
                            pe.wait_ge(out_stored, n - 1)
                        for k in range(MT):
                            mm = nc.tensor.matmul(ps[:, 4 + n % 2, 0:P], vx[:, k, h * XD:(h + 1) * XD],
                                                  pt[:, n % 2, k * P:(k + 1) * P], start=k == 0, stop=k == MT - 1)
                        mm.then_inc(out_ready, 1)

            def vector(dve):
                for u in range(U + 2):
                    if u < U:
                        dve.wait_ge(scores_ready, u + 1)
                        dve.tensor_reduce(shift[:, u:u + 1], ps[:, u % 2, 0:MEM], AX.X, ALU.max, negate=True)\
                            .then_inc(shift_ready, 1)
                    if 1 <= u <= U:
                        n = u - 1
                        dve.wait_ge(probs_ready, n + 1)
                        dve.reciprocal(den[:, n:n + 1], total[:, n:n + 1])
                        dve.drain()
                        dve.tensor_scalar(pr[:, n % 2, :], pr[:, n % 2, :], den[:, n:n + 1], None, ALU.mult)\
                            .then_inc(normed, 1)
                    if u >= 2:
                        n = u - 2
                        h, b = units[n]
                        dve.wait_ge(out_ready, n + 1)
                        dve.tensor_copy(ox[:, h, b * P:(b + 1) * P], ps[:, 4 + n % 2, 0:P]).then_inc(out_stored, 1)

            def scalar(act):
                for u in range(U + 1):
                    if u < U:
                        act.wait_ge(shift_ready, u + 1)
                        if u >= 2:
                            act.wait_ge(probs_turned, u - 1)
                        act.activation(pr[:, u % 2, :], ps[:, u % 2, 0:MEM], ACT.Exp, bias=shift[:, u:u + 1],
                                       accum_out=total[:, u:u + 1]).then_inc(probs_ready, 1)
                        act.wait_ge(probs_ready, u + 1)
                        act.drain().then_inc(scores_read, 1)
                    if u >= 1:
                        n = u - 1
                        act.wait_ge(probs_turned, n + 1)
                        if n >= 2:
                            act.wait_ge(out_ready, n - 1)
                        act.activation(pt[:, n % 2, :], ps[:, 2 + n % 2, 0:MEM], ACT.Copy).then_inc(turned_copied, 1)
            yield dict(pe=tensor, dve=vector, act=scalar)
            yield project([Job("features", columns_of(IN["w_xo"][0], X_HEADS, 512), ox, X_HEADS, 512, 2,
                               add_store(xT), on="dve")])

        def row(t, m):
            return t[:, bass.ds(m, 1), :].rearrange("p a n -> p (a n)")

        def down(w, act):
            return Job("features", columns_of(w, 32, P), act, 32, P, DC,
                       lambda eng, i, u, acc: eng.tensor_tensor(row(xT, i), acc, row(xT, i), ALU.add),
                       on="dve", loop=True, needs=True)

        def stages_ffn():
            mark = core.top
            upT = core.take(D_FF // P, T)
            yield feature_norm(core, 0, xT, col["norm_ffn"], hT)
            core.top = mark

            def relu2_store(eng, i, u, acc):
                dst = row(upT, i * 4 + u)
                eng.activation(dst, acc, ACT.Relu)
                eng.drain()
                return eng.activation(dst, dst, ACT.Square)
            yield project([Job("features", columns_of(IN["w_up"][0], DC, 512), hT, DC, 512, D_FF // 512,
                               relu2_store, loop=True),
                           down(IN["w_down"][0], upT)])
            yield feature_norm(core, 0, xT, col["norm_final"], xT)

        w2 = IN["w_in_2"][0]

        def stages_delta(gated):
            mark = core.top
            QKV = 3 * AH * AD
            zt = core.take(NT, AH * AD)
            beta = core.take(NT, AH)
            g = core.take(NT, AH)
            into, whole, onward = core.take(NT, AH), core.take(NT, AH), core.take(NT, AH)
            alog, bias = core.take(AH), core.take(AH)
            ngain = core.take(AD)
            soft = [core.take(NT * AH) for _ in range(3)]
            norm_r = [core.take(NT * 2 * AH) for _ in range(3)]
            tok = core.take(NT, QKV)
            base = core.top
            PAD = TAPS_2 - 1
            up = core.take(12, T + PAD)
            cv = core.take(12, T)
            core.top = base
            (s_par, sp0, sp1, s_a, s_g, s_sums, s_exp, pads, conv_ready, feat_ready, s_turned, tok_ready, sq_ready,
             v_ready, root_ready, s_beta) = (
                sem(f"delta_{n}") for n in ("parameters_landed", "softplus_arg", "softplus_exp", "a_log_exp",
                                            "log_decays_ready", "decay_sums_ready", "decays_ready", "pads_zeroed",
                                            "conv_ready", "features_ready", "turned", "tokens_ready",
                                            "squares_ready", "variance_ready", "root_ready", "beta_ready"))
            wv = w2.rearrange("(k p) n -> p k n", p=P)
            al = OFF2["a_beta"]

            def ba_store(eng, i, u, acc):
                eng.activation(beta[:, u, :], acc[:, 0:AH], ACT.Sigmoid)
                return eng.activation(g[:, u, :], acc[:, AH:2 * AH], ACT.Copy)
            first = project([
                Job("features", columns_of(w2, DC, 512), hT, DC, 512, 3,
                    lambda eng, i, u, acc: eng.activation(up[:, i * 4 + u, PAD:PAD + T], acc, ACT.Copy)),
                Job("tokens", columns_of(w2, DC, 512, OFF2["a_z"]), hT, DC, 512, 1,
                    lambda eng, i, u, acc: eng.activation(zt[:, u, :], acc, ACT.Silu)),
                Job("tokens", columns_of(w2, DC, 2 * AH, al), hT, DC, 2 * AH, 1, ba_store)])
            first_sp, first_act = first["sp"], first["act"]

            before = len(stages)

            def sync(sp):
                core.begin(sp, before)
                for dst, src, n in ((alog, "a_log_2", AH), (bias, "dt_bias_2", AH), (ngain, "a_norm_g_2", AD)):
                    sp.dma_start(dst, broadcast(IN[src], n)).then_inc(s_par, 16)
                first_sp(sp)

            def scalar(act):
                act.wait_ge(pads, 1)
                first_act(act)
            first.update(sp=sync, act=scalar)
            first["dve"] = lambda dve: dve.memset(up[:, :, 0:PAD], 0.0).then_inc(pads, 1)
            yield first

            gf = g.rearrange("p c h -> p (c h)")
            soft_v, soft_a = softplus(gf, soft[0], soft[1], soft[2], (sp0, sp1), 0, None)
            cw = col["conv_w_2"].rearrange("p (t c) -> p t c", t=TAPS_2)

            def conv_vector(dve):
                dve.wait_ge(s_par, 48)
                dve.tensor_tensor(g, g, bias.unsqueeze(1).to_broadcast([P, NT, AH]), ALU.add)
                dve.drain()
                soft_v(dve)
                dve.wait_ge(s_a, 1)
                dve.scalar_tensor_tensor(out=g, in0=g, scalar=-1.0, in1=alog.unsqueeze(1).to_broadcast([P, NT, AH]),
                                         op0=ALU.mult, op1=ALU.mult).then_inc(s_g, 1)
                for c in range(12):
                    dve.tensor_scalar(cv[:, c, :], up[:, c, 0:T], cw[:, 0, c:c + 1], None, ALU.mult)
                for k in range(1, TAPS_2):
                    dve.drain()
                    for c in range(12):
                        ins = dve.scalar_tensor_tensor(out=cv[:, c, :], in0=up[:, c, k:k + T],
                                                       scalar=cw[:, k, c:c + 1], in1=cv[:, c, :],
                                                       op0=ALU.mult, op1=ALU.add)
                        if k == TAPS_2 - 1:
                            ins.then_inc(conv_ready, 1)
                v, r, a = norm_r
                dve.wait_ge(sq_ready, NT)
                for t in range(NT):
                    dve.tensor_reduce(v[:, t * 2 * AH:(t + 1) * 2 * AH],
                                      squares[:, t, :].rearrange("p (h n) -> p h n", n=AD), AX.X, ALU.add)
                dve.drain()
                dve.tensor_scalar(v, v, EPS, None, ALU.add).then_inc(v_ready, 1)
                dve.wait_ge(root_ready, 1)
                newton_rsqrt(core, dve, v, r, a)
                r3 = r.rearrange("p (t h) -> p t h", t=NT)
                dve.tensor_scalar(r3[:, :, 0:AH], r3[:, :, 0:AH], AD ** -0.5, None, ALU.mult)
                dve.drain()
                for t in range(NT):
                    x = tok[:, t, 0:2 * AH * AD].rearrange("p (h n) -> p h n", n=AD)
                    dve.tensor_tensor(x, x, r3[:, t, :].unsqueeze(2).to_broadcast([P, 2 * AH, AD]), ALU.mult)

            squares = up.rearrange("p a b -> p (a b)")[:, 0:NT * 2 * AH * AD].rearrange("p (t n) -> p t n", t=NT)

            def conv_scalar(act):
                act.wait_ge(s_par, 48)
                act.activation(alog, alog, ACT.Exp).then_inc(s_a, 1)
                soft_a(act)
                act.wait_ge(s_sums, 1)
                for n, dst in enumerate((into, whole, onward)):
                    act.activation(dst.rearrange("p c h -> p (c h)"), ps[:, 7, n * 32:(n + 1) * 32], ACT.Exp)
                for c in range(12):
                    act.wait_ge(conv_ready, c + 1)
                    act.activation(cv[:, c, :], cv[:, c, :], ACT.Silu).then_inc(feat_ready, 1)
                for c in range(12):
                    act.wait_ge(s_turned, c + 1)
                    act.activation(tok[:, :, c * P:(c + 1) * P], ps[:, c % 6, :].rearrange("p (t n) -> p t n", t=NT),
                                   ACT.Copy).then_inc(tok_ready, 1)
                act.wait_ge(tok_ready, 12)
                for t in range(NT):
                    act.activation(squares[:, t, :], tok[:, t, 0:2 * AH * AD], ACT.Square).then_inc(sq_ready, 1)
                act.wait_ge(v_ready, 1)
                act.activation(norm_r[1], norm_r[0], ACT.Sqrt).then_inc(root_ready, 1)

            def conv_tensor(pe):
                pe.wait_ge(s_g, 1)
                for n, mask in enumerate((LE, core.ones, GT)):
                    mm = nc.tensor.matmul(ps[:, 7, n * 32:(n + 1) * 32], mask, gf, start=True, stop=True)
                mm.then_inc(s_sums, 1)
                for c in range(12):
                    pe.wait_ge(feat_ready, c + 1)
                    if c >= 6:
                        pe.wait_ge(tok_ready, c - 5)
                    for t in range(NT):
                        mm = nc.tensor.transpose(ps[:, c % 6, t * P:(t + 1) * P], cv[:, c, t * P:(t + 1) * P],
                                                 core.ident)
                    mm.then_inc(s_turned, 1)
            yield dict(pe=conv_tensor, act=conv_scalar, dve=conv_vector)

            core.top = base
            qkT = core.take(8, T)
            qdT = core.take(4, T)
            kb = core.take(NT, AH * AD)
            vb = core.take(NT, AH * AD)
            kd = core.take(NT, AH * AD)
            after = core.top
            qd = core.take(NT, AH * AD)
            (made, t_turned, t_copied) = (sem(f"delta_{n}") for n in ("decayed_made", "qk_turned", "qk_copied"))
            hd = lambda t: t.rearrange("p (h n) -> p h n", n=AD)
            spread = lambda t: t.unsqueeze(2).to_broadcast([P, AH, AD])

            def prep_pool(gp):
                for c in range(NT):
                    q, k, v = (tok[:, c, n * 512:(n + 1) * 512] for n in range(3))
                    gp.tensor_tensor(hd(qd[:, c, :]), hd(q), spread(into[:, c, :]), ALU.mult)
                    gp.tensor_tensor(hd(vb[:, c, :]), hd(v), spread(beta[:, c, :]), ALU.mult)
                    gp.tensor_tensor(hd(kd[:, c, :]), hd(k), spread(onward[:, c, :]), ALU.mult)
                    gp.tensor_tensor(hd(kb[:, c, :]), hd(k), spread(beta[:, c, :]), ALU.mult)
                gp.drain()
                for c in range(NT):
                    ins = gp.tensor_tensor(hd(kb[:, c, :]), hd(kb[:, c, :]), spread(into[:, c, :]), ALU.mult)
                gp.drain().then_inc(made, 1)

            def prep_tensor(pe):
                for c in range(12):
                    if c >= 8:
                        pe.wait_ge(made, 1)
                        pe.wait_ge(t_copied, c - 7)
                    src = tok[:, :, c * P:(c + 1) * P] if c < 8 else qd[:, :, (c - 8) * P:(c - 7) * P]
                    for t in range(NT):
                        mm = nc.tensor.transpose(ps[:, c % 8, t * P:(t + 1) * P], src[:, t, :], core.ident)
                    mm.then_inc(t_turned, 1)

            def prep_scalar(act):
                for c in range(12):
                    act.wait_ge(t_turned, c + 1)
                    act.activation(qkT[:, c, :] if c < 8 else qdT[:, c - 8, :], ps[:, c % 8, :], ACT.Copy)\
                        .then_inc(t_copied, 1)
            yield dict(pe=prep_tensor, act=prep_scalar, pool=prep_pool)

            core.top = after
            B4 = 4
            LEVELS = 7
            levels = core.take(LEVELS, P)
            levelsT = core.take(LEVELS, P)
            gm = core.take(2, B4, P)
            E = core.take(2, B4 * P)
            N = core.take(B4, P)
            NTr = core.take(B4, P)
            NL = core.take(B4, P)
            X = core.take(B4, P)
            XT = core.take(B4, P)
            Y = core.take(B4, P)
            QK = core.take(2, B4, P)
            U = core.take(2, B4 * AD)
            WT = core.take(4, P)
            V = core.take(2, B4 * AD)
            S = core.take(4, AD)
            O = tok
            core.top = mark + 0
            b4 = lambda t: t.rearrange("p (r n) -> p r n", r=B4)
            wide = lambda t: t.rearrange("p r n -> p (r n)")
            over = lambda m: m.unsqueeze(1).to_broadcast([P, B4, P])
            names = ("masks_made", "steps_made", "sums_ready", "decays_ready", "products_ready", "n_made", "n_turned",
                     "nt_copied", "level_masked", "y_made", "y_copied", "z_made", "x_updated", "uw_ready", "uw_copied",
                     "ws_ready", "v_ready", "out_made", "out_stored", "state_updated", "qk_made", "x_started")
            (masks, steps, sums, decays, prods, n_made, n_turned, nt_copied, lmasked, y_made, y_copied, z_made, x_up,
             uw_ready, uw_copied, ws_ready, v_made, out_made, out_stored, state_up, qk_made, x_start) = (
                sem(f"delta_{n}_") for n in names)

            def mask_pool(gp):
                for tile, lower in ((levels, True), (levelsT, False)):
                    gp.memset(tile, 0.0)
                gp.drain()
                for l in range(LEVELS):
                    b = 1 << l
                    nb = P // (2 * b)
                    v = levels[:, l, :].rearrange("p (n a b) -> p n a b", a=2, b=b)[:, :, 0, :]
                    vT = levelsT[:, l, :].rearrange("p (n a b) -> p n a b", a=2, b=b)[:, :, 1, :]
                    gp.memset(v, 1.0)
                    gp.memset(vT, 1.0)
                gp.drain()
                for l in range(LEVELS):
                    b = 1 << l
                    nb = P // (2 * b)
                    v = levels[:, l, :].rearrange("p (n a b) -> p n a b", a=2, b=b)[:, :, 0, :]
                    vT = levelsT[:, l, :].rearrange("p (n a b) -> p n a b", a=2, b=b)[:, :, 1, :]
                    gp.affine_select(out=v, in_=v, compare_op=ALU.is_ge, fill=0.0, base=-b,
                                     pattern=[[-2 * b, nb], [0, b]], channel_multiplier=1)
                    gp.affine_select(out=vT, in_=vT, compare_op=ALU.is_ge, fill=0.0, base=0,
                                     pattern=[[-2 * b, nb], [0, b]], channel_multiplier=1)
                gp.drain()
                for l in range(LEVELS):
                    b = 1 << l
                    nb = P // (2 * b)
                    v = levels[:, l, :].rearrange("p (n a b) -> p n a b", a=2, b=b)[:, :, 0, :]
                    vT = levelsT[:, l, :].rearrange("p (n a b) -> p n a b", a=2, b=b)[:, :, 1, :]
                    gp.affine_select(out=v, in_=v, compare_op=ALU.is_ge, fill=0.0, base=2 * b - 1,
                                     pattern=[[2 * b, nb], [0, b]], channel_multiplier=-1)
                    gp.affine_select(out=vT, in_=vT, compare_op=ALU.is_ge, fill=0.0, base=b - 1,
                                     pattern=[[2 * b, nb], [0, b]], channel_multiplier=-1)
                gp.drain().then_inc(masks, 1)

            def of_batch(t, c, h):
                return t[:, c, :].rearrange("p (r b) -> p r b", b=2)[:, :, h]

            BATCHES = [(c, h) for c in range(NT) for h in range(2)]

            def delta_pool(gp):
                mask_pool(gp)
                for n, (c, h) in enumerate(BATCHES):
                    if n:
                        gp.wait_ge(sums, 2 * n)
                    gb = of_batch(g, c, h).unsqueeze(2).to_broadcast([P, B4, P])
                    gp.tensor_tensor(gm[:, 0], over(LE), gb, ALU.mult).then_inc(steps, 1)
                    gp.tensor_tensor(gm[:, 1], over(GT), gb, ALU.mult).then_inc(steps, 1)
                    for l in range(1, LEVELS):
                        gp.wait_ge(nt_copied, n + 1)
                        if l > 1 or n:
                            gp.wait_ge(y_made, n * (LEVELS - 1) + l - 1)
                        gp.tensor_tensor(NL, NTr, over(levelsT[:, l, :]), ALU.mult).then_inc(lmasked, 1)

            def pair(t, head, c):
                p0 = 64 * (head % 2)
                return t[p0:p0 + 64, head // 2, c * P:(c + 1) * P]

            def delta_tensor(pe):
                for n, (c, h) in enumerate(BATCHES):
                    hs = range(h, AH, 2)
                    p0 = 64 * h
                    for d, (m1, m2) in enumerate(((LE, GT), (GT, LE))):
                        pe.wait_ge(steps, 2 * n + d + 1)
                        if n:
                            pe.wait_ge(decays, 2 * (n - 1) + d + 1)
                            if d == 1:
                                pe.wait_ge(uw_copied, 2 * n)
                        for r in range(B4):
                            mm = nc.tensor.matmul(ps[:, d, r * P:(r + 1) * P], gm[:, d, r, :], m2,
                                                  start=True, stop=True)
                        mm.then_inc(sums, 1)
                    if n:
                        pe.wait_ge(qk_made, n)
                        pe.wait_ge(x_up, n * (LEVELS - 1) * 2)
                    for r, head in enumerate(hs):
                        kk = pair(qkT[:, 4:8], head, c)
                        nc.tensor.matmul(ps[:, 2, r * P:(r + 1) * P], kk, kk, start=True, stop=True)
                    for r, head in enumerate(hs):
                        mm = nc.tensor.matmul(ps[:, 3, r * P:(r + 1) * P], pair(qkT[:, 4:8], head, c),
                                              pair(qkT, head, c), start=True, stop=True)
                    mm.then_inc(prods, 1)
                    pe.wait_ge(n_made, n + 1)
                    for r in range(B4):
                        mm = nc.tensor.transpose(ps[:, 4, r * P:(r + 1) * P], N[:, r, :], core.ident)
                    mm.then_inc(n_turned, 1)
                    pe.wait_ge(x_start, n + 1)
                    for l in range(1, LEVELS):
                        k = n * (LEVELS - 1) + l
                        pe.wait_ge(lmasked, k)
                        if k > 1:
                            pe.wait_ge(x_up, 2 * (k - 1))
                        for r in range(B4):
                            mm = nc.tensor.matmul(ps[:, 4, r * P:(r + 1) * P], NL[:, r, :], X[:, r, :],
                                                  start=True, stop=True)
                        mm.then_inc(y_made, 1)
                        pe.wait_ge(y_copied, k)
                        for r in range(B4):
                            mm = nc.tensor.matmul(ps[:, 5, r * P:(r + 1) * P], XT[:, r, :], Y[:, r, :],
                                                  start=True, stop=True)
                        mm.then_inc(z_made, 1)
                        for r in range(B4):
                            mm = nc.tensor.matmul(ps[:, 6, r * P:(r + 1) * P], Y[:, r, :], XT[:, r, :],
                                                  start=True, stop=True)
                        mm.then_inc(z_made, 1)
                    pe.wait_ge(x_up, (n + 1) * (LEVELS - 1) * 2)
                    for r, head in enumerate(hs):
                        mm = nc.tensor.matmul(ps[:, 7, r * AD:(r + 1) * AD], XT[:, r, :],
                                              vb[:, c, head * AD:(head + 1) * AD], start=True, stop=True)
                    mm.then_inc(uw_ready, 1)
                    for r, head in enumerate(hs):
                        mm = nc.tensor.matmul(ps[p0:p0 + 64, 1, r * P:(r + 1) * P],
                                              kb[:, c, head * AD:(head + 1) * AD], XT[:, r, :],
                                              start=True, stop=True)
                    mm.then_inc(uw_ready, 1)
                    pe.wait_ge(uw_copied, 2 * (n + 1))
                    if c or h:
                        pe.wait_ge(state_up, n)
                    for r, head in enumerate(hs):
                        mm = nc.tensor.matmul(ps[:, 7, r * AD:(r + 1) * AD],
                                              WT[p0:p0 + 64, r, :], S[p0:p0 + 64, r, :],
                                              start=True, stop=True)
                    mm.then_inc(ws_ready, 1)
                    pe.wait_ge(v_made, n + 1)
                    pe.wait_ge(qk_made, n + 1)
                    for r, head in enumerate(hs):
                        o = ps[:, 4, r * AD:(r + 1) * AD]
                        nc.tensor.matmul(o, pair(qdT, head, c), S[p0:p0 + 64, r, :], start=True, stop=False)
                        mm = nc.tensor.matmul(o, QK[:, h, r, :], V[:, h, r * AD:(r + 1) * AD],
                                              start=False, stop=True)
                    mm.then_inc(out_made, 1)
                    for r, head in enumerate(hs):
                        mm = nc.tensor.matmul(ps[p0:p0 + 64, 5, r * AD:(r + 1) * AD],
                                              kd[:, c, head * AD:(head + 1) * AD],
                                              V[:, h, r * AD:(r + 1) * AD], start=True, stop=True)
                    mm.then_inc(out_made, 1)

            def delta_scalar(act):
                for n, (c, h) in enumerate(BATCHES):
                    if n:
                        act.wait_ge(n_made, n)
                        act.wait_ge(qk_made, n)
                    for d in range(2):
                        act.wait_ge(sums, 2 * n + d + 1)
                        act.activation(E[:, d, :], ps[:, d, :], ACT.Exp).then_inc(decays, 1)
                    act.wait_ge(n_turned, n + 1)
                    if n:
                        act.wait_ge(lmasked, n * (LEVELS - 1))
                    act.activation(wide(NTr), ps[:, 4, :], ACT.Copy).then_inc(nt_copied, 1)
                    for l in range(1, LEVELS):
                        k = n * (LEVELS - 1) + l
                        act.wait_ge(y_made, k)
                        if k > 1:
                            act.wait_ge(z_made, 2 * (k - 1))
                        act.activation(wide(Y), ps[:, 4, :], ACT.Copy).then_inc(y_copied, 1)
                    act.wait_ge(uw_ready, 2 * n + 1)
                    if n:
                        act.wait_ge(v_made, n)
                    act.activation(U[:, h, :], ps[:, 7, 0:B4 * AD], ACT.Copy).then_inc(uw_copied, 1)
                    act.wait_ge(uw_ready, 2 * n + 2)
                    if n:
                        act.wait_ge(ws_ready, n)
                    q = slice(64 * h, 64 * h + 64)
                    act.activation(wide(WT[q]), ps[q, 1, :], ACT.Copy).then_inc(uw_copied, 1)

            def delta_vector(dve):
                dve.memset(S, 0.0)
                dve.wait_ge(masks, 1)
                dve.drain()
                for n, (c, h) in enumerate(BATCHES):
                    bb = of_batch(beta, c, h).unsqueeze(2).to_broadcast([P, B4, P])
                    dve.wait_ge(prods, n + 1)
                    dve.tensor_tensor(N, b4(ps[:, 2, :]), over(GT), ALU.mult)
                    dve.tensor_tensor(QK[:, h], b4(ps[:, 3, :]), over(LE), ALU.mult)
                    dve.drain()
                    dve.wait_ge(decays, 2 * n + 1)
                    dve.tensor_tensor(N, N, b4(E[:, 0, :]), ALU.mult)
                    dve.wait_ge(decays, 2 * n + 2)
                    dve.tensor_tensor(QK[:, h], QK[:, h], b4(E[:, 1, :]), ALU.mult).then_inc(qk_made, 1)
                    dve.drain()
                    dve.tensor_tensor(N, N, bb, ALU.mult).then_inc(n_made, 1)
                    dve.drain()
                    dve.tensor_tensor(X, N, over(levels[:, 0, :]), ALU.mult)
                    dve.drain()
                    dve.tensor_tensor(X, over(core.ident), X, ALU.subtract)
                    dve.wait_ge(nt_copied, n + 1)
                    dve.tensor_tensor(XT, NTr, over(levelsT[:, 0, :]), ALU.mult)
                    dve.drain()
                    dve.tensor_tensor(XT, over(core.ident), XT, ALU.subtract).then_inc(x_start, 1)
                    for l in range(1, LEVELS):
                        k = n * (LEVELS - 1) + l
                        dve.wait_ge(z_made, 2 * k)
                        dve.tensor_tensor(wide(X), wide(X), ps[:, 5, :], ALU.subtract).then_inc(x_up, 1)
                        dve.tensor_tensor(wide(XT), wide(XT), ps[:, 6, :], ALU.subtract).then_inc(x_up, 1)
                        dve.drain()
                    dve.wait_ge(ws_ready, n + 1)
                    dve.tensor_tensor(V[:, h, :], U[:, h, :], ps[:, 7, 0:B4 * AD], ALU.subtract).then_inc(v_made, 1)
                    dve.wait_ge(out_made, 2 * n + 1)
                    dve.tensor_copy(O[:, c, 0:512].rearrange("p (r b n) -> p r b n", b=2, n=AD)[:, :, h, :],
                                    ps[:, 4, 0:B4 * AD].rearrange("p (r n) -> p r n", r=B4))
                    dve.wait_ge(out_made, 2 * n + 2)
                    q = slice(64 * h, 64 * h + 64)
                    dve.tensor_tensor(S[q], S[q], of_batch(whole, c, h)[q].unsqueeze(2).to_broadcast([64, B4, AD]),
                                      ALU.mult)
                    dve.drain()
                    dve.tensor_tensor(wide(S[q]), wide(S[q]), ps[q, 5, 0:B4 * AD], ALU.add)\
                        .then_inc(state_up, 1)
            yield dict(pool=delta_pool, pe=delta_tensor, act=delta_scalar, dve=delta_vector)

            core.top = base
            oT = core.take(4, T)
            gate = core.take(DC, T)
            sqs = core.take(NT, AH * AD)
            osq, ov, oroot, ogain, oturned = (sem(f"delta_out_{n}") for n in (
                "squares_ready", "variance_ready", "root_ready", "gained", "turned"))
            v, r, a = (t[:, 0:NT * AH] for t in norm_r)
            oturn = turn(O[:, :, 0:512], oT, 4, oturned, 0)

            def out_scalar(act):
                act.activation(sqs, O[:, :, 0:512], ACT.Square).then_inc(osq, 1)
                act.wait_ge(ov, 1)
                act.activation(r, v, ACT.Sqrt).then_inc(oroot, 1)

            def out_vector(dve):
                dve.wait_ge(osq, 1)
                for t in range(NT):
                    dve.tensor_reduce(v[:, t * AH:(t + 1) * AH], hd(sqs[:, t, :]), AX.X, ALU.add)
                dve.drain()
                dve.tensor_scalar(v, v, 1.0 / AD, EPS, ALU.mult, ALU.add).then_inc(ov, 1)
                dve.wait_ge(oroot, 1)
                newton_rsqrt(core, dve, v, r, a)
                for t in range(NT):
                    o = hd(O[:, t, 0:512])
                    dve.tensor_tensor(o, o, spread(r[:, t * AH:(t + 1) * AH]), ALU.mult)
                    dve.drain()
                    dve.tensor_tensor(o, o, ngain.unsqueeze(1).to_broadcast([P, AH, AD]), ALU.mult)
                    dve.drain()
                    ins = dve.tensor_tensor(O[:, t, 0:512], O[:, t, 0:512], zt[:, t, :], ALU.mult)
                ins.then_inc(ogain, 1)
                oturn["dve"](dve)

            def out_tensor(pe):
                pe.wait_ge(ogain, 1)
                oturn["pe"](pe)
            yield dict(act=out_scalar, dve=out_vector, pe=out_tensor)
            core.top = mark
            yield project([
                Job("features", columns_of(w2, DC, 512, OFF2["gate_a"]), hT, DC, 512, 2,
                    gate_store(gate, col["b_gate_2"][:, 0:8])),
                Job("features", columns_of(IN["w_proj_a_2"][0], 4, 512), oT, 4, 512, 2,
                    times_store(gated, gate), on="dve")])

        def stages_sparse(gated):
            mark = core.top
            SLOTS = 22
            RK, RI, RIK = 8, 12, 20
            v = core.take(NT, BKV * 64)
            iw = core.take(NT, IH)
            inv = core.take(32)
            pos_f = core.take(NT)
            pos_i = core.take(NT)
            sin, cos = core.take(NT, 32), core.take(NT, 32)
            ang, kk, t1 = core.take(NT, 32), core.take(NT, 32), core.take(NT, 32)
            base = core.top
            R = core.take(NT, SLOTS * 64)
            F = core.take(SLOTS // 2, T)
            tmp = core.take(2, 20 * 32)
            heads_of = lambda t, a, b: R[:, t, a * 64:b * 64].rearrange("p (h n) -> p h n", n=64)
            s_pos, s_inv, s_ang, s_trig, pools, s_rot, s_turned, s_copied2 = (
                sem(f"sparse_{n}") for n in ("positions_landed", "frequencies_made", "angles_ready", "sines_ready",
                                             "rotated_part", "rotated", "turned", "copied"))

            def bk_store(eng, i, u, acc):
                for h in range(BKV):
                    eng.activation(heads_of(u, RK + 2 * h, RK + 2 * h + 1), acc[:, h * 64:(h + 1) * 64].unsqueeze(1),
                                   ACT.Copy)
                return eng.activation(v[:, u, :], acc[:, 128:256], ACT.Copy)

            def ik_store(eng, i, u, acc):
                eng.activation(R[:, u, RIK * 64:(RIK + 1) * 64], acc[:, 0:64], ACT.Copy)
                return eng.activation(iw[:, u, :], acc[:, 64:72], ACT.Copy, scale=float((IH * 64) ** -0.5))
            first = project([
                Job("tokens", columns_of(w2, DC, 512, OFF2["b_q"]), hT, DC, 512, 1,
                    lambda eng, i, u, acc: eng.activation(R[:, u, 0:512], acc, ACT.Copy)),
                Job("tokens", columns_of(w2, DC, 256, OFF2["b_k"]), hT, DC, 256, 1, bk_store),
                Job("tokens", columns_of(w2, DC, 512, OFF2["i_q"]), hT, DC, 512, 1,
                    lambda eng, i, u, acc: eng.activation(R[:, u, RI * 64:(RI + 8) * 64], acc, ACT.Copy)),
                Job("tokens", columns_of(w2, DC, 72, OFF2["i_k"]), hT, DC, 72, 1, ik_store)])
            first_sp = first["sp"]
            before = len(stages)

            def sync(sp):
                core.begin(sp, before)
                sp.dma_start(pos_i.bitcast(I32), IN["positions_2"][0].rearrange("(t p) -> p t", p=P),
                             allow_slow_non_contiguous=True).then_inc(s_pos, 16)
                first_sp(sp)

            def freq_pool(gp):
                for i in range(32):
                    gp.memset(inv[:, i:i + 1], float(ROPE_INV[i]))
                gp.drain().then_inc(s_inv, 1)

            def angle_vector(dve):
                dve.wait_ge(s_pos, 16)
                dve.tensor_copy(pos_f, pos_i.bitcast(I32))
                dve.wait_ge(s_inv, 1)
                dve.drain()
                for t in range(NT):
                    dve.tensor_scalar(ang[:, t, :], inv, pos_f[:, t:t + 1], None, ALU.mult)
                dve.drain()
                TWO_PI = 2 * np.pi
                c1 = float(np.float32(6.28125))
                c2 = float(np.float32(TWO_PI - c1))
                c2 = float(np.array(c2, np.float32).view(np.uint32).__and__(0xFFFFF000).astype(np.uint32).view(np.float32))
                c3 = float(np.float32(TWO_PI - c1 - c2))
                MAGIC = 1.5 * 2.0 ** 23
                for dst, shift, edge in ((sin, 0.0, 0.0), (cos, 0.25, np.pi / 2)):
                    dve.tensor_scalar(kk, ang, 1.0 / TWO_PI, shift, ALU.mult, ALU.add)
                    dve.drain()
                    dve.tensor_scalar(kk, kk, MAGIC, None, ALU.add)
                    dve.drain()
                    dve.tensor_scalar(kk, kk, -MAGIC, None, ALU.add)
                    dve.drain()
                    dve.scalar_tensor_tensor(out=dst, in0=kk, scalar=-c1, in1=ang, op0=ALU.mult, op1=ALU.add)
                    dve.drain()
                    dve.scalar_tensor_tensor(out=dst, in0=kk, scalar=-c2, in1=dst, op0=ALU.mult, op1=ALU.add)
                    dve.drain()
                    dve.scalar_tensor_tensor(out=dst, in0=kk, scalar=-c3, in1=dst, op0=ALU.mult, op1=ALU.add)
                    dve.drain()
                    if edge:
                        dve.tensor_scalar(dst, dst, edge, None, ALU.add)
                        dve.drain()
                    dve.tensor_scalar(dst, dst, float(np.float32(3.1415925)), -float(np.float32(3.1415925)),
                                      ALU.min, ALU.max)
                dve.drain().then_inc(s_ang, 1)
            first.update(sp=sync, pool=freq_pool, dve=angle_vector)
            yield first

            def rotate(eng, t, a, b, c, s_, x, y):
                n = b - a
                h = heads_of(t, a, b)
                x1, x2 = h[:, :, 0:32], h[:, :, 32:64]
                cb_ = cos[:, t, :].unsqueeze(1).to_broadcast([P, n, 32])
                sb_ = sin[:, t, :].unsqueeze(1).to_broadcast([P, n, 32])
                xx = x[:, 0:n * 32].rearrange("p (h n) -> p h n", n=32)
                yy = y[:, 0:n * 32].rearrange("p (h n) -> p h n", n=32)
                eng.tensor_tensor(xx, x2, sb_, ALU.mult)
                eng.tensor_tensor(yy, x1, sb_, ALU.mult)
                eng.drain()
                eng.tensor_tensor(x1, x1, cb_, ALU.mult)
                eng.tensor_tensor(x2, x2, cb_, ALU.mult)
                eng.drain()
                eng.tensor_tensor(x1, x1, xx, ALU.subtract)
                eng.tensor_tensor(x2, x2, yy, ALU.add)
                eng.drain()

            tmp2 = core.take(2, 20 * 32)
            MAPS = ((RK + 1, RK), (RK + 3, RK + 2), (RIK + 1, RIK))

            def rot(eng, tiles, buf, name):
                eng.wait_ge(s_trig, 1)
                for t in tiles:
                    for a, b in ((0, 8), (RK, RK + 1), (RK + 2, RK + 3), (RI, RIK + 1)):
                        rotate(eng, t, a, b, cos, sin, buf[:, 0], buf[:, 1])
                    for dst, src in MAPS:
                        eng.tensor_copy(R[:, t, dst * 64:(dst + 1) * 64], R[:, t, src * 64:(src + 1) * 64])
                    eng.drain().then_inc(s_rot if name == "dve" else pools, 1)

            def rot_tensor(pe):
                pe.wait_ge(s_rot, 2)
                pe.wait_ge(pools, 2)
                for c in range(SLOTS // 2):
                    if c >= 8:
                        pe.wait_ge(s_copied2, c - 7)
                    for t in range(NT):
                        mm = nc.tensor.transpose(ps[:, c % 8, t * P:(t + 1) * P], R[:, t, c * P:(c + 1) * P],
                                                 core.ident)
                    mm.then_inc(s_turned, 1)

            def rot_scalar(act):
                act.wait_ge(s_ang, 1)
                act.activation(sin.rearrange("p t n -> p (t n)"), sin.rearrange("p t n -> p (t n)"), ACT.Sin)
                act.activation(cos.rearrange("p t n -> p (t n)"), cos.rearrange("p t n -> p (t n)"), ACT.Sin)
                act.drain().then_inc(s_trig, 1)
                for c in range(SLOTS // 2):
                    act.wait_ge(s_turned, c + 1)
                    act.activation(F[:, c, :], ps[:, c % 8, :], ACT.Copy).then_inc(s_copied2, 1)
            yield dict(act=rot_scalar, pe=rot_tensor, dve=lambda e: rot(e, (0, 1), tmp, "dve"),
                       pool=lambda e: rot(e, (2, 3), tmp2, "pool"))

            core.top = base
            bias = core.take(NT, T)
            score = core.take(NT, T)
            relu = core.take(2, T)
            best = core.take(8)
            assert core.top <= base + NT * SLOTS * 64
            qF, kF, iqF, ikF = F[:, 0:4], F[:, 4:6], F[:, 6:10], F[:, 10]
            i_scored, i_relu, i_used, i_picked = (sem(f"index_{n}") for n in ("scored", "rectified", "added", "picked"))
            FOUND = -3e38
            IU = [(t, h) for t in range(NT) for h in range(IH)]

            def index_tensor(pe):
                for n, (t, h) in enumerate(IU):
                    p0 = 64 * (h % 2)
                    if n >= 2:
                        pe.wait_ge(i_relu, n - 1)
                    nc.tensor.matmul(ps[:, n % 2, 0:(t + 1) * P], iqF[p0:p0 + 64, h // 2, t * P:(t + 1) * P],
                                     ikF[p0:p0 + 64, 0:(t + 1) * P], start=True, stop=True).then_inc(i_scored, 1)

            def index_scalar(act):
                for n, (t, h) in enumerate(IU):
                    act.wait_ge(i_scored, n + 1)
                    if n >= 2:
                        act.wait_ge(i_used, n - 1)
                    act.activation(relu[:, n % 2, 0:(t + 1) * P], ps[:, n % 2, 0:(t + 1) * P], ACT.Relu)\
                        .then_inc(i_relu, 1)

            def index_vector(dve):
                for n, (t, h) in enumerate(IU):
                    k = (t + 1) * P
                    sc = score[:, t, 0:k]
                    dve.wait_ge(i_relu, n + 1)
                    if h == 0:
                        dve.tensor_scalar(sc, relu[:, n % 2, 0:k], iw[:, t, 0:1], None, ALU.mult).then_inc(i_used, 1)
                    else:
                        dve.drain()
                        dve.scalar_tensor_tensor(out=sc, in0=relu[:, n % 2, 0:k], scalar=iw[:, t, h:h + 1], in1=sc,
                                                 op0=ALU.mult, op1=ALU.add).then_inc(i_used, 1)
                    if h < IH - 1:
                        continue
                    dve.drain()
                    dve.memset(score[0:CAUSAL, t, k - CAUSAL:k], NEG)
                    dve.drain()
                    if k <= TOPK:
                        dve.tensor_scalar(bias[:, t, 0:k], sc, NEG / 2, NEG, ALU.is_le, ALU.mult)
                        continue
                    for _ in range(TOPK // 8):
                        dve.max(best, sc)
                        dve.drain()
                        dve.match_replace(out=sc, in_to_replace=best, in_values=sc, imm_value=FOUND)
                        dve.drain()
                    dve.tensor_scalar(bias[:, t, 0:k], sc, FOUND / 2, NEG, ALU.is_gt, ALU.mult)
            yield dict(pe=index_tensor, act=index_scalar, dve=index_vector)

            core.top = base + NT * T
            s, pr, pt = core.take(2, T), core.take(2, T), core.take(2, T)
            U = BH * NT
            shift, total, den = (core.take(U) for _ in range(3))
            assert core.top <= base + NT * SLOTS * 64
            core.top = base + NT * SLOTS * 64 + SLOTS // 2 * T
            o = core.take(NT, BH * 64)
            (scores_ready, scores_read, shift_ready, probs_ready, probs_turned, turned_copied, out_ready,
             out_stored) = (sem(f"sparse_{n}") for n in (
                 "scores_ready", "scores_read", "shift_ready", "probs_ready", "probs_turned", "turned_copied",
                 "mix_ready", "mix_stored"))
            units = [(t, h) for t in range(NT) for h in range(BH)]

            def tensor(pe):
                for u in range(U + 2):
                    if u < U:
                        t, h = units[u]
                        p0 = 64 * (h % 2)
                        if u >= 2:
                            pe.wait_ge(scores_read, u - 1)
                        nc.tensor.matmul(ps[:, u % 2, 0:(t + 1) * P], qF[p0:p0 + 64, h // 2, t * P:(t + 1) * P],
                                         kF[p0:p0 + 64, h // 4, 0:(t + 1) * P], start=True, stop=True)\
                            .then_inc(scores_ready, 1)
                    if 1 <= u <= U:
                        n = u - 1
                        t, h = units[n]
                        pe.wait_ge(probs_ready, n + 1)
                        if n >= 2:
                            pe.wait_ge(turned_copied, n - 1)
                        for k in range(t + 1):
                            mm = nc.tensor.transpose(ps[:, 2 + n % 2, k * P:(k + 1) * P],
                                                     pr[:, n % 2, k * P:(k + 1) * P], core.ident)
                        mm.then_inc(probs_turned, 1)
                    if u >= 2:
                        n = u - 2
                        t, h = units[n]
                        pe.wait_ge(turned_copied, n + 1)
                        if n >= 2:
                            pe.wait_ge(out_stored, n - 1)
                        for k in range(t + 1):
                            mm = nc.tensor.matmul(ps[:, 4 + n % 2, 0:64], pt[:, n % 2, k * P:(k + 1) * P],
                                                  v[:, k, (h // 4) * 64:(h // 4 + 1) * 64],
                                                  start=k == 0, stop=k == t)
                        mm.then_inc(out_ready, 1)

            def vector(dve):
                for u in range(U + 2):
                    if u < U:
                        t, h = units[u]
                        n = (t + 1) * P
                        dve.wait_ge(scores_ready, u + 1)
                        if u >= 2:
                            dve.wait_ge(probs_ready, u - 1)
                        dve.scalar_tensor_tensor(out=s[:, u % 2, 0:n], in0=ps[:, u % 2, 0:n], scalar=64 ** -0.5,
                                                 in1=bias[:, t, 0:n], op0=ALU.mult, op1=ALU.add)\
                            .then_inc(scores_read, 1)
                        dve.drain()
                        dve.tensor_reduce(shift[:, u:u + 1], s[:, u % 2, 0:n], AX.X, ALU.max, negate=True)\
                            .then_inc(shift_ready, 1)
                    if u >= 2:
                        n = u - 2
                        t, h = units[n]
                        dve.wait_ge(probs_ready, n + 1)
                        dve.reciprocal(den[:, n:n + 1], total[:, n:n + 1])
                        dve.drain()
                        dve.wait_ge(out_ready, n + 1)
                        dve.tensor_scalar(o[:, t, h * 64:(h + 1) * 64], ps[:, 4 + n % 2, 0:64], den[:, n:n + 1],
                                          None, ALU.mult).then_inc(out_stored, 1)

            def scalar(act):
                for u in range(U + 1):
                    if u < U:
                        t, h = units[u]
                        n = (t + 1) * P
                        act.wait_ge(shift_ready, u + 1)
                        if u >= 2:
                            act.wait_ge(probs_turned, u - 1)
                        act.activation(pr[:, u % 2, 0:n], s[:, u % 2, 0:n], ACT.Exp, bias=shift[:, u:u + 1],
                                       accum_out=total[:, u:u + 1]).then_inc(probs_ready, 1)
                    if u >= 1:
                        n = u - 1
                        t, h = units[n]
                        act.wait_ge(probs_turned, n + 1)
                        if n >= 2:
                            act.wait_ge(out_ready, n - 1)
                        act.activation(pt[:, n % 2, 0:(t + 1) * P], ps[:, 2 + n % 2, 0:(t + 1) * P], ACT.Copy)\
                            .then_inc(turned_copied, 1)
            yield dict(pe=tensor, dve=vector, act=scalar)
            core.top = base
            oT = core.take(4, T)
            gate = core.take(DC, T)
            yield turn(o, oT, 4, sem("sparse_mix_turned"), 0)
            core.top = mark
            yield project([
                Job("features", columns_of(w2, DC, 512, OFF2["gate_b"]), hT, DC, 512, 2,
                    gate_store(gate, col["b_gate_2"][:, 8:16])),
                Job("features", columns_of(IN["w_proj_b_2"][0], 4, 512), oT, 4, 512, 2,
                    add_times_store(gated, gate, 4), on="dve"),
                Job("features", columns_of(IN["w_out_2"][0], DC, 512), gated, DC, 512, 2, add_store(xT), on="dve",
                    needs=True)])

        def stages_moe():
            mark = core.top
            yield feature_norm(core, 0, xT, col["norm2_g_2"], hT)
            core.top = mark
            LG = EG + EXPERTS
            actT = core.take(2 * EXPERTS, T)
            share = core.take(EXPERTS, T)
            silu = core.take(2, 2, T)
            low = core.top
            logit = core.take(NT, LG)
            rb = core.take(LG)
            comb = core.take(NT, EXPERTS)
            combT = core.take(T)
            pick = actT[:, 2 * EXPERTS - 4:, :].rearrange("p a b -> p (a b)").rearrange("p (e n) -> p e n", e=EXPERTS)
            g4, e4, one1, one2, rem, tmp = (core.take(NT, EG) for _ in range(6))
            el16, mm1, mm2, sm = core.take(NT, EXPERTS), core.take(NT), core.take(NT), core.take(NT)
            s_rb, s_arg, s_exp, s_comb, s_ct, s_ctc, s_sh, s_shc = (
                sem(f"router_{n}") for n in ("bias_landed", "logits_shifted", "exponentials", "weights_made",
                                             "weights_turned", "weights_copied", "shares_made",
                                             "shares_stored"))
            wg = IN["w_router_group_2"][0].rearrange("(k p) n -> p k n", p=P)
            we = IN["w_router_expert_2"][0].rearrange("(k p) n -> p k n", p=P)
            first = project([Job("tokens", lambda i: [(0, wg), (EG, we)], hT, DC, LG, 1,
                                 lambda eng, i, u, acc: eng.activation(logit[:, u, :], acc[:, 0:LG], ACT.Copy))])
            first_sp = first["sp"]
            before = len(stages)

            def sync(sp):
                core.begin(sp, before)
                sp.dma_start(rb[:, 0:EG], broadcast(IN["b_router_group_2"], EG)).then_inc(s_rb, 16)
                sp.dma_start(rb[:, EG:LG], broadcast(IN["b_router_expert_2"], EXPERTS)).then_inc(s_rb, 16)
                first_sp(sp)
            first["sp"] = sync
            yield first

            def row_max(dve, dst, src):
                dve.tensor_reduce(dst, src, AX.X, ALU.max)
                dve.drain()

            def along(t):
                return t.unsqueeze(2).to_broadcast([P, NT, EG])

            def first_of(dve, one, src, top):
                dve.tensor_tensor(one, src, along(top), ALU.is_equal)
                dve.memset(rem[:, :, 0], 1.0)
                dve.drain()
                for j in range(EG):
                    if j:
                        dve.tensor_tensor(rem[:, :, 0], rem[:, :, 0], one[:, :, j - 1], ALU.subtract)
                        dve.drain()
                        dve.tensor_tensor(one[:, :, j], one[:, :, j], rem[:, :, 0], ALU.mult)
                        dve.drain()

            def router_vector(dve):
                dve.wait_ge(s_rb, 32)
                dve.tensor_tensor(logit, logit, rb.unsqueeze(1).to_broadcast([P, NT, LG]), ALU.add)
                dve.drain()
                dve.tensor_copy(g4, logit[:, :, 0:EG])
                dve.drain()
                row_max(dve, mm1, g4)
                first_of(dve, one1, g4, mm1)
                dve.tensor_tensor(g4, g4, along(mm1), ALU.subtract)
                dve.tensor_tensor(el16.rearrange("p t (g k) -> p t g k", g=EG),
                                  logit[:, :, EG:LG].rearrange("p t (g k) -> p t g k", g=EG),
                                  one1.unsqueeze(3).to_broadcast([P, NT, EG, EG]), ALU.mult)
                dve.drain()
                dve.tensor_reduce(e4, el16.rearrange("p t (g k) -> p t k g", g=EG), AX.X, ALU.add)
                dve.drain()
                row_max(dve, mm2, e4)
                dve.tensor_tensor(e4, e4, along(mm2), ALU.subtract)
                dve.drain().then_inc(s_arg, 1)
                dve.wait_ge(s_exp, 1)
                dve.tensor_reduce(mm1, g4, AX.X, ALU.add)
                dve.tensor_reduce(mm2, e4, AX.X, ALU.add)
                dve.drain()
                dve.reciprocal(mm1, mm1)
                dve.reciprocal(mm2, mm2)
                dve.drain()
                dve.tensor_tensor(e4, e4, along(mm2), ALU.mult)
                dve.drain()
                row_max(dve, sm, e4)
                first_of(dve, g4, e4, sm)
                dve.scalar_tensor_tensor(out=tmp, in0=g4, scalar=-2.0, in1=e4, op0=ALU.mult, op1=ALU.add)
                dve.drain()
                row_max(dve, sm, tmp)
                first_of(dve, one2, tmp, sm)
                dve.tensor_tensor(one2, one2, g4, ALU.add)
                dve.drain()
                dve.tensor_tensor(e4, e4, one2, ALU.mult)
                dve.drain()
                dve.tensor_reduce(sm, e4, AX.X, ALU.add)
                dve.drain()
                dve.reciprocal(sm, sm)
                dve.drain()
                dve.tensor_tensor(sm, sm, mm1, ALU.mult)
                dve.drain()
                dve.tensor_tensor(e4, e4, along(sm), ALU.mult)
                dve.drain()
                for gi in range(EG):
                    dve.tensor_tensor(comb[:, :, gi * EG:(gi + 1) * EG], e4,
                                      one1[:, :, gi:gi + 1].to_broadcast([P, NT, EG]), ALU.mult)
                dve.drain().then_inc(s_comb, 1)
                dve.wait_ge(s_ct, 1)
                dve.tensor_copy(combT[0:EXPERTS, :], ps[0:EXPERTS, 4, :]).then_inc(s_ctc, 1)

            def router_scalar(act):
                act.wait_ge(s_arg, 1)
                act.activation(g4, g4, ACT.Exp)
                act.activation(e4, e4, ACT.Exp)
                act.drain().then_inc(s_exp, 1)

            def router_tensor(pe):
                pe.wait_ge(s_comb, 1)
                for t in range(NT):
                    mm = nc.tensor.transpose(ps[0:EXPERTS, 4, t * P:(t + 1) * P], comb[:, t, :], core.ident)
                mm.then_inc(s_ct, 1)

            def router_pool(gp):
                gp.memset(pick, 1.0)
                gp.drain()
                gp.affine_select(out=pick, in_=pick, compare_op=ALU.is_equal, fill=0.0, base=0,
                                 pattern=[[-1, EXPERTS], [0, P]], channel_multiplier=1)
            yield dict(dve=router_vector, act=router_scalar, pe=router_tensor, pool=router_pool)
            def share_tensor(pe):
                for e in range(EXPERTS):
                    if e >= 4:
                        pe.wait_ge(s_shc, e - 3)
                    nc.tensor.matmul(ps[:, 4 + e % 4, :], pick[0:EXPERTS, e, :], combT[0:EXPERTS, :],
                                     start=True, stop=True).then_inc(s_sh, 1)

            def share_vector(dve):
                for e in range(EXPERTS):
                    dve.wait_ge(s_sh, e + 1)
                    dve.tensor_copy(share[:, e, :], ps[:, 4 + e % 4, :]).then_inc(s_shc, 1)
            yield dict(pe=share_tensor, dve=share_vector)

            w1v = IN["w_exp_gate_2"][0].rearrange("e (k p) n -> e p k n", p=P)
            w3v = IN["w_exp_up_2"][0].rearrange("e (k p) n -> e p k n", p=P)
            taken0 = core.taken_count["act"]

            def expert_weights(e):
                return [(0, pick_row(w1v, e)), (DE, pick_row(w3v, e))]

            def pick_row(t, e):
                return t[bass.ds(e, 1)].rearrange("a p k n -> (a p) k n")

            def parity_store(s):
                def store(eng, i, u, acc):
                    if u < 2:
                        return eng.activation(silu[:, s, u, :], acc, ACT.Silu)
                    dst = row(actT, 2 * i + (u - 2))
                    eng.wait_ge(core.unit_taken["act"].sem, taken0 + 2 * i + (u - 1))
                    eng.tensor_tensor(dst, acc, silu[:, s, u - 2, :], ALU.mult)
                    eng.drain()
                    return eng.tensor_tensor(dst, dst, row(share, i), ALU.mult)
                return store
            experts = Job("features", expert_weights, hT, DC, 2 * DE, EXPERTS, None,
                          on=("act", "act", "dve", "dve"), loop=True)
            experts.by_parity = [parity_store(0), parity_store(1)]
            yield project([experts, down(IN["w_exp_down_2"][0].rearrange("e f n -> (e f) n"), actT)])

        def stages_store():
            mark = core.top
            yield feature_norm(core, 0, xT, col["final_norm_g_2"], hT)
            core.top = mark
            final = core.take(NT, D)
            f_turned, f_copied = sem("result_turned"), sem("result_copied")

            def tensor(pe):
                for c in range(DC):
                    for t in range(NT):
                        mm = nc.tensor.transpose(ps[:, c, t * P:(t + 1) * P], hT[:, c, t * P:(t + 1) * P], core.ident)
                    mm.then_inc(f_turned, 1)

            def vector(dve):
                for c in range(0, DC, 2):
                    dve.wait_ge(f_turned, c + 1)
                    dve.tensor_copy(final[:, :, c * P:(c + 1) * P], ps[:, c, :].rearrange("p (t n) -> p t n", t=NT))

            def scalar(act):
                for c in range(1, DC, 2):
                    act.wait_ge(f_turned, c + 1)
                    act.activation(final[:, :, c * P:(c + 1) * P], ps[:, c, :].rearrange("p (t n) -> p t n", t=NT),
                                   ACT.Copy)
            yield dict(pe=tensor, dve=vector, act=scalar)
            before = len(stages)

            def sync(sp):
                core.begin(sp, before)
                for t in range(NT):
                    sp.dma_start(out[0, t * P:(t + 1) * P, :], final[:, t, :]).then_inc(s_out, 16)
                sp.wait_ge(s_out, 16 * NT)
            yield dict(sp=sync)

        stages = []
        run = stages.append
        run(stage_load())
        run(feature_norm(core, 1, xT, col["norm_mix"], hT))
        merged = core.take(DC, T)
        mark2 = core.top
        proj_qkv, attention, attn = stage_attention()
        run(proj_qkv)
        run(attention)
        mark = core.top
        attnT = core.take(DC, T)
        core.take(KV_HEADS, T)
        core.take(NT, KV_HEADS * HD)
        core.take(NT, D)
        gate = core.take(DC, T)
        core.top = mark
        s_attn_turned = sem("attn_turned")
        run(turn(attn, attnT, DC, s_attn_turned, 0))
        w1 = IN["w_in"][0]
        run(project([
            Job("features", columns_of(w1, DC, 512, OFF_GATE), hT, DC, 512, 2, gate_store(gate)),
            Job("features", columns_of(IN["w_attn_branch"][0], DC, 512), attnT, DC, 512, 2,
                times_store(merged, gate), on="dve")]))
        core.top = mark2
        for st in stages_ssd():
            run(st)
        core.top = mark2 = core.top - DC * T
        for st in stages_cross():
            run(st)
        for st in stages_ffn():
            run(st)
        run(feature_norm(core, 0, xT, col["norm1_g_2"], hT))
        merged2 = core.take(DC, T)
        for st in stages_delta(merged2):
            run(st)
        for st in stages_sparse(merged2):
            run(st)
        core.top = mark2
        for st in stages_moe():
            run(st)
        core.top = mark2
        for st in stages_store():
            run(st)

        if debug:
            dbg = sem("debug_stored")
            def dump(sp):
                n = 0
                for name, buf in dict(merged=merged, hT=hT, xT=xT, merged2=merged2).items():
                    if name in debug:
                        sp.dma_start(debug[name].rearrange("(c p) t -> p c t", p=P), buf).then_inc(dbg, 16)
                        n += 1
                sp.wait_ge(dbg, 16 * n)

        def program(eng, name):
            for n, st in enumerate(stages):
                if name != "sp":
                    core.begin(eng, n)
                if name in st:
                    st[name](eng)
                if name != "sp":
                    core.finish(eng, name)

        with nc.Block() as block:
            @block.sync
            def _(sp):
                program(sp, "sp")
                core.begin(sp, len(stages))
                if debug:
                    dump(sp)

            @block.tensor
            def _(pe):
                program(pe, "pe")

            @block.vector
            def _(dve):
                program(dve, "dve")

            @block.scalar
            def _(act):
                program(act, "act")

            @block.gpsimd
            def _(gp):
                program(gp, "pool")


_DEBUG = {}


def kernel(**inputs):
    from concourse import bacc
    from concourse.bass_utils import run_bass_kernel_spmd

    nc = bacc.Bacc("TRN2", target_bir_lowering=False, num_devices=1)
    arrays, IN = {}, {}
    for name, value in inputs.items():
        a = np.ascontiguousarray(value)
        arrays[f"in_{name}"] = a
        IN[name] = nc.dram_tensor(f"in_{name}", a.shape, mybir.dt.from_np(a.dtype), kind="ExternalInput").ap()
    out = nc.dram_tensor("out", (1, T, D), F32, kind="ExternalOutput").ap()
    debug = {n: nc.dram_tensor(f"debug_{n}", shape, F32, kind="ExternalOutput").ap() for n, shape in _DEBUG.items()}
    mixer_kernel(nc, IN, out, debug)
    r = run_bass_kernel_spmd(nc, [arrays], core_ids=[0])
    got = r.results[0]["out"]
    if _DEBUG:
        return (got,) + tuple(r.results[0][f"debug_{n}"] for n in _DEBUG)
    return got
```

```python
from contextlib import ExitStack

import numpy as np
import concourse.bass as bass
from concourse import mybir

ALU = mybir.AluOpType
ACT = mybir.ActivationFunctionType
F32 = mybir.dt.float32
I32 = mybir.dt.int32
F32R = mybir.dt.float32r
AX = mybir.AxisListType

P = 128
T = 512
NT = T // P
D = 1024
DC = D // P
BANK = 512
EPS = 1e-6
NEG = -1e30

MEM = 256
HEADS, KV_HEADS, HD = 16, 4, 64
D_INNER, SSD_HEADS, GROUPS, D_STATE, TAPS = 2048, 32, 8, 128, 5
GH = SSD_HEADS // GROUPS
GW = D_INNER // GROUPS
X_HEADS, XD = 4, 128
D_FF = 4096
OFF_K = HEADS * HD
OFF_V = OFF_K + KV_HEADS * HD
OFF_Z = OFF_V + KV_HEADS * HD
OFF_XBC = OFF_Z + D_INNER
OFF_DT = OFF_XBC + D_INNER + 2 * GROUPS * D_STATE
OFF_GATE = OFF_DT + 2 * SSD_HEADS

AH, AD, TAPS_2 = 8, 64, 4
BH, BKV = 8, 2
IH = 8
TOPK = min(256, T // 4)
CAUSAL = 64
EXPERTS, EG, DE = 16, 4, 256
OFF2 = {}
_at = 0
for _name, _n in (("a_q", 512), ("a_k", 512), ("a_v", 512), ("a_z", 512), ("a_beta", 8), ("a_alpha", 8),
                  ("b_q", 512), ("b_k", 128), ("b_v", 128), ("i_q", 512), ("i_k", 64), ("i_w", 8),
                  ("gate_a", 1024), ("gate_b", 1024)):
    OFF2[_name] = _at
    _at += _n
ROPE_INV = (10000.0 ** (-np.arange(32) / 32)).astype(np.float32)


class Pair:

    def __init__(self, tensor):
        self.hi, self.lo = tensor[:, 0], tensor[:, 1]

    def shaped(self, chunks, n):
        part = Pair.__new__(Pair)
        part.hi, part.lo = (t.rearrange("p a b -> p (a b)")[:, 0:chunks * n].rearrange("p (a b) -> p a b", a=chunks)
                            for t in (self.hi, self.lo))
        return part


class Core:

    def __init__(self, nc, ctx):
        self.nc, self.ctx = nc, ctx
        self.ps = ctx.enter_context(nc.psum_tensor("ps", [P, 8, BANK], F32))
        self.ring = ctx.enter_context(nc.sbuf_tensor("ring", [P, 2, 4096], F32))
        self.arena_size = 44800
        self.arena = ctx.enter_context(nc.sbuf_tensor("arena", [P, self.arena_size], F32))
        self.arena_at = nc.sbuf_base - 4 * self.arena_size
        self.top = 0
        self.pairs = 0
        self.landed = [self.semaphore(f"raw_weights_landed_{s}") for s in range(Project.RAW)]
        self.raw_count = [0] * Project.RAW
        self.hi_made = self.semaphore("weights_hi_made")
        self.split = self.semaphore("weights_split")
        self.pair_hi = self.semaphore("activation_hi_made")
        self.pair_made = self.semaphore("activation_split")
        self.unit_ready = self.semaphore("product_ready")
        self.unit_stored = {e: self.semaphore(f"product_stored_{e}") for e in ("act", "dve")}
        self.followed = self.semaphore("product_followed")
        self.slots = self.units = self.chunks = self.follows = 0
        self.stored = {"act": 0, "dve": 0}
        self.fence = {e: self.semaphore(f"stage_done_{e}") for e in ("pe", "act", "dve", "pool")}

    def semaphore(self, name):
        return self.ctx.enter_context(self.nc.semaphore(name))

    def take_pair(self, chunks, n):
        size = 2 * chunks * n
        self.top = -(-self.top // 8) * 8
        assert self.top + size <= self.arena_size, (self.top, size)
        t = self.nc.alloc_sbuf_tensor_at(f"pair_{self.pairs}", [P, 2, chunks, n], F32R,
                                         offset=self.arena_at + 4 * self.top)
        self.pairs += 1
        self.top += size
        return Pair(t)

    def take(self, *shape):
        n = int(np.prod(shape))
        assert self.top + n <= self.arena_size, (self.top, n)
        v = self.arena[:, self.top:self.top + n]
        self.top += n
        if len(shape) == 2:
            v = v.rearrange("p (a b) -> p a b", a=shape[0])
        elif len(shape) == 3:
            v = v.rearrange("p (a b c) -> p a b c", a=shape[0], b=shape[1])
        elif len(shape) == 4:
            v = v.rearrange("p (a b c d) -> p a b c d", a=shape[0], b=shape[1], c=shape[2])
        return v

    def finish(self, eng, name):
        eng.drain().then_inc(self.fence[name], 1)

    def begin(self, eng, stage):
        if stage:
            for other in self.fence.values():
                eng.wait_ge(other, stage)


def product(nc, out, lhs, rhs, start, stop):
    nc.tensor.matmul(out, lhs[1], rhs[0], start=start, stop=False)
    nc.tensor.matmul(out, lhs[0], rhs[1], start=False, stop=False)
    return nc.tensor.matmul(out, lhs[0], rhs[0], start=False, stop=stop)


class Job:

    def __init__(self, kind, weights, act, kc, cols, slots, store, on="act", nt=T, needs=False, source=None,
                 follow=None, with_last=False):
        self.kind, self.weights, self.act, self.kc, self.cols = kind, weights, act, kc, cols
        self.slots, self.store, self.on, self.nt, self.needs = slots, store, on, nt, needs
        self.source, self.follow, self.with_last = source, follow, with_last
        self.per_slot = -(-cols // P) if kind == "features" else nt // P
        assert kc * cols <= Project.SLOT
        assert not follow or on == "act"


class Project:

    BANKS = 4
    SLOT = 2048
    RAW = 4

    def __init__(self, core, weights, jobs, repeat=1, start=None):
        self.core, self.repeat, self.pair, self.start = core, repeat, weights, start
        self.plan, self.units = [], []
        count = {"act": 0, "dve": 0}
        chunks = follows = 0
        self.slot0, self.unit0, self.stored0 = core.slots, core.units, dict(core.stored)
        if start:
            core.chunks += start[2]
        self.chunk0, self.follow0, self.landed0 = core.chunks, core.follows, list(core.raw_count)
        for j in jobs:
            for i in range(j.slots):
                first = len(self.units)
                step = dict(j=j, i=i, first=first, needs=dict(count) if j.needs and i == 0 else None,
                            follows=follows, chunks=chunks, source=j.source is not None and i == 0)
                if step["source"]:
                    chunks += j.kc
                step["chunks_after"] = chunks
                for u in range(j.per_slot):
                    count[j.on] += 1
                    follows += j.follow is not None
                    self.units.append((j.on, count[j.on], follows if j.follow else 0))
                self.plan.append(step)
        self.count, self.chunks, self.follows = count, chunks, follows
        self.n = len(self.plan)
        self.extra = 2 if repeat > 1 else 0
        for k in range(repeat * self.n + self.extra):
            core.raw_count[k % self.RAW] += 16
        core.slots += repeat * self.n + self.extra
        core.units += repeat * len(self.units)
        core.chunks += repeat * chunks
        core.follows += repeat * follows
        for e in count:
            core.stored[e] += repeat * count[e]
        assert repeat == 1 or (self.n % self.RAW == 0 and len(self.units) % self.BANKS == 0)

    def rounds(self, eng, body):
        if self.repeat == 1:
            return body(0)
        with eng.Fori(0, self.repeat) as r:
            body(r)

    def raw(self, k):
        par = k % self.RAW
        half = self.core.ring[:, par // 2, :]
        return half[:, (par % 2) * self.SLOT:(par % 2 + 1) * self.SLOT]

    def sync(self, sp):
        core = self.core
        if self.slot0:
            sp.wait_ge(core.split, self.slot0)
        self.rounds(sp, lambda r: [self.load(sp, k, r) for k in range(self.n)])
        for k in range(self.extra):
            self.load(sp, k, self.repeat)

    def load(self, sp, k, r):
        j, i = self.plan[k]["j"], self.plan[k]["i"]
        if k >= self.RAW or self.repeat > 1:
            assert self.slot0 + k - (self.RAW - 1) > 0
            sp.wait_ge(self.core.split, self.slot0 + k - (self.RAW - 1) + r * self.n)
        view = self.raw(k)[:, 0:j.kc * j.cols].rearrange("p (k n) -> p k n", k=j.kc)
        w = j.weights(i, 0 if isinstance(r, int) else r)
        self.core.nc.sync.dma_start(view, w).then_inc(self.core.landed[k % self.RAW], 16)

    def width(self, k):
        j = self.plan[k % self.n]["j"]
        return j.kc * j.cols

    def split_hi(self, act, k, r):
        core, n = self.core, self.width(k)
        par = k % self.RAW
        act.wait_ge(core.landed[par], self.landed0[par] + 16 * (k // self.RAW + 1) + 16 // self.RAW * self.n * r)
        act.activation(self.pair.hi[:, k % 2, 0:n], self.raw(k)[:, 0:n], ACT.Copy).then_inc(core.hi_made, 1)

    def split_lo(self, dve, k, r):
        core, n = self.core, self.width(k)
        dve.wait_ge(core.hi_made, self.slot0 + k + 1 + r * self.n)
        dve.tensor_tensor(self.pair.lo[:, k % 2, 0:n], self.raw(k)[:, 0:n],
                          self.pair.hi[:, k % 2, 0:n].bitcast(F32), ALU.subtract).then_inc(core.split, 1)

    def wait_needs(self, eng, step, r):
        if step["needs"]:
            for e, c in step["needs"].items():
                if c:
                    eng.wait_ge(self.core.unit_stored[e], self.stored0[e] + c + r * self.count[e])
            if step["follows"]:
                eng.wait_ge(self.core.followed, self.follow0 + step["follows"] + r * self.follows)

    def start_hi(self, act):
        if self.start:
            pair, source, kc = self.start
            for c in range(kc):
                act.activation(pair.hi[:, c, :], source[:, c, :], ACT.Copy).then_inc(self.core.pair_hi, 1)

    def start_lo(self, dve):
        if self.start:
            pair, source, kc = self.start
            for c in range(kc):
                dve.wait_ge(self.core.pair_hi, self.chunk0 - kc + c + 1)
                dve.tensor_tensor(pair.lo[:, c, :], source[:, c, :], pair.hi[:, c, :].bitcast(F32),
                                  ALU.subtract).then_inc(self.core.pair_made, 1)

    def source_hi(self, act, k, r):
        if k < self.n and self.plan[k]["source"]:
            step = self.plan[k]
            j = step["j"]
            self.wait_needs(act, step, r)
            for c in range(j.kc):
                act.activation(j.act.hi[:, c, 0:j.nt], j.source[:, c, 0:j.nt], ACT.Copy).then_inc(self.core.pair_hi, 1)

    def source_lo(self, dve, k, r):
        if k < self.n and self.plan[k]["source"]:
            step = self.plan[k]
            j = step["j"]
            for c in range(j.kc):
                dve.wait_ge(self.core.pair_hi, self.chunk0 + step["chunks"] + c + 1 + r * self.chunks)
                dve.tensor_tensor(j.act.lo[:, c, 0:j.nt], j.source[:, c, 0:j.nt],
                                  j.act.hi[:, c, 0:j.nt].bitcast(F32), ALU.subtract).then_inc(self.core.pair_made, 1)

    def multiply(self, pe, k, r):
        core, nc = self.core, self.core.nc
        step = self.plan[k]
        j, first = step["j"], step["first"]
        pe.wait_ge(core.split, self.slot0 + k + 1 + r * self.n)
        self.wait_needs(pe, step, r)
        w = [t[:, k % 2, 0:j.kc * j.cols].rearrange("p (k n) -> p k n", k=j.kc) for t in (self.pair.hi, self.pair.lo)]
        a = (j.act.hi, j.act.lo)
        for u in range(j.per_slot):
            m = first + u
            bank = m % self.BANKS
            if m >= self.BANKS or self.repeat > 1:
                e, c, f = self.units[m - self.BANKS]
                if m < self.BANKS:
                    c, f = c - self.count[e], f and f - self.follows
                assert self.stored0[e] + c > 0
                pe.wait_ge(core.unit_stored[e], self.stored0[e] + c + r * self.count[e])
                if f > 0:
                    pe.wait_ge(core.followed, self.follow0 + f + r * self.follows)
                else:
                    assert not self.units[m - self.BANKS][2] or m < self.BANKS and self.repeat == 1
            for c in range(j.kc):
                if step["source"] and u == 0:
                    pe.wait_ge(core.pair_made, self.chunk0 + step["chunks"] + c + 1 + r * self.chunks)
                flags = dict(start=c == 0, stop=c == j.kc - 1)
                if j.kind == "features":
                    width = min(P, j.cols - u * P)
                    mm = product(nc, core.ps[0:width, bank, 0:j.nt], [x[:, c, u * P:u * P + width] for x in w],
                                 [x[:, c, 0:j.nt] for x in a], **flags)
                else:
                    mm = product(nc, core.ps[:, bank, 0:j.cols], [x[:, c, u * P:(u + 1) * P] for x in a],
                                 [x[:, c, :] for x in w], **flags)
            mm.then_inc(core.unit_ready, 1)

    def put(self, eng, name, k, r):
        core, step = self.core, self.plan[k]
        j, i, first = step["j"], step["i"], step["first"]
        for u in range(j.per_slot):
            m = first + u
            if j.on == name:
                eng.wait_ge(core.unit_ready, self.unit0 + m + 1 + r * len(self.units))
                if j.with_last:
                    e, c, _ = self.units[m - j.per_slot]
                    eng.wait_ge(core.unit_stored[e], self.stored0[e] + c + r * self.count[e])
                j.store(eng, i, u, core.ps[:, m % self.BANKS, :], r).then_inc(core.unit_stored[name], 1)
            elif j.follow:
                eng.wait_ge(core.unit_stored["act"], self.stored0["act"] + self.units[m][1] + r * self.count["act"])
                j.follow(eng, i, u, r).then_inc(core.followed, 1)
        if k + 2 < self.n or self.repeat > 1:
            if name == "act":
                eng.wait_ge(core.unit_ready, self.unit0 + first + j.per_slot + r * len(self.units))
                self.split_hi(eng, k + 2, r)
            else:
                self.split_lo(eng, k + 2, r)
        if k + 1 < self.n and self.plan[k + 1]["source"]:
            if name == "act":
                eng.wait_ge(core.unit_ready, self.unit0 + first + j.per_slot + r * len(self.units))
                self.source_hi(eng, k + 1, r)
            else:
                self.source_lo(eng, k + 1, r)

    def scalar(self, act):
        self.split_hi(act, 0, 0)
        assert not (self.plan[0]["source"] and self.repeat > 1)
        self.start_hi(act)
        self.source_hi(act, 0, 0)
        if self.n > 1:
            self.split_hi(act, 1, 0)
        self.rounds(act, lambda r: [self.put(act, "act", k, r) for k in range(self.n)])

    def vector(self, dve):
        self.split_lo(dve, 0, 0)
        self.start_lo(dve)
        self.source_lo(dve, 0, 0)
        if self.n > 1:
            self.split_lo(dve, 1, 0)
        self.rounds(dve, lambda r: [self.put(dve, "dve", k, r) for k in range(self.n)])

    def tensor(self, pe):
        if self.start:
            pe.wait_ge(self.core.pair_made, self.chunk0)
        self.rounds(pe, lambda r: [self.multiply(pe, k, r) for k in range(self.n)])

    def programs(self):
        return dict(sp=self.sync, pe=self.tensor, act=self.scalar, dve=self.vector)


def columns_of(w, kc, width, base=0, row0=0):
    view = w.rearrange("(k p) n -> p k n", p=P)
    return lambda i, r: view[:, row0:row0 + kc, base + i * width:base + (i + 1) * width]


def feature_norm(core, stage, src, gain, dst, nt=T):
    nc, ps = core.nc, core.ps
    mark = core.top
    sq = core.take(DC, nt)
    v, r, a = core.take(nt), core.take(nt), core.take(nt)
    core.top = mark
    squares, summed, var_ready, root_ready = core.norm_sems
    k = core.norms
    core.norms += 1

    def scalar(act):
        for c in range(DC):
            act.activation(sq[:, c, :], src[:, c, :], ACT.Square).then_inc(squares, 1)
        act.wait_ge(var_ready, k + 1)
        act.activation(r, v, ACT.Sqrt).then_inc(root_ready, 1)

    def tensor(pe):
        for c in range(DC):
            pe.wait_ge(squares, DC * k + c + 1)
            mm = nc.tensor.matmul(ps[:, 4, 0:nt], core.ones, sq[:, c, :], start=c == 0, stop=c == DC - 1)
        mm.then_inc(summed, 1)

    def vector(dve):
        dve.wait_ge(summed, k + 1)
        dve.tensor_scalar(v, ps[:, 4, 0:nt], 1.0 / D, EPS, ALU.mult, ALU.add).then_inc(var_ready, 1)
        dve.wait_ge(root_ready, k + 1)
        newton_rsqrt(core, dve, v, r, a)
        for c in range(DC):
            dve.scalar_tensor_tensor(out=dst[:, c, :], in0=src[:, c, :], scalar=gain[:, c:c + 1], in1=r,
                                     op0=ALU.mult, op1=ALU.mult)

    return dict(act=scalar, pe=tensor, dve=vector)


def newton_rsqrt(core, dve, v, r, a):
    dve.reciprocal(r, r)
    dve.drain()
    dve.tensor_tensor(a, r, r, ALU.mult)
    dve.drain()
    dve.tensor_tensor(a, a, v, ALU.mult)
    dve.drain()
    dve.tensor_scalar(a, a, -0.5, 1.5, ALU.mult, ALU.add)
    dve.drain()
    dve.tensor_tensor(r, r, a, ALU.mult)
    dve.drain()


def mixer_kernel(nc, IN, out, debug):
    with ExitStack() as ctx:
        core = Core(nc, ctx)
        ps = core.ps
        sem = core.semaphore
        core.norm_sems = [core.semaphore(n) for n in ("squares_ready", "squares_summed", "variance_ready", "root_ready")]
        core.norms = 0

        core.ident = core.take(P)
        core.ones = core.take(P)
        LE, GT, LT, GE = (core.take(P) for _ in range(4))
        PROWS = 3
        rows = core.take(PROWS, P)
        cols = core.take(PROWS * P)
        col = {}
        pieces, at = [], 0
        for name, n in (("norm_mix", 8), ("norm_cross", 8), ("norm_mem", 8), ("norm_ffn", 8), ("norm_final", 8),
                        ("ssd_norm", 16), ("conv_b", 32), ("conv_w", 160), ("norm1_g_2", 8), ("norm2_g_2", 8),
                        ("b_gate_2", 16), ("conv_w_2", 48), ("final_norm_g_2", 8)):
            flat = IN[name]
            flat = {1: lambda a: a.rearrange("(r c) -> r c", c=P),
                    2: lambda a: a.rearrange("a (r c) -> (a r) c", c=P),
                    3: lambda a: a.rearrange("a t (r c) -> (a t r) c", c=P)}[len(flat.shape)](flat)
            col[name] = cols[:, at:at + n]
            done = 0
            while done < n:
                m = min(n - done, P - at % P)
                pieces.append((rows[at % P:at % P + m, at // P, :], flat[done:done + m, :]))
                done, at = done + m, at + m
        assert at <= PROWS * P
        xT = core.take(DC, T)
        hT = core.take(DC, T)
        floor = core.top

        s_small = sem("parameters_landed")
        s_x = sem("x_landed")
        s_made = sem("constants_made")
        s_prow = sem("parameter_rows_zeroed")
        s_turned = sem("chunks_turned")
        s_out = sem("output_stored")
        s_copied = sem("chunks_copied")

        def stage_load():
            mark = core.top
            xt = core.take(NT, D)
            core.top = mark

            def sync(sp):
                for t in range(NT):
                    sp.dma_start(xt[:, t, :], IN["x"][0, t * P:(t + 1) * P, :]).then_inc(s_x, 16)
                sp.wait_ge(s_prow, 1)
                for dst, src in pieces:
                    sp.dma_start(dst, src).then_inc(s_small, 16)

            def pool(gp):
                gp.memset(core.ident, 0.0)
                gp.memset(core.ones, 1.0)
                for m in (LE, GT, LT, GE):
                    gp.memset(m, 1.0)
                gp.drain()
                gp.affine_select(out=core.ident, in_=core.ident, compare_op=ALU.not_equal, fill=1.0, base=0,
                                 pattern=[[-1, P]], channel_multiplier=1)
                for m, cmp, mult in ((LE, ALU.is_ge, -1), (GT, ALU.is_gt, 1), (LT, ALU.is_gt, -1), (GE, ALU.is_ge, 1)):
                    gp.affine_select(out=m, in_=m, compare_op=cmp, fill=0.0, base=0,
                                     pattern=[[-mult, P]], channel_multiplier=mult)

            def vector(dve):
                dve.memset(rows, 0.0).then_inc(s_prow, 1)
                for c in range(DC // 2):
                    dve.wait_ge(s_turned, c + 1)
                    dve.tensor_copy(xT[:, c, :], ps[:, c, :]).then_inc(s_copied, 1)
                dve.wait_ge(s_turned, DC + 1)
                dve.tensor_copy(cols, ps[:, 0, 0:PROWS * P]).then_inc(s_made, 1)

            def scalar(act):
                for c in range(DC // 2, DC):
                    act.wait_ge(s_turned, c + 1)
                    act.activation(xT[:, c, :], ps[:, c, :], ACT.Copy)

            def tensor(pe):
                pe.wait_ge(core.fence["pool"], 1)
                pe.wait_ge(s_x, 16 * NT)
                for c in range(DC):
                    for t in range(NT):
                        mm = nc.tensor.transpose(ps[:, c, t * P:(t + 1) * P], xt[:, t, c * P:(c + 1) * P], core.ident)
                    mm.then_inc(s_turned, 1)
                pe.wait_ge(s_small, 16 * len(pieces))
                pe.wait_ge(s_copied, 1)
                for t in range(PROWS):
                    mm = nc.tensor.transpose(ps[:, 0, t * P:(t + 1) * P], rows[:, t, :], core.ident)
                mm.then_inc(s_turned, 1)
            return dict(sp=sync, pool=pool, dve=vector, act=scalar, pe=tensor)


        s_turned_to = sem("activations_turned")
        turns = [0]

        def turn(src, dst, chunks, nt=T):
            base = turns[0]
            turns[0] += chunks

            def tensor(pe):
                for c in range(chunks):
                    for t in range(nt // P):
                        mm = nc.tensor.transpose(ps[:, c, t * P:(t + 1) * P], src[:, t, c * P:(c + 1) * P], core.ident)
                    mm.then_inc(s_turned_to, 1)

            def vector(dve):
                for c in range(chunks):
                    dve.wait_ge(s_turned_to, base + c + 1)
                    dve.tensor_copy(dst[:, c, :], ps[:, c, 0:nt])
            return dict(pe=tensor, dve=vector)

        def project(jobs):
            mark = core.top
            n = max(j.source.shape[1] * j.source.shape[2] for j in jobs)
            act, weights = core.take_pair(1, n), core.take_pair(2, Project.SLOT)
            core.top = mark
            last = None
            for j in jobs:
                same = j.source is last
                last = j.source
                j.act = act.shaped(j.kc, j.nt)
                if same:
                    j.source = None
            return Project(core, weights, jobs).programs()

        def copy_store(dst, scale=1.0, per_slot=2):
            return lambda eng, i, u, acc, r: eng.activation(dst[:, i * per_slot + u, :], acc, ACT.Copy, scale=scale)

        def add_store(dst, per_slot=2):
            return lambda eng, i, u, acc, r: eng.tensor_tensor(dst[:, i * per_slot + u, :], acc,
                                                               dst[:, i * per_slot + u, :], ALU.add)

        def gate_store(dst, bias=None):
            def store(eng, i, u, acc, r):
                m = i * 2 + u
                return eng.activation(dst[:, m, :], acc, ACT.Sigmoid, bias=0.0 if bias is None else bias[:, m:m + 1])
            return store

        def times_store(dst, gate, per_slot=2):
            def store(eng, i, u, acc, r):
                m = i * per_slot + u
                return eng.tensor_tensor(dst[:, m, :], acc, gate[:, m, :], ALU.mult)
            return store

        def add_times_store(dst, gate, scratch, per_slot=2):
            def store(eng, i, u, acc, r):
                m = i * per_slot + u
                eng.tensor_tensor(scratch[:, u % 2, :], acc, gate[:, m, :], ALU.mult)
                eng.drain()
                return eng.tensor_tensor(dst[:, m, :], dst[:, m, :], scratch[:, u % 2, :], ALU.add)
            return store

        def broadcast(src, n):
            return bass.AP(src.tensor, src.offset, [[0, P], [1, n]])

        mix_sems = [sem(f"attention_{n}") for n in ("scores_ready", "scores_read", "shift_ready", "probs_ready",
                                                    "probs_turned", "turned_copied", "mix_ready", "mix_stored")]

        def stage_attention():
            mark = core.top
            qT = core.take(DC, T)
            kd = core.take(KV_HEADS, T)
            v = core.take(NT, KV_HEADS * HD)
            W = 3 * P
            dist = core.take(W)
            dist2 = core.take(W)
            sink = core.take(HEADS)
            above = core.top
            attn = core.take(NT, D)
            s, pr, pt = core.take(2, W), core.take(2, W), core.take(2, W)
            U = HEADS * NT
            top, shift, total, esink, den = (core.take(U) for _ in range(5))
            core.top = above
            w = IN["w_in"][0]

            def k_store(eng, i, u, acc, r):
                for half in range(2):
                    for copy in range(2):
                        ins = eng.activation(kd[64 * copy:64 * copy + 64, 2 * u + half, :],
                                             acc[64 * half:64 * half + 64, :], ACT.Copy)
                return ins

            jobs = [Job("features", columns_of(w, DC, 256), None, DC, 256, 4, copy_store(qT, HD ** -0.5),
                             source=hT),
                    Job("features", columns_of(w, DC, 256, OFF_K), None, DC, 256, 1, k_store, source=hT),
                    Job("tokens", columns_of(w, DC, 256, OFF_V), None, DC, 256, 1,
                             lambda eng, i, u, acc, r: eng.activation(v[:, u, :], acc[:, 0:256], ACT.Copy),
                             source=hT)]
            first = project(jobs)
            core.top = mark
            s_sink, s_dist, sum_ready = sem("sink_landed"), sem("distances_made"), sem("sums_ready")
            (scores_ready, scores_read, shift_ready, probs_ready, probs_turned, turned_copied, out_ready,
             out_stored) = mix_sems
            first_sp = first["sp"]

            def sync(sp):
                sp.dma_start(sink, broadcast(IN["attn_sink"], HEADS)).then_inc(s_sink, 16)
                first_sp(sp)
            first["sp"] = sync

            def pool(gp):
                gp.iota(dist, pattern=[[-1, W]], base=P, channel_multiplier=1, allow_small_or_imprecise_dtypes=True)
                gp.drain()
                gp.tensor_scalar(dist2, dist, -1.0, None, ALU.mult)
                gp.drain()
                gp.affine_select(out=dist, in_=dist, compare_op=ALU.is_ge, fill=1e32, base=0,
                                 pattern=[[1, W]], channel_multiplier=-1)
                gp.affine_select(out=dist2, in_=dist2, compare_op=ALU.is_ge, fill=1e32, base=2 * P,
                                 pattern=[[-1, W]], channel_multiplier=1)
                gp.drain().then_inc(s_dist, 1)
            first["pool"] = pool

            units = [(h, b, max(0, b - 1), min(NT, b + 2)) for h in range(HEADS) for b in range(NT)]

            def tensor(pe):
                for u in range(U + 2):
                    if u < U:
                        h, b, k0, k1 = units[u]
                        r = 64 * (h % 2)
                        if u >= 2:
                            pe.wait_ge(scores_read, u - 1)
                        nc.tensor.matmul(ps[:, u % 2, 0:(k1 - k0) * P], qT[r:r + 64, h // 2, b * P:(b + 1) * P],
                                         kd[r:r + 64, h // 4, k0 * P:k1 * P], start=True, stop=True)\
                            .then_inc(scores_ready, 1)
                    if 1 <= u <= U:
                        n = u - 1
                        h, b, k0, k1 = units[n]
                        pe.wait_ge(probs_ready, n + 1)
                        if n >= 2:
                            pe.wait_ge(turned_copied, n - 1)
                        for k in range(k1 - k0):
                            mm = nc.tensor.transpose(ps[:, 2 + n % 2, k * P:(k + 1) * P],
                                                     pr[:, n % 2, k * P:(k + 1) * P], core.ident)
                        mm.then_inc(probs_turned, 1)
                    if u >= 2:
                        n = u - 2
                        h, b, k0, k1 = units[n]
                        pe.wait_ge(turned_copied, n + 1)
                        if n >= 2:
                            pe.wait_ge(out_stored, n - 1)
                        for k in range(k1 - k0):
                            mm = nc.tensor.matmul(ps[:, 4 + n % 2, 0:HD], pt[:, n % 2, k * P:(k + 1) * P],
                                                  v[:, k0 + k, (h // 4) * HD:(h // 4 + 1) * HD],
                                                  start=k == 0, stop=k == k1 - k0 - 1)
                        mm.then_inc(out_ready, 1)

            def vector(dve):
                dve.wait_ge(s_dist, 1)
                dve.tensor_tensor(dist, dist, dist2, ALU.max)
                dve.drain()
                dve.wait_ge(s_sink, 16)
                for u in range(U + 2):
                    if u < U:
                        h, b, k0, k1 = units[u]
                        n = (k1 - k0) * P
                        w0 = (k0 - b + 1) * P
                        dve.wait_ge(scores_ready, u + 1)
                        if u >= 2:
                            dve.wait_ge(probs_ready, u - 1)
                        dve.scalar_tensor_tensor(out=s[:, u % 2, 0:n], in0=dist[:, w0:w0 + n],
                                                 scalar=-(2.0 ** (-8.0 * (h + 1) / HEADS)),
                                                 in1=ps[:, u % 2, 0:n], op0=ALU.mult, op1=ALU.add)\
                            .then_inc(scores_read, 1)
                        dve.drain()
                        dve.tensor_reduce(top[:, u:u + 1], s[:, u % 2, 0:n], AX.X, ALU.max)
                        dve.drain()
                        dve.tensor_scalar(shift[:, u:u + 1], top[:, u:u + 1], sink[:, h:h + 1], -1.0,
                                          ALU.max, ALU.mult).then_inc(shift_ready, 1)
                    if u >= 2:
                        n = u - 2
                        h, b = units[n][:2]
                        dve.wait_ge(sum_ready, n + 1)
                        dve.tensor_tensor(den[:, n:n + 1], total[:, n:n + 1], esink[:, n:n + 1], ALU.add)
                        dve.drain()
                        dve.reciprocal(den[:, n:n + 1], den[:, n:n + 1])
                        dve.drain()
                        dve.wait_ge(out_ready, n + 1)
                        dve.tensor_scalar(attn[:, b, h * HD:(h + 1) * HD], ps[:, 4 + n % 2, 0:HD],
                                          den[:, n:n + 1], None, ALU.mult).then_inc(out_stored, 1)

            def scalar(act):
                act.wait_ge(s_sink, 16)
                for u in range(U + 1):
                    if u < U:
                        h, b, k0, k1 = units[u]
                        n = (k1 - k0) * P
                        act.wait_ge(shift_ready, u + 1)
                        if u >= 2:
                            act.wait_ge(probs_turned, u - 1)
                        act.activation(pr[:, u % 2, 0:n], s[:, u % 2, 0:n], ACT.Exp, bias=shift[:, u:u + 1],
                                       accum_out=total[:, u:u + 1]).then_inc(probs_ready, 1)
                        act.activation(esink[:, u:u + 1], sink[:, h:h + 1], ACT.Exp, bias=shift[:, u:u + 1])\
                            .then_inc(sum_ready, 1)
                    if u >= 1:
                        n = u - 1
                        h, b, k0, k1 = units[n]
                        act.wait_ge(probs_turned, n + 1)
                        if n >= 2:
                            act.wait_ge(out_ready, n - 1)
                        act.activation(pt[:, n % 2, 0:(k1 - k0) * P], ps[:, 2 + n % 2, 0:(k1 - k0) * P], ACT.Copy)\
                            .then_inc(turned_copied, 1)
            return first, dict(pe=tensor, dve=vector, act=scalar), attn

        def softplus(x, u, a, b, ready, base, act_too):
            r0, r1 = ready

            def vector(dve):
                dve.tensor_scalar(a, x, -1.0, None, ALU.mult)
                dve.drain()
                dve.tensor_tensor(u, a, x, ALU.min).then_inc(r0, 1)
                dve.wait_ge(r1, base + 1)
                dve.tensor_scalar(a, u, 2.0, None, ALU.add)
                dve.drain()
                dve.reciprocal(a, a)
                dve.drain()
                dve.tensor_tensor(u, u, a, ALU.mult)
                dve.drain()
                dve.tensor_tensor(a, u, u, ALU.mult)
                dve.drain()
                dve.tensor_scalar(b, a, 2.0 / 17, 2.0 / 15, ALU.mult, ALU.add)
                for k in (13, 11, 9, 7, 5, 3, 1):
                    dve.drain()
                    dve.tensor_tensor(b, b, a, ALU.mult)
                    dve.drain()
                    dve.tensor_scalar(b, b, 2.0 / k, None, ALU.add)
                dve.drain()
                dve.tensor_tensor(b, b, u, ALU.mult)
                dve.drain()
                dve.scalar_tensor_tensor(out=x, in0=x, scalar=0.0, in1=b, op0=ALU.max, op1=ALU.add)
                dve.drain()

            def scalar(act):
                act.wait_ge(r0, base + 1)
                act.activation(u, u, ACT.Exp).then_inc(r1, 1)
            return vector, scalar

        ssdT = None

        def stages_ssd():
            mark = core.top
            w = IN["w_in"][0]
            ssdT = core.take(2 * GROUPS, T)
            inner = core.top
            H = SSD_HEADS
            dt = core.take(2, NT, H)
            a = core.take(2, NT, H)
            into = core.take(2, NT, H)
            wst = core.take(2, NT, H)
            whole = core.take(2, NT, H)
            bias, alog = core.take(2, H), core.take(2, H)
            dskip = core.take(H)
            after_dt = core.top
            raw, u_, a_, b_ = (core.take(NT * 2 * H) for _ in range(4))
            core.top = after_dt
            raw4 = raw.rearrange("p (c d h) -> p c d h", c=NT, d=2)
            s_par, sp0, sp1, s_a, s_exp, s_a_ready, s_sums = (
                sem(n) for n in ("ssd_parameters_landed", "softplus_arg", "softplus_exp", "a_log_exp", "decay_exp",
                                 "log_decays_ready", "decay_sums_ready"))

            def raw_store(eng, i, u, acc, r):
                return eng.activation(raw[:, u * 2 * H:(u + 1) * 2 * H], acc[:, 0:2 * H], ACT.Copy)
            core.top = after_dt + 4 * NT * 2 * H
            proj_dt = project([Job("tokens", columns_of(w, DC, 2 * H, OFF_DT), None, DC, 2 * H, 1,
                                              raw_store, source=hT)])
            core.top = after_dt
            dt_sp = proj_dt["sp"]
            before = len(stages)

            def sync(sp):
                core.begin(sp, before)
                sp.dma_start(bias.rearrange("p d h -> p (d h)"), broadcast(IN["dt_bias"], 2 * H)).then_inc(s_par, 16)
                sp.dma_start(alog.rearrange("p d h -> p (d h)"), broadcast(IN["a_log"], 2 * H)).then_inc(s_par, 16)
                sp.dma_start(dskip, broadcast(IN["d_skip"], H)).then_inc(s_par, 16)
                dt_sp(sp)
            proj_dt["sp"] = sync
            soft_v, soft_a = softplus(raw, u_, a_, b_, (sp0, sp1), 0, None)

            def decay_vector(dve):
                dve.wait_ge(s_par, 48)
                for c in range(NT):
                    dve.tensor_tensor(raw4[:, c], raw4[:, c], bias, ALU.add)
                dve.drain()
                soft_v(dve)
                for d in range(2):
                    dve.tensor_copy(dt[:, d], raw4[:, :, d, :])
                dve.drain()
                dve.wait_ge(s_a, 1)
                for d in range(2):
                    for c in range(NT):
                        ins = dve.scalar_tensor_tensor(out=a[:, d, c, :], in0=dt[:, d, c, :], scalar=-1.0,
                                                       in1=alog[:, d, :], op0=ALU.mult, op1=ALU.mult)
                ins.then_inc(s_a_ready, 1)
                dve.wait_ge(s_exp, 1)
                dve.tensor_tensor(wst, wst, dt, ALU.mult)

            def decay_scalar(act):
                act.wait_ge(s_par, 48)
                act.activation(alog, alog, ACT.Exp).then_inc(s_a, 1)
                soft_a(act)
                act.wait_ge(s_sums, 1)
                flat = lambda t: t.rearrange("p d c h -> p (d c h)")
                act.activation(flat(into), ps[:, 0, 0:2 * NT * H], ACT.Exp)
                act.activation(flat(whole), ps[:, 1, 0:2 * NT * H], ACT.Exp)
                act.activation(flat(wst), ps[:, 2, 0:2 * NT * H], ACT.Exp).then_inc(s_exp, 1)

            def decay_tensor(pe):
                pe.wait_ge(s_a_ready, 1)
                n = NT * H
                for bank, masks in ((0, (LE, GE)), (1, (core.ones, core.ones)), (2, (GT, LT))):
                    for d in range(2):
                        mm = nc.tensor.matmul(ps[:, bank, d * n:(d + 1) * n], masks[d],
                                              a[:, d].rearrange("p c h -> p (c h)"), start=True, stop=True)
                mm.then_inc(s_sums, 1)

            PAD = TAPS // 2
            up = core.take(4, T + 2 * PAD)
            cv = core.take(4, T)
            fT = core.take(4, T)
            xt = core.take(NT, GW)
            Bt = core.take(NT, D_STATE)
            xw = core.take(4, NT, GW)
            xd = core.take(NT, GW)
            prev = core.take(2, NT, GW)
            cb = core.take(2, NT, P)
            am = core.take(4, GH, P)
            ex = core.take(2, GH * P)
            M = xw[:, 2:4].rearrange("p a c n -> p (a c n)").rearrange("p (a n) -> p a n", a=4)
            off = core.take(2, GW)
            junk = core.take(NT, GW)
            ss, vv, rr, aa = (core.take(NT) for _ in range(4))
            core.top = mark
            zt, y = (core.ring[:, 1, DC * GW + i * NT * GW:DC * GW + (i + 1) * NT * GW]
                     .rearrange("p (c n) -> p c n", c=NT) for i in range(2))
            (w_landed0, w_landed1, u_ready, u_copied, z_ready, z_stored, conv_ready, feat_ready, turned,
             tok_ready, xw_ready, st_ready, prev_ready, cb_ready, cb_read, am_ready, diff_ready, ex_ready, m_ready,
             y_ready, y_read, y_done, ss_ready, v_ready, root_ready, y_final, y_turned, y_stored, diag_done, pads_zeroed) = (
                sem(f"ssd_{n}") for n in (
                    "xbc_weights_landed", "z_weights_landed", "xbc_ready", "xbc_copied", "z_ready",
                    "z_stored", "conv_ready", "features_ready", "turned", "tokens_ready", "weighted_ready",
                    "chunk_states_ready", "states_ready", "cb_ready", "cb_read", "steps_ready", "sums_ready",
                    "decays_ready", "mixers_ready", "y_ready", "y_read", "y_gated", "squares_ready", "variance_ready",
                    "root_ready", "y_normed", "y_turned", "y_stored", "diagonal_made", "pads_zeroed"))
            split_before = core.slots
            wv = w.rearrange("(k p) n -> p k n", p=P)
            slot0 = core.ring[:, 0, :].rearrange("p (k n) -> p k n", k=DC)
            slot1 = core.ring[:, 1, 0:DC * GW].rearrange("p (k n) -> p k n", k=DC)
            OFF_B = OFF_XBC + D_INNER
            OFF_C = OFF_B + GROUPS * D_STATE
            cw = col["conv_w"].rearrange("p (t c) -> p t c", t=TAPS)
            ORDER = (2, 3, 0, 1)
            BANKS_X = (3, 0, 1, 2)
            SUMS = (4, 6)

            def chunk_of(g, j):
                return (2 * g, 2 * g + 1, g + 2 * GROUPS, g + 3 * GROUPS)[j]

            def after(eng, s, value):
                if not isinstance(value, int) or value > 0:
                    eng.wait_ge(s, value)

            def columns(at, n):
                return slice(at, at + n) if isinstance(at, int) else bass.ds(at, n)

            def chunk(t, m):
                return t[:, columns(m, 1)]

            def looped(eng, first, middle, last):
                first()
                with eng.Fori(0, GROUPS - 1) as g:
                    middle(g)
                last(GROUPS - 1)

            def ssd_sync(sp):
                def load(g):
                    after(sp, u_ready, g * 4)
                    for c, n, at in ((0, GW, OFF_XBC + g * GW), (GW, D_STATE, OFF_B + g * D_STATE),
                                     (GW + D_STATE, D_STATE, OFF_C + g * D_STATE)):
                        sp.dma_start(slot0[:, :, c:c + n], wv[:, :, columns(at, n)]).then_inc(w_landed0, 16)
                    after(sp, z_ready, g * 4)
                    sp.dma_start(slot1, wv[:, :, columns(OFF_Z + g * GW, GW)]).then_inc(w_landed1, 16)
                sp.wait_ge(core.split, split_before)
                looped(sp, lambda: load(0), lambda g: load(g + 1), lambda g: None)
                sp.wait_ge(z_ready, NT * GROUPS)
                sp.wait_ge(y_turned, 2 * GROUPS)

            def ssd_tensor(pe):
                def features(g, n):
                    j, bank = ORDER[n], BANKS_X[n]
                    if n == 0:
                        pe.wait_ge(w_landed0, g * 48 + 48)
                        after(pe, cb_read, g)
                    if n == 1:
                        after(pe, prev_ready, g)
                    for k in range(DC):
                        mm = nc.tensor.matmul(ps[:, bank, :], slot0[:, k, j * P:(j + 1) * P], hT[:, k, :],
                                              start=k == 0, stop=k == DC - 1)
                    mm.then_inc(u_ready, 1)

                def sums(g, n):
                    pe.wait_ge(am_ready, g * 8 + (n + 1))
                    if n == 0:
                        pe.wait_ge(z_stored, g * 4 + 4)
                    if n == 1:
                        after(pe, y_stored, g * 2)
                    after(pe, ex_ready, g * 8 + (n - 1))
                    for r in range(GH):
                        mm = nc.tensor.matmul(ps[:, SUMS[n % 2], r * P:(r + 1) * P], am[:, n % 4, r, :],
                                              (LE, GE)[n % 2], start=True, stop=True)
                    mm.then_inc(diff_ready, 1)

                def turn_y(g):
                    pe.wait_ge(y_final, g + 1)
                    for j in range(2):
                        for t in range(NT):
                            mm = nc.tensor.transpose(ps[:, 6 + j, t * P:(t + 1) * P], y[:, t, j * P:(j + 1) * P],
                                                     core.ident)
                        mm.then_inc(y_turned, 1)

                def front(g, turn_last):
                    pe.wait_ge(feat_ready, g * 4 + 2)
                    pe.wait_ge(u_copied, g * 4 + 4)
                    for c in range(NT):
                        t = slice(c * P, (c + 1) * P)
                        mm = nc.tensor.matmul(ps[:, 3, t], fT[:, 2, t], fT[:, 3, t], start=True, stop=True)
                    mm.then_inc(cb_ready, 1)
                    pe.wait_ge(feat_ready, g * 4 + 4)
                    for j in range(3):
                        for t in range(NT):
                            mm = nc.tensor.transpose(ps[:, j, t * P:(t + 1) * P], fT[:, j, t * P:(t + 1) * P],
                                                     core.ident)
                        mm.then_inc(turned, 1)
                    pe.wait_ge(w_landed1, g * 16 + 16)
                    after(pe, y_read, g * 4)
                    for t in range(NT):
                        for k in range(DC):
                            mm = nc.tensor.matmul(ps[:, 4 + t // 2, t % 2 * GW:(t % 2 + 1) * GW],
                                                  hT[:, k, t * P:(t + 1) * P], slot1[:, k, :],
                                                  start=k == 0, stop=k == DC - 1)
                        mm.then_inc(z_ready, 1)
                    turn_last()
                    pe.wait_ge(xw_ready, g * 4 + 2)
                    pe.wait_ge(tok_ready, g * 3 + 3)
                    n = 0
                    for d, chunks in ((0, (0, 1, 2)), (1, (3, 2, 1))):
                        for c in chunks:
                            mm = nc.tensor.matmul(ps[:, n // 2, (n % 2) * GW:(n % 2 + 1) * GW], Bt[:, c, :],
                                                  xw[:, 2 + d, c, :], start=True, stop=True)
                            n += 1
                    mm.then_inc(st_ready, 1)
                    sums(g, 0)
                    sums(g, 1)

                def back(g, between):
                    for c in range(NT):
                        between(c)
                        if c + 1 < NT:
                            sums(g, 2 * c + 2)
                            sums(g, 2 * c + 3)
                        t = slice(c * P, (c + 1) * P)
                        if c == 0:
                            pe.wait_ge(prev_ready, g + 1)
                            pe.wait_ge(xw_ready, g * 4 + 4)
                        else:
                            pe.wait_ge(y_read, g * 4 + c)
                        if c > 0:
                            nc.tensor.matmul(ps[:, 5, 0:GW], fT[:, 3, t], prev[:, 0, c, :], start=True, stop=True)
                        if c < NT - 1:
                            nc.tensor.matmul(ps[:, 5, GW:2 * GW], fT[:, 3, t], prev[:, 1, c, :], start=True, stop=True)
                        pe.wait_ge(m_ready, g * 8 + (2 * c + 2))
                        for r in range(GH):
                            for d in range(2):
                                mm = nc.tensor.matmul(ps[:, 7, r * 64:(r + 1) * 64],
                                                      M[:, (2 * c + d) % 4, r * P:(r + 1) * P],
                                                      xw[:, d, c, r * 64:(r + 1) * 64], start=d == 0, stop=d == 1)
                        mm.then_inc(y_ready, 1)

                def first():
                    for n in range(4):
                        features(0, n)
                    front(0, lambda: None)

                def middle(g):
                    back(g, lambda n: features(g + 1, n))
                    front(g + 1, lambda: turn_y(g))

                def last(g):
                    back(g, lambda n: None)
                    turn_y(g)
                looped(pe, first, middle, last)

            def ssd_scalar(act):
                def copy_up(g, n):
                    act.wait_ge(u_ready, g * 4 + (n + 1))
                    after(act, conv_ready, g * 4)
                    act.activation(up[:, ORDER[n], PAD:PAD + T], ps[:, BANKS_X[n], :], ACT.Copy).then_inc(u_copied, 1)

                def silus(g):
                    after(act, y_ready, g * 4)
                    for n, j in enumerate(ORDER):
                        act.wait_ge(conv_ready, g * 4 + (n + 1))
                        act.activation(fT[:, j, :], cv[:, j, :], ACT.Silu,
                                       bias=chunk(col["conv_b"], chunk_of(g, j))).then_inc(feat_ready, 1)

                def to_tokens(g):
                    for j in range(3):
                        act.wait_ge(turned, g * 3 + (j + 1))
                        src = ps[:, j, :].rearrange("p (t n) -> p t n", t=NT)
                        dst = xt[:, :, j * P:(j + 1) * P] if j < 2 else Bt
                        act.activation(dst, src, ACT.Copy).then_inc(tok_ready, 1)

                def silu_z(g):
                    for t in range(NT):
                        act.wait_ge(z_ready, g * 4 + (t // 2 * 2 + 2))
                        act.activation(zt[:, t, :], ps[:, 4 + t // 2, t % 2 * GW:(t % 2 + 1) * GW],
                                       ACT.Silu).then_inc(z_stored, 1)

                def decay(g, n):
                    act.wait_ge(diff_ready, g * 8 + (n + 1))
                    after(act, m_ready, g * 8 + (n - 1))
                    act.activation(ex[:, n % 2, :], ps[:, SUMS[n % 2], :], ACT.Exp).then_inc(ex_ready, 1)

                def square(g, c):
                    act.wait_ge(y_done, g * 4 + (c + 1))
                    act.activation(junk[:, c, :], y[:, c, :], ACT.Square, accum_out=ss[:, c:c + 1]).then_inc(ss_ready, 1)

                def back(g, between):
                    for c in range(NT):
                        between(c)
                        if c + 1 < NT:
                            decay(g, 2 * c + 2)
                            decay(g, 2 * c + 3)
                        if c:
                            square(g, c - 1)
                    square(g, NT - 1)

                def root(g):
                    act.wait_ge(v_ready, g + 1)
                    act.activation(rr, vv, ACT.Sqrt).then_inc(root_ready, 1)

                def store_y(g):
                    for j in range(2):
                        act.wait_ge(y_turned, g * 2 + (j + 1))
                        act.activation(chunk(ssdT, 2 * g + j).rearrange("p a t -> p (a t)"), ps[:, 6 + j, :], ACT.Copy,
                                       scale=chunk(col["ssd_norm"], 2 * g + j)).then_inc(y_stored, 1)

                def first():
                    act.wait_ge(pads_zeroed, 1)
                    for n in range(4):
                        copy_up(0, n)
                    silus(0)
                    to_tokens(0)
                    silu_z(0)
                    decay(0, 0)
                    decay(0, 1)

                def middle(g):
                    back(g, lambda n: copy_up(g + 1, n))
                    silus(g + 1)
                    root(g)
                    to_tokens(g + 1)
                    silu_z(g + 1)
                    store_y(g)
                    decay(g + 1, 0)
                    decay(g + 1, 1)

                def last(g):
                    back(g, lambda n: None)
                    root(g)
                    store_y(g)
                looped(act, first, middle, last)

            def per_head(t, g, d, c=None):
                if c is None:
                    return t[:, d, :, columns(g * GH, GH)].unsqueeze(3).to_broadcast([P, NT, GH, 64])
                return t[:, d, c, columns(g * GH, GH)].unsqueeze(2).to_broadcast([P, GH, 64])

            heads = lambda t: t.rearrange("p (r n) -> p r n", r=GH)

            def ssd_vector(dve):
                def conv(g, n):
                    j, m = ORDER[n], chunk_of(g, ORDER[n])
                    dve.wait_ge(u_copied, g * 4 + (n + 1))
                    after(dve, feat_ready, g * 4)
                    dve.tensor_scalar(cv[:, j, :], up[:, j, 0:T], chunk(cw[:, 0, :], m), None, ALU.mult)
                    for k in range(1, TAPS):
                        dve.drain()
                        ins = dve.scalar_tensor_tensor(out=cv[:, j, :], in0=up[:, j, k:k + T],
                                                       scalar=chunk(cw[:, k, :], m), in1=cv[:, j, :],
                                                       op0=ALU.mult, op1=ALU.add)
                    ins.then_inc(conv_ready, 1)

                def states(g):
                    dve.wait_ge(cb_ready, g + 1)
                    for d, mask in enumerate((LE, GE)):
                        ins = dve.tensor_tensor(cb[:, d], ps[:, 3, :].rearrange("p (c n) -> p c n", c=NT),
                                                mask.unsqueeze(1).to_broadcast([P, NT, P]), ALU.mult)
                    ins.then_inc(cb_read, 1)
                    dve.drain()
                    dve.wait_ge(st_ready, g + 1)
                    adds = {}
                    for n in range(6):
                        adds[n // 3, n % 3] = ps[:, n // 2, (n % 2) * GW:(n % 2 + 1) * GW]
                    for d in range(2):
                        dve.tensor_copy(prev[:, d, (1, 2)[d], :], adds[d, 0])
                    for i in (1, 2):
                        steps = [(d, (i, 3 - i)[d], (i + 1, 2 - i)[d]) for d in range(2)]
                        dve.drain()
                        for d, c, to in steps:
                            dve.tensor_tensor(heads(prev[:, d, to, :]), heads(prev[:, d, c, :]),
                                              per_head(whole, g, d, c), ALU.mult)
                        dve.drain()
                        for d, c, to in steps:
                            dve.tensor_tensor(prev[:, d, to, :], adds[d, i], prev[:, d, to, :], ALU.add)
                    dve.drain().then_inc(prev_ready, 1)

                def mixers(g, n):
                    c, d = n // 2, n % 2
                    dve.wait_ge(ex_ready, g * 8 + (n + 1))
                    if n >= 4:
                        dve.wait_ge(y_ready, g * 4 + (n // 2 - 1))
                    dve.tensor_tensor(heads(M[:, n % 4, :]), heads(ex[:, n % 2, :]),
                                      cb[:, d, c, :].unsqueeze(1).to_broadcast([P, GH, P]), ALU.mult)\
                        .then_inc(m_ready, 1)

                def back(g, between):
                    mixers(g, 0)
                    mixers(g, 1)
                    for c in range(NT):
                        if c + 1 < NT:
                            mixers(g, 2 * c + 2)
                            mixers(g, 2 * c + 3)
                        dve.wait_ge(y_ready, g * 4 + (c + 1))
                        dve.wait_ge(diag_done, g + 1)
                        if c > 0:
                            dve.tensor_tensor(heads(off[:, 0, :]), heads(ps[:, 5, 0:GW]), per_head(into, g, 0, c),
                                              ALU.mult)
                        if c < NT - 1:
                            dve.tensor_tensor(heads(off[:, 1, :]), heads(ps[:, 5, GW:2 * GW]),
                                              per_head(into, g, 1, c), ALU.mult)
                        dve.tensor_tensor(y[:, c, :], ps[:, 7, 0:GW], xd[:, c, :], ALU.add).then_inc(y_read, 1)
                        dve.drain()
                        if c > 0:
                            dve.tensor_tensor(y[:, c, :], y[:, c, :], off[:, 0, :], ALU.add)
                            dve.drain()
                        if c < NT - 1:
                            dve.tensor_tensor(y[:, c, :], y[:, c, :], off[:, 1, :], ALU.add)
                            dve.drain()
                        dve.tensor_tensor(y[:, c, :], y[:, c, :], zt[:, c, :], ALU.mult).then_inc(y_done, 1)
                        between(c)

                def norm(g):
                    dve.wait_ge(ss_ready, g * 4 + 4)
                    dve.tensor_scalar(vv, ss, 1.0 / GW, EPS, ALU.mult, ALU.add).then_inc(v_ready, 1)
                    dve.wait_ge(root_ready, g + 1)
                    newton_rsqrt(core, dve, vv, rr, aa)
                    for c in range(NT):
                        ins = dve.tensor_scalar(y[:, c, :], y[:, c, :], rr[:, c:c + 1], None, ALU.mult)
                    ins.then_inc(y_final, 1)

                def first():
                    dve.memset(up, 0.0).then_inc(pads_zeroed, 1)
                    for n in range(4):
                        conv(0, n)
                    states(0)

                def middle(g):
                    back(g, lambda n: conv(g + 1, n))
                    norm(g)
                    states(g + 1)

                def last(g):
                    back(g, lambda n: None)
                    norm(g)
                looped(dve, first, middle, last)

            def ssd_pool(gp):
                with gp.Fori(0, GROUPS) as g:
                    def steps(n):
                        c, d = n // 2, n % 2
                        if n >= 4:
                            gp.wait_ge(diff_ready, g * 8 + (n - 3))
                        gp.tensor_tensor(am[:, n % 4], (GT, LT)[d].unsqueeze(1).to_broadcast([P, GH, P]),
                                         a[:, d, c, bass.ds(g * GH, GH)].unsqueeze(2).to_broadcast([P, GH, P]),
                                         ALU.mult).then_inc(am_ready, 1)
                    gp.wait_ge(tok_ready, g * 3 + 2)
                    for n, t in ((2, wst), (3, wst)):
                        for c in range(NT):
                            ins = gp.tensor_tensor(heads(xw[:, n, c, :]), heads(xt[:, c, :]),
                                                   per_head(t, g, n % 2, c), ALU.mult)
                        ins.then_inc(xw_ready, 1)
                    for n in range(4):
                        steps(n)
                    for n, t in ((0, dt), (1, dt)):
                        for c in range(NT):
                            ins = gp.tensor_tensor(heads(xw[:, n, c, :]), heads(xt[:, c, :]),
                                                   per_head(t, g, n % 2, c), ALU.mult)
                        ins.then_inc(xw_ready, 1)
                    for c in range(NT):
                        ins = gp.tensor_tensor(heads(xd[:, c, :]), heads(xt[:, c, :]),
                                               dskip[:, bass.ds(g * GH, GH)].unsqueeze(2).to_broadcast([P, GH, 64]),
                                               ALU.mult)
                    ins.then_inc(diag_done, 1)
                    for n in range(4, 8):
                        steps(n)

            ssd = dict(sp=ssd_sync, pe=ssd_tensor, act=ssd_scalar, dve=ssd_vector, pool=ssd_pool)
            gate = core.arena[:, inner:inner + DC * T].rearrange("p (a b) -> p a b", a=DC)
            core.top = inner + DC * T
            scratch = core.take(2, T)
            w_branch = IN["w_ssd_branch"][0]
            join = project(
                [Job("features", columns_of(w, DC, 256, OFF_GATE + D), None, DC, 256, 4, gate_store(gate),
                          source=hT)] +
                [Job("features", columns_of(w_branch, DC, 256, row0=c), None, DC, 256, 4,
                          add_times_store(merged, gate, scratch), on="dve", source=ssdT[:, c:c + DC, :])
                 for c in (0, DC)] +
                [Job("features", columns_of(IN["w_out"][0], DC, 256), None, DC, 256, 4, add_store(xT),
                          on="dve", source=merged, needs=True)])
            core.top = mark
            return proj_dt, dict(pe=decay_tensor, act=decay_scalar, dve=decay_vector), ssd, join

        def stages_cross():
            mark = core.top
            MT = MEM // P
            memT = core.take(DC, MEM)
            kx = core.take(X_HEADS, MEM)
            vx = core.take(MT, X_HEADS * XD)
            qx = core.take(X_HEADS, T)
            ox = core.take(X_HEADS, T)
            s, pr, pt = core.take(2, MEM), core.take(2, MEM), core.take(2, MEM)
            U = X_HEADS * NT
            shift, total, den = (core.take(U) for _ in range(3))
            above = core.top
            mt = core.take(MT, D)
            s_mem, normed = sem("memory_landed"), sem("cross_probs_normed")
            (scores_ready, scores_read, shift_ready, probs_ready, probs_turned, turned_copied, out_ready,
             out_stored) = mix_sems
            U0 = HEADS * NT
            before = len(stages)
            load = turn(mt, memT, DC, nt=MEM)
            turn_pe = load["pe"]

            def sync(sp):
                core.begin(sp, before)
                for t in range(MT):
                    sp.dma_start(mt[:, t, :], IN["mem"][0, t * P:(t + 1) * P, :]).then_inc(s_mem, 16)
            load["sp"] = sync

            def wait_turn(pe):
                pe.wait_ge(s_mem, 16 * MT)
                turn_pe(pe)
            load["pe"] = wait_turn
            yield load
            yield feature_norm(core, 0, memT, col["norm_mem"], memT, nt=MEM)
            yield feature_norm(core, 0, xT, col["norm_cross"], hT)
            core.top = mark
            wkv = IN["w_xkv"][0]
            core.top = above
            yield project([
                Job("features", columns_of(IN["w_xq"][0], DC, 256), None, DC, 256, 2,
                         copy_store(qx, XD ** -0.5), source=hT),
                Job("features", columns_of(wkv, DC, 256), None, DC, 256, 2,
                         lambda eng, i, u, acc, r: eng.activation(kx[:, 2 * i + u, :], acc[:, 0:MEM], ACT.Copy),
                         nt=MEM, source=memT),
                Job("tokens", columns_of(wkv, DC, 256, 512), None, DC, 256, 2,
                         lambda eng, i, u, acc, r: eng.activation(vx[:, u, i * 256:(i + 1) * 256], acc[:, 0:256],
                                                                  ACT.Copy), nt=MEM, source=memT)])
            core.top = mark
            units = [(h, b) for h in range(X_HEADS) for b in range(NT)]

            def tensor(pe):
                for u in range(U + 2):
                    if u < U:
                        h, b = units[u]
                        if u >= 2:
                            pe.wait_ge(scores_read, U0 + u - 1)
                        nc.tensor.matmul(ps[:, u % 2, 0:MEM], qx[:, h, b * P:(b + 1) * P], kx[:, h, :],
                                         start=True, stop=True).then_inc(scores_ready, 1)
                    if 1 <= u <= U:
                        n = u - 1
                        pe.wait_ge(normed, n + 1)
                        if n >= 2:
                            pe.wait_ge(turned_copied, U0 + n - 1)
                        for k in range(MT):
                            mm = nc.tensor.transpose(ps[:, 2 + n % 2, k * P:(k + 1) * P],
                                                     pr[:, n % 2, k * P:(k + 1) * P], core.ident)
                        mm.then_inc(probs_turned, 1)
                    if u >= 2:
                        n = u - 2
                        h, b = units[n]
                        pe.wait_ge(turned_copied, U0 + n + 1)
                        if n >= 2:
                            pe.wait_ge(out_stored, U0 + n - 1)
                        for k in range(MT):
                            mm = nc.tensor.matmul(ps[:, 4 + n % 2, 0:P], vx[:, k, h * XD:(h + 1) * XD],
                                                  pt[:, n % 2, k * P:(k + 1) * P], start=k == 0, stop=k == MT - 1)
                        mm.then_inc(out_ready, 1)

            def vector(dve):
                for u in range(U + 2):
                    if u < U:
                        dve.wait_ge(scores_ready, U0 + u + 1)
                        dve.tensor_reduce(shift[:, u:u + 1], ps[:, u % 2, 0:MEM], AX.X, ALU.max, negate=True)\
                            .then_inc(shift_ready, 1)
                    if 1 <= u <= U:
                        n = u - 1
                        dve.wait_ge(probs_ready, U0 + n + 1)
                        dve.reciprocal(den[:, n:n + 1], total[:, n:n + 1])
                        dve.drain()
                        dve.tensor_scalar(pr[:, n % 2, :], pr[:, n % 2, :], den[:, n:n + 1], None, ALU.mult)\
                            .then_inc(normed, 1)
                    if u >= 2:
                        n = u - 2
                        h, b = units[n]
                        dve.wait_ge(out_ready, U0 + n + 1)
                        dve.tensor_copy(ox[:, h, b * P:(b + 1) * P], ps[:, 4 + n % 2, 0:P]).then_inc(out_stored, 1)

            def scalar(act):
                for u in range(U + 1):
                    if u < U:
                        act.wait_ge(shift_ready, U0 + u + 1)
                        if u >= 2:
                            act.wait_ge(probs_turned, U0 + u - 1)
                        act.activation(pr[:, u % 2, :], ps[:, u % 2, 0:MEM], ACT.Exp, bias=shift[:, u:u + 1],
                                       accum_out=total[:, u:u + 1]).then_inc(probs_ready, 1)
                        act.wait_ge(probs_ready, U0 + u + 1)
                        act.drain().then_inc(scores_read, 1)
                    if u >= 1:
                        n = u - 1
                        act.wait_ge(probs_turned, U0 + n + 1)
                        if n >= 2:
                            act.wait_ge(out_ready, U0 + n - 1)
                        act.activation(pt[:, n % 2, :], ps[:, 2 + n % 2, 0:MEM], ACT.Copy).then_inc(turned_copied, 1)
            yield dict(pe=tensor, dve=vector, act=scalar)
            core.top = above
            yield project([Job("features", columns_of(IN["w_xo"][0], X_HEADS, 512), None, X_HEADS, 512,
                                          2, add_store(xT, 4), on="dve", source=ox)])
            core.top = mark

        ROUNDS = 4

        def hidden(w, r):
            return w.rearrange("(r k p) n -> r p k n", p=P, k=DC)[bass.ds(r, 1)].rearrange("a p k n -> (a p) k n")

        def down(w, act):
            return Job("features", lambda i, r: hidden(w, r)[:, :, i * 256:(i + 1) * 256], act, DC, 256, 4,
                            add_store(xT), on="dve", needs=True)

        def stages_ffn():
            mark = core.top
            yield feature_norm(core, 0, xT, col["norm_ffn"], hT)
            up = core.take(4, T)
            upT, hP, weights = core.take_pair(DC, T), core.take_pair(DC, T), core.take_pair(2, Project.SLOT)
            core.top = mark
            w_up = IN["w_up"][0].rearrange("(k p) (r n) -> r p k n", p=P, r=ROUNDS)

            def relu2_store(eng, i, u, acc, r):
                eng.activation(up[:, i % 2 * 2 + u, :], acc, ACT.Relu)
                eng.drain()
                eng.activation(up[:, i % 2 * 2 + u, :], up[:, i % 2 * 2 + u, :], ACT.Square)
                eng.drain()
                return eng.activation(upT.hi[:, i * 2 + u, :], up[:, i % 2 * 2 + u, :], ACT.Copy)

            def relu2_low(dve, i, u, r):
                c = i * 2 + u
                return dve.tensor_tensor(upT.lo[:, c, :], up[:, i % 2 * 2 + u, :], upT.hi[:, c, :].bitcast(F32), ALU.subtract)
            yield Project(core, weights, [
                Job("features", lambda i, r: w_up[bass.ds(r, 1)].rearrange("a p k n -> (a p) k n")
                         [:, :, i * 256:(i + 1) * 256], hP, DC, 256, 4, relu2_store, follow=relu2_low),
                down(IN["w_down"][0], upT)], repeat=ROUNDS, start=(hP, hT, DC)).programs()
            yield feature_norm(core, 0, xT, col["norm_final"], xT)

        w2 = IN["w_in_2"][0]

        def stages_delta(gated):
            mark = core.top
            QKV = 3 * AH * AD
            tok = core.take(NT, QKV)
            zt = core.take(NT, AH * AD)
            beta = core.take(NT, AH)
            g = core.take(NT, AH)
            into, whole, onward = core.take(NT, AH), core.take(NT, AH), core.take(NT, AH)
            alog, bias = core.take(AH), core.take(AH)
            ngain = core.take(AD)
            soft = [core.take(NT * AH) for _ in range(3)]
            norm_r = [core.take(NT * 2 * AH) for _ in range(3)]
            base = core.top
            PAD = TAPS_2 - 1
            up = core.take(12, T + PAD)
            cv = core.take(12, T)
            core.top = base
            (s_par, sp0, sp1, s_a, s_g, s_sums, s_exp, pads, conv_ready, feat_ready, s_turned, tok_ready, sq_ready,
             v_ready, root_ready, s_beta) = (
                sem(f"delta_{n}") for n in ("parameters_landed", "softplus_arg", "softplus_exp", "a_log_exp",
                                            "log_decays_ready", "decay_sums_ready", "decays_ready", "pads_zeroed",
                                            "conv_ready", "features_ready", "turned", "tokens_ready",
                                            "squares_ready", "variance_ready", "root_ready", "beta_ready"))
            wv = w2.rearrange("(k p) n -> p k n", p=P)
            al = OFF2["a_beta"]

            def ba_store(eng, i, u, acc, r):
                eng.activation(beta[:, u, :], acc[:, 0:AH], ACT.Sigmoid)
                return eng.activation(g[:, u, :], acc[:, AH:2 * AH], ACT.Copy)
            core.top = mark - DC * T
            weights = core.take_pair(2, Project.SLOT)
            core.top = base + 12 * (T + PAD)
            hP = core.take_pair(DC, T)
            core.top = base
            first = Project(core, weights, [
                Job("features", columns_of(w2, DC, 256), hP, DC, 256, 6,
                         lambda eng, i, u, acc, r: eng.activation(up[:, i * 2 + u, PAD:PAD + T], acc, ACT.Copy),
                         source=hT),
                Job("tokens", columns_of(w2, DC, 256, OFF2["a_z"]), hP, DC, 256, 2,
                         lambda eng, i, u, acc, r: eng.activation(zt[:, u, i * 256:(i + 1) * 256], acc[:, 0:256],
                                                                  ACT.Silu)),
                Job("tokens", columns_of(w2, DC, 2 * AH, al), hP, DC, 2 * AH, 1, ba_store)]).programs()
            first_sp, first_act = first["sp"], first["act"]

            before = len(stages)

            def sync(sp):
                core.begin(sp, before)
                for dst, src, n in ((alog, "a_log_2", AH), (bias, "dt_bias_2", AH), (ngain, "a_norm_g_2", AD)):
                    sp.dma_start(dst, broadcast(IN[src], n)).then_inc(s_par, 16)
                first_sp(sp)

            def scalar(act):
                act.wait_ge(pads, 1)
                first_act(act)
            first.update(sp=sync, act=scalar)
            first_dve = first["dve"]

            def vector(dve):
                dve.memset(up[:, :, 0:PAD], 0.0).then_inc(pads, 1)
                first_dve(dve)
            first["dve"] = vector
            yield first

            gf = g.rearrange("p c h -> p (c h)")
            soft_v, soft_a = softplus(gf, soft[0], soft[1], soft[2], (sp0, sp1), 0, None)
            cw = col["conv_w_2"].rearrange("p (t c) -> p t c", t=TAPS_2)

            def conv_vector(dve):
                dve.wait_ge(s_par, 48)
                dve.tensor_tensor(g, g, bias.unsqueeze(1).to_broadcast([P, NT, AH]), ALU.add)
                dve.drain()
                soft_v(dve)
                dve.wait_ge(s_a, 1)
                dve.scalar_tensor_tensor(out=g, in0=g, scalar=-1.0, in1=alog.unsqueeze(1).to_broadcast([P, NT, AH]),
                                         op0=ALU.mult, op1=ALU.mult).then_inc(s_g, 1)
                for c in range(12):
                    dve.tensor_scalar(cv[:, c, :], up[:, c, 0:T], cw[:, 0, c:c + 1], None, ALU.mult)
                for k in range(1, TAPS_2):
                    dve.drain()
                    for c in range(12):
                        ins = dve.scalar_tensor_tensor(out=cv[:, c, :], in0=up[:, c, k:k + T],
                                                       scalar=cw[:, k, c:c + 1], in1=cv[:, c, :],
                                                       op0=ALU.mult, op1=ALU.add)
                        if k == TAPS_2 - 1:
                            ins.then_inc(conv_ready, 1)
                v, r, a = norm_r
                dve.wait_ge(sq_ready, NT)
                for t in range(NT):
                    dve.tensor_reduce(v[:, t * 2 * AH:(t + 1) * 2 * AH],
                                      squares[:, t, :].rearrange("p (h n) -> p h n", n=AD), AX.X, ALU.add)
                dve.drain()
                dve.tensor_scalar(v, v, EPS, None, ALU.add).then_inc(v_ready, 1)
                dve.wait_ge(root_ready, 1)
                newton_rsqrt(core, dve, v, r, a)
                r3 = r.rearrange("p (t h) -> p t h", t=NT)
                dve.tensor_scalar(r3[:, :, 0:AH], r3[:, :, 0:AH], AD ** -0.5, None, ALU.mult)
                dve.drain()
                for t in range(NT):
                    x = tok[:, t, 0:2 * AH * AD].rearrange("p (h n) -> p h n", n=AD)
                    dve.tensor_tensor(x, x, r3[:, t, :].unsqueeze(2).to_broadcast([P, 2 * AH, AD]), ALU.mult)

            squares = up.rearrange("p a b -> p (a b)")[:, 0:NT * 2 * AH * AD].rearrange("p (t n) -> p t n", t=NT)

            def conv_scalar(act):
                act.wait_ge(s_par, 48)
                act.activation(alog, alog, ACT.Exp).then_inc(s_a, 1)
                soft_a(act)
                act.wait_ge(s_sums, 1)
                for n, dst in enumerate((into, whole, onward)):
                    act.activation(dst.rearrange("p c h -> p (c h)"), ps[:, 7, n * 32:(n + 1) * 32], ACT.Exp)
                for c in range(12):
                    act.wait_ge(conv_ready, c + 1)
                    act.activation(cv[:, c, :], cv[:, c, :], ACT.Silu).then_inc(feat_ready, 1)
                for c in range(12):
                    act.wait_ge(s_turned, c + 1)
                    act.activation(tok[:, :, c * P:(c + 1) * P], ps[:, c % 6, :].rearrange("p (t n) -> p t n", t=NT),
                                   ACT.Copy).then_inc(tok_ready, 1)
                act.wait_ge(tok_ready, 12)
                for t in range(NT):
                    act.activation(squares[:, t, :], tok[:, t, 0:2 * AH * AD], ACT.Square).then_inc(sq_ready, 1)
                act.wait_ge(v_ready, 1)
                act.activation(norm_r[1], norm_r[0], ACT.Sqrt).then_inc(root_ready, 1)

            def conv_tensor(pe):
                pe.wait_ge(s_g, 1)
                for n, mask in enumerate((LE, core.ones, GT)):
                    mm = nc.tensor.matmul(ps[:, 7, n * 32:(n + 1) * 32], mask, gf, start=True, stop=True)
                mm.then_inc(s_sums, 1)
                for c in range(12):
                    pe.wait_ge(feat_ready, c + 1)
                    if c >= 6:
                        pe.wait_ge(tok_ready, c - 5)
                    for t in range(NT):
                        mm = nc.tensor.transpose(ps[:, c % 6, t * P:(t + 1) * P], cv[:, c, t * P:(t + 1) * P],
                                                 core.ident)
                    mm.then_inc(s_turned, 1)
            yield dict(pe=conv_tensor, act=conv_scalar, dve=conv_vector)

            core.top = base
            qkT = core.take(8, T)
            qdT = core.take(4, T)
            kb = core.take(NT, AH * AD)
            vb = core.take(NT, AH * AD)
            kd = core.take(NT, AH * AD)
            after = core.top
            qd = core.take(NT, AH * AD)
            (made, t_turned, t_copied) = (sem(f"delta_{n}") for n in ("decayed_made", "qk_turned", "qk_copied"))
            hd = lambda t: t.rearrange("p (h n) -> p h n", n=AD)
            spread = lambda t: t.unsqueeze(2).to_broadcast([P, AH, AD])

            def prep_pool(gp):
                for c in range(NT):
                    q, k, v = (tok[:, c, n * 512:(n + 1) * 512] for n in range(3))
                    gp.tensor_tensor(hd(qd[:, c, :]), hd(q), spread(into[:, c, :]), ALU.mult)
                    gp.tensor_tensor(hd(vb[:, c, :]), hd(v), spread(beta[:, c, :]), ALU.mult)
                    gp.tensor_tensor(hd(kd[:, c, :]), hd(k), spread(onward[:, c, :]), ALU.mult)
                    gp.tensor_tensor(hd(kb[:, c, :]), hd(k), spread(beta[:, c, :]), ALU.mult)
                gp.drain()
                for c in range(NT):
                    ins = gp.tensor_tensor(hd(kb[:, c, :]), hd(kb[:, c, :]), spread(into[:, c, :]), ALU.mult)
                gp.drain().then_inc(made, 1)

            def prep_tensor(pe):
                for c in range(12):
                    if c >= 8:
                        pe.wait_ge(made, 1)
                        pe.wait_ge(t_copied, c - 7)
                    src = tok[:, :, c * P:(c + 1) * P] if c < 8 else qd[:, :, (c - 8) * P:(c - 7) * P]
                    for t in range(NT):
                        mm = nc.tensor.transpose(ps[:, c % 8, t * P:(t + 1) * P], src[:, t, :], core.ident)
                    mm.then_inc(t_turned, 1)

            def prep_scalar(act):
                for c in range(12):
                    act.wait_ge(t_turned, c + 1)
                    act.activation(qkT[:, c, :] if c < 8 else qdT[:, c - 8, :], ps[:, c % 8, :], ACT.Copy)\
                        .then_inc(t_copied, 1)
            yield dict(pe=prep_tensor, act=prep_scalar, pool=prep_pool)

            core.top = after
            B4 = 4
            LEVELS = 7
            levels = core.take(LEVELS, P)
            levelsT = core.take(LEVELS, P)
            gm = core.take(2, B4, P)
            E = core.take(2, B4 * P)
            N = core.take(B4, P)
            NTr = core.take(B4, P)
            NL = core.take(B4, P)
            X = core.take(B4, P)
            XT = core.take(B4, P)
            Y = core.take(B4, P)
            QK = core.take(2, B4, P)
            U = core.take(2, B4 * AD)
            WT = core.take(4, P)
            V = core.take(2, B4 * AD)
            S = core.take(4, AD)
            O = tok
            core.top = mark + 0
            b4 = lambda t: t.rearrange("p (r n) -> p r n", r=B4)
            wide = lambda t: t.rearrange("p r n -> p (r n)")
            over = lambda m: m.unsqueeze(1).to_broadcast([P, B4, P])
            names = ("masks_made", "steps_made", "sums_ready", "decays_ready", "products_ready", "n_made", "n_turned",
                     "nt_copied", "level_masked", "y_made", "y_copied", "z_made", "x_updated", "uw_ready", "uw_copied",
                     "ws_ready", "v_ready", "out_made", "out_stored", "state_updated", "qk_made", "x_started")
            (masks, steps, sums, decays, prods, n_made, n_turned, nt_copied, lmasked, y_made, y_copied, z_made, x_up,
             uw_ready, uw_copied, ws_ready, v_made, out_made, out_stored, state_up, qk_made, x_start) = (
                sem(f"delta_{n}_") for n in names)

            def mask_pool(gp):
                for tile, lower in ((levels, True), (levelsT, False)):
                    gp.memset(tile, 0.0)
                gp.drain()
                for l in range(LEVELS):
                    b = 1 << l
                    nb = P // (2 * b)
                    v = levels[:, l, :].rearrange("p (n a b) -> p n a b", a=2, b=b)[:, :, 0, :]
                    vT = levelsT[:, l, :].rearrange("p (n a b) -> p n a b", a=2, b=b)[:, :, 1, :]
                    gp.memset(v, 1.0)
                    gp.memset(vT, 1.0)
                gp.drain()
                for l in range(LEVELS):
                    b = 1 << l
                    nb = P // (2 * b)
                    v = levels[:, l, :].rearrange("p (n a b) -> p n a b", a=2, b=b)[:, :, 0, :]
                    vT = levelsT[:, l, :].rearrange("p (n a b) -> p n a b", a=2, b=b)[:, :, 1, :]
                    gp.affine_select(out=v, in_=v, compare_op=ALU.is_ge, fill=0.0, base=-b,
                                     pattern=[[-2 * b, nb], [0, b]], channel_multiplier=1)
                    gp.affine_select(out=vT, in_=vT, compare_op=ALU.is_ge, fill=0.0, base=0,
                                     pattern=[[-2 * b, nb], [0, b]], channel_multiplier=1)
                gp.drain()
                for l in range(LEVELS):
                    b = 1 << l
                    nb = P // (2 * b)
                    v = levels[:, l, :].rearrange("p (n a b) -> p n a b", a=2, b=b)[:, :, 0, :]
                    vT = levelsT[:, l, :].rearrange("p (n a b) -> p n a b", a=2, b=b)[:, :, 1, :]
                    gp.affine_select(out=v, in_=v, compare_op=ALU.is_ge, fill=0.0, base=2 * b - 1,
                                     pattern=[[2 * b, nb], [0, b]], channel_multiplier=-1)
                    gp.affine_select(out=vT, in_=vT, compare_op=ALU.is_ge, fill=0.0, base=b - 1,
                                     pattern=[[2 * b, nb], [0, b]], channel_multiplier=-1)
                gp.drain().then_inc(masks, 1)

            def of_batch(t, c, h):
                return t[:, c, :].rearrange("p (r b) -> p r b", b=2)[:, :, h]

            BATCHES = [(c, h) for c in range(NT) for h in range(2)]

            def delta_pool(gp):
                mask_pool(gp)
                for n, (c, h) in enumerate(BATCHES):
                    if n:
                        gp.wait_ge(sums, 2 * n)
                    gb = of_batch(g, c, h).unsqueeze(2).to_broadcast([P, B4, P])
                    gp.tensor_tensor(gm[:, 0], over(LE), gb, ALU.mult).then_inc(steps, 1)
                    gp.tensor_tensor(gm[:, 1], over(GT), gb, ALU.mult).then_inc(steps, 1)
                    for l in range(1, LEVELS):
                        gp.wait_ge(nt_copied, n + 1)
                        if l > 1 or n:
                            gp.wait_ge(y_made, n * (LEVELS - 1) + l - 1)
                        gp.tensor_tensor(NL, NTr, over(levelsT[:, l, :]), ALU.mult).then_inc(lmasked, 1)

            def pair(t, head, c):
                p0 = 64 * (head % 2)
                return t[p0:p0 + 64, head // 2, c * P:(c + 1) * P]

            def delta_tensor(pe):
                for n, (c, h) in enumerate(BATCHES):
                    hs = range(h, AH, 2)
                    p0 = 64 * h
                    for d, (m1, m2) in enumerate(((LE, GT), (GT, LE))):
                        pe.wait_ge(steps, 2 * n + d + 1)
                        if n:
                            pe.wait_ge(decays, 2 * (n - 1) + d + 1)
                            if d == 1:
                                pe.wait_ge(uw_copied, 2 * n)
                        for r in range(B4):
                            mm = nc.tensor.matmul(ps[:, d, r * P:(r + 1) * P], gm[:, d, r, :], m2,
                                                  start=True, stop=True)
                        mm.then_inc(sums, 1)
                    if n:
                        pe.wait_ge(qk_made, n)
                        pe.wait_ge(x_up, n * (LEVELS - 1) * 2)
                    for r, head in enumerate(hs):
                        kk = pair(qkT[:, 4:8], head, c)
                        nc.tensor.matmul(ps[:, 2, r * P:(r + 1) * P], kk, kk, start=True, stop=True)
                    for r, head in enumerate(hs):
                        mm = nc.tensor.matmul(ps[:, 3, r * P:(r + 1) * P], pair(qkT[:, 4:8], head, c),
                                              pair(qkT, head, c), start=True, stop=True)
                    mm.then_inc(prods, 1)
                    pe.wait_ge(n_made, n + 1)
                    for r in range(B4):
                        mm = nc.tensor.transpose(ps[:, 4, r * P:(r + 1) * P], N[:, r, :], core.ident)
                    mm.then_inc(n_turned, 1)
                    pe.wait_ge(x_start, n + 1)
                    for l in range(1, LEVELS):
                        k = n * (LEVELS - 1) + l
                        pe.wait_ge(lmasked, k)
                        if k > 1:
                            pe.wait_ge(x_up, 2 * (k - 1))
                        for r in range(B4):
                            mm = nc.tensor.matmul(ps[:, 4, r * P:(r + 1) * P], NL[:, r, :], X[:, r, :],
                                                  start=True, stop=True)
                        mm.then_inc(y_made, 1)
                        pe.wait_ge(y_copied, k)
                        for r in range(B4):
                            mm = nc.tensor.matmul(ps[:, 5, r * P:(r + 1) * P], XT[:, r, :], Y[:, r, :],
                                                  start=True, stop=True)
                        mm.then_inc(z_made, 1)
                        for r in range(B4):
                            mm = nc.tensor.matmul(ps[:, 6, r * P:(r + 1) * P], Y[:, r, :], XT[:, r, :],
                                                  start=True, stop=True)
                        mm.then_inc(z_made, 1)
                    pe.wait_ge(x_up, (n + 1) * (LEVELS - 1) * 2)
                    for r, head in enumerate(hs):
                        mm = nc.tensor.matmul(ps[:, 7, r * AD:(r + 1) * AD], XT[:, r, :],
                                              vb[:, c, head * AD:(head + 1) * AD], start=True, stop=True)
                    mm.then_inc(uw_ready, 1)
                    for r, head in enumerate(hs):
                        mm = nc.tensor.matmul(ps[p0:p0 + 64, 1, r * P:(r + 1) * P],
                                              kb[:, c, head * AD:(head + 1) * AD], XT[:, r, :],
                                              start=True, stop=True)
                    mm.then_inc(uw_ready, 1)
                    pe.wait_ge(uw_copied, 2 * (n + 1))
                    if c or h:
                        pe.wait_ge(state_up, n)
                    for r, head in enumerate(hs):
                        mm = nc.tensor.matmul(ps[:, 7, r * AD:(r + 1) * AD],
                                              WT[p0:p0 + 64, r, :], S[p0:p0 + 64, r, :],
                                              start=True, stop=True)
                    mm.then_inc(ws_ready, 1)
                    pe.wait_ge(v_made, n + 1)
                    pe.wait_ge(qk_made, n + 1)
                    for r, head in enumerate(hs):
                        o = ps[:, 4, r * AD:(r + 1) * AD]
                        nc.tensor.matmul(o, pair(qdT, head, c), S[p0:p0 + 64, r, :], start=True, stop=False)
                        mm = nc.tensor.matmul(o, QK[:, h, r, :], V[:, h, r * AD:(r + 1) * AD],
                                              start=False, stop=True)
                    mm.then_inc(out_made, 1)
                    for r, head in enumerate(hs):
                        mm = nc.tensor.matmul(ps[p0:p0 + 64, 5, r * AD:(r + 1) * AD],
                                              kd[:, c, head * AD:(head + 1) * AD],
                                              V[:, h, r * AD:(r + 1) * AD], start=True, stop=True)
                    mm.then_inc(out_made, 1)

            def delta_scalar(act):
                for n, (c, h) in enumerate(BATCHES):
                    if n:
                        act.wait_ge(n_made, n)
                        act.wait_ge(qk_made, n)
                    for d in range(2):
                        act.wait_ge(sums, 2 * n + d + 1)
                        act.activation(E[:, d, :], ps[:, d, :], ACT.Exp).then_inc(decays, 1)
                    act.wait_ge(n_turned, n + 1)
                    if n:
                        act.wait_ge(lmasked, n * (LEVELS - 1))
                    act.activation(wide(NTr), ps[:, 4, :], ACT.Copy).then_inc(nt_copied, 1)
                    for l in range(1, LEVELS):
                        k = n * (LEVELS - 1) + l
                        act.wait_ge(y_made, k)
                        if k > 1:
                            act.wait_ge(z_made, 2 * (k - 1))
                        act.activation(wide(Y), ps[:, 4, :], ACT.Copy).then_inc(y_copied, 1)
                    act.wait_ge(uw_ready, 2 * n + 1)
                    if n:
                        act.wait_ge(v_made, n)
                    act.activation(U[:, h, :], ps[:, 7, 0:B4 * AD], ACT.Copy).then_inc(uw_copied, 1)
                    act.wait_ge(uw_ready, 2 * n + 2)
                    if n:
                        act.wait_ge(ws_ready, n)
                    q = slice(64 * h, 64 * h + 64)
                    act.activation(wide(WT[q]), ps[q, 1, :], ACT.Copy).then_inc(uw_copied, 1)

            def delta_vector(dve):
                dve.memset(S, 0.0)
                dve.wait_ge(masks, 1)
                dve.drain()
                for n, (c, h) in enumerate(BATCHES):
                    bb = of_batch(beta, c, h).unsqueeze(2).to_broadcast([P, B4, P])
                    dve.wait_ge(prods, n + 1)
                    dve.tensor_tensor(N, b4(ps[:, 2, :]), over(GT), ALU.mult)
                    dve.tensor_tensor(QK[:, h], b4(ps[:, 3, :]), over(LE), ALU.mult)
                    dve.drain()
                    dve.wait_ge(decays, 2 * n + 1)
                    dve.tensor_tensor(N, N, b4(E[:, 0, :]), ALU.mult)
                    dve.wait_ge(decays, 2 * n + 2)
                    dve.tensor_tensor(QK[:, h], QK[:, h], b4(E[:, 1, :]), ALU.mult).then_inc(qk_made, 1)
                    dve.drain()
                    dve.tensor_tensor(N, N, bb, ALU.mult).then_inc(n_made, 1)
                    dve.drain()
                    dve.tensor_tensor(X, N, over(levels[:, 0, :]), ALU.mult)
                    dve.drain()
                    dve.tensor_tensor(X, over(core.ident), X, ALU.subtract)
                    dve.wait_ge(nt_copied, n + 1)
                    dve.tensor_tensor(XT, NTr, over(levelsT[:, 0, :]), ALU.mult)
                    dve.drain()
                    dve.tensor_tensor(XT, over(core.ident), XT, ALU.subtract).then_inc(x_start, 1)
                    for l in range(1, LEVELS):
                        k = n * (LEVELS - 1) + l
                        dve.wait_ge(z_made, 2 * k)
                        dve.tensor_tensor(wide(X), wide(X), ps[:, 5, :], ALU.subtract).then_inc(x_up, 1)
                        dve.tensor_tensor(wide(XT), wide(XT), ps[:, 6, :], ALU.subtract).then_inc(x_up, 1)
                        dve.drain()
                    dve.wait_ge(ws_ready, n + 1)
                    dve.tensor_tensor(V[:, h, :], U[:, h, :], ps[:, 7, 0:B4 * AD], ALU.subtract).then_inc(v_made, 1)
                    dve.wait_ge(out_made, 2 * n + 1)
                    dve.tensor_copy(O[:, c, 0:512].rearrange("p (r b n) -> p r b n", b=2, n=AD)[:, :, h, :],
                                    ps[:, 4, 0:B4 * AD].rearrange("p (r n) -> p r n", r=B4))
                    dve.wait_ge(out_made, 2 * n + 2)
                    q = slice(64 * h, 64 * h + 64)
                    dve.tensor_tensor(S[q], S[q], of_batch(whole, c, h)[q].unsqueeze(2).to_broadcast([64, B4, AD]),
                                      ALU.mult)
                    dve.drain()
                    dve.tensor_tensor(wide(S[q]), wide(S[q]), ps[q, 5, 0:B4 * AD], ALU.add)\
                        .then_inc(state_up, 1)
            yield dict(pool=delta_pool, pe=delta_tensor, act=delta_scalar, dve=delta_vector)

            core.top = base
            oT = core.take(4, T)
            sqs = core.take(NT, AH * AD)
            osq, ov, oroot, ogain = (sem(f"delta_out_{n}") for n in (
                "squares_ready", "variance_ready", "root_ready", "gained"))
            v, r, a = (t[:, 0:NT * AH] for t in norm_r)
            oturn = turn(O[:, :, 0:512], oT, 4)

            def out_scalar(act):
                act.activation(sqs, O[:, :, 0:512], ACT.Square).then_inc(osq, 1)
                act.wait_ge(ov, 1)
                act.activation(r, v, ACT.Sqrt).then_inc(oroot, 1)

            def out_vector(dve):
                dve.wait_ge(osq, 1)
                for t in range(NT):
                    dve.tensor_reduce(v[:, t * AH:(t + 1) * AH], hd(sqs[:, t, :]), AX.X, ALU.add)
                dve.drain()
                dve.tensor_scalar(v, v, 1.0 / AD, EPS, ALU.mult, ALU.add).then_inc(ov, 1)
                dve.wait_ge(oroot, 1)
                newton_rsqrt(core, dve, v, r, a)
                for t in range(NT):
                    o = hd(O[:, t, 0:512])
                    dve.tensor_tensor(o, o, spread(r[:, t * AH:(t + 1) * AH]), ALU.mult)
                    dve.drain()
                    dve.tensor_tensor(o, o, ngain.unsqueeze(1).to_broadcast([P, AH, AD]), ALU.mult)
                    dve.drain()
                    ins = dve.tensor_tensor(O[:, t, 0:512], O[:, t, 0:512], zt[:, t, :], ALU.mult)
                ins.then_inc(ogain, 1)
                oturn["dve"](dve)

            def out_tensor(pe):
                pe.wait_ge(ogain, 1)
                oturn["pe"](pe)
            yield dict(act=out_scalar, dve=out_vector, pe=out_tensor)
            core.top = mark
            gate = core.take(DC, T)
            core.top = base + 4 * T
            yield project([
                Job("features", columns_of(w2, DC, 256, OFF2["gate_a"]), None, DC, 256, 4,
                         gate_store(gate, col["b_gate_2"][:, 0:8]), source=hT),
                Job("features", columns_of(IN["w_proj_a_2"][0], 4, 512), None, 4, 512, 2,
                         times_store(gated, gate, 4), on="dve", source=oT)])
            core.top = mark

        def stages_sparse(gated):
            mark = core.top
            SLOTS = 22
            RK, RI, RIK = 8, 12, 20
            v = core.take(NT, BKV * 64)
            iw = core.take(NT, IH)
            inv = core.take(32)
            pos_f = core.take(NT)
            pos_i = core.take(NT)
            sin, cos = core.take(NT, 32), core.take(NT, 32)
            ang, kk, t1 = core.take(NT, 32), core.take(NT, 32), core.take(NT, 32)
            base = core.top
            R = core.take(NT, SLOTS * 64)
            F = core.take(SLOTS // 2, T)
            tmp = core.take(2, 20 * 32)
            heads_of = lambda t, a, b: R[:, t, a * 64:b * 64].rearrange("p (h n) -> p h n", n=64)
            s_pos, s_inv, s_ang, s_trig, pools, s_rot, s_turned, s_copied2 = (
                sem(f"sparse_{n}") for n in ("positions_landed", "frequencies_made", "angles_ready", "sines_ready",
                                             "rotated_part", "rotated", "turned", "copied"))

            def bk_store(eng, i, u, acc, r):
                for h in range(BKV):
                    eng.activation(heads_of(u, RK + 2 * h, RK + 2 * h + 1), acc[:, h * 64:(h + 1) * 64].unsqueeze(1),
                                   ACT.Copy)
                return eng.activation(v[:, u, :], acc[:, 128:256], ACT.Copy)

            def ik_store(eng, i, u, acc, r):
                eng.activation(R[:, u, RIK * 64:(RIK + 1) * 64], acc[:, 0:64], ACT.Copy)
                return eng.activation(iw[:, u, :], acc[:, 64:72], ACT.Copy, scale=float((IH * 64) ** -0.5))
            core.top = base + NT * SLOTS * 64

            def to_R(column):
                return lambda eng, i, u, acc, r: eng.activation(R[:, u, column + i * 256:column + (i + 1) * 256],
                                                                acc[:, 0:256], ACT.Copy)
            first = project([
                Job("tokens", columns_of(w2, DC, 256, OFF2["b_q"]), None, DC, 256, 2, to_R(0), source=hT),
                Job("tokens", columns_of(w2, DC, 256, OFF2["b_k"]), None, DC, 256, 1, bk_store, source=hT),
                Job("tokens", columns_of(w2, DC, 256, OFF2["i_q"]), None, DC, 256, 2, to_R(RI * 64),
                         source=hT),
                Job("tokens", columns_of(w2, DC, 72, OFF2["i_k"]), None, DC, 72, 1, ik_store, source=hT)])
            core.top = base + NT * SLOTS * 64 + SLOTS // 2 * T + 2 * 20 * 32
            first_dve = first["dve"]
            first_sp = first["sp"]
            before = len(stages)

            def sync(sp):
                core.begin(sp, before)
                sp.dma_start(pos_i.bitcast(I32), IN["positions_2"][0].rearrange("(t p) -> p t", p=P),
                             allow_slow_non_contiguous=True).then_inc(s_pos, 16)
                first_sp(sp)

            def freq_pool(gp):
                for i in range(32):
                    gp.memset(inv[:, i:i + 1], float(ROPE_INV[i]))
                gp.drain().then_inc(s_inv, 1)

            def angle_vector(dve):
                dve.wait_ge(s_pos, 16)
                dve.tensor_copy(pos_f, pos_i.bitcast(I32))
                dve.wait_ge(s_inv, 1)
                dve.drain()
                for t in range(NT):
                    dve.tensor_scalar(ang[:, t, :], inv, pos_f[:, t:t + 1], None, ALU.mult)
                dve.drain()
                TWO_PI = 2 * np.pi
                c1 = float(np.float32(6.28125))
                c2 = float(np.float32(TWO_PI - c1))
                c2 = float(np.array(c2, np.float32).view(np.uint32).__and__(0xFFFFF000).astype(np.uint32).view(np.float32))
                c3 = float(np.float32(TWO_PI - c1 - c2))
                MAGIC = 1.5 * 2.0 ** 23
                for dst, shift, edge in ((sin, 0.0, 0.0), (cos, 0.25, np.pi / 2)):
                    dve.tensor_scalar(kk, ang, 1.0 / TWO_PI, shift, ALU.mult, ALU.add)
                    dve.drain()
                    dve.tensor_scalar(kk, kk, MAGIC, None, ALU.add)
                    dve.drain()
                    dve.tensor_scalar(kk, kk, -MAGIC, None, ALU.add)
                    dve.drain()
                    dve.scalar_tensor_tensor(out=dst, in0=kk, scalar=-c1, in1=ang, op0=ALU.mult, op1=ALU.add)
                    dve.drain()
                    dve.scalar_tensor_tensor(out=dst, in0=kk, scalar=-c2, in1=dst, op0=ALU.mult, op1=ALU.add)
                    dve.drain()
                    dve.scalar_tensor_tensor(out=dst, in0=kk, scalar=-c3, in1=dst, op0=ALU.mult, op1=ALU.add)
                    dve.drain()
                    if edge:
                        dve.tensor_scalar(dst, dst, edge, None, ALU.add)
                        dve.drain()
                    dve.tensor_scalar(dst, dst, float(np.float32(3.1415925)), -float(np.float32(3.1415925)),
                                      ALU.min, ALU.max)
                dve.drain().then_inc(s_ang, 1)

            def vector(dve):
                first_dve(dve)
                angle_vector(dve)
            first.update(sp=sync, pool=freq_pool, dve=vector)
            yield first

            def rotate(eng, t, a, b, c, s_, x, y):
                n = b - a
                h = heads_of(t, a, b)
                x1, x2 = h[:, :, 0:32], h[:, :, 32:64]
                cb_ = cos[:, t, :].unsqueeze(1).to_broadcast([P, n, 32])
                sb_ = sin[:, t, :].unsqueeze(1).to_broadcast([P, n, 32])
                xx = x[:, 0:n * 32].rearrange("p (h n) -> p h n", n=32)
                yy = y[:, 0:n * 32].rearrange("p (h n) -> p h n", n=32)
                eng.tensor_tensor(xx, x2, sb_, ALU.mult)
                eng.tensor_tensor(yy, x1, sb_, ALU.mult)
                eng.drain()
                eng.tensor_tensor(x1, x1, cb_, ALU.mult)
                eng.tensor_tensor(x2, x2, cb_, ALU.mult)
                eng.drain()
                eng.tensor_tensor(x1, x1, xx, ALU.subtract)
                eng.tensor_tensor(x2, x2, yy, ALU.add)
                eng.drain()

            tmp2 = core.take(2, 20 * 32)
            MAPS = ((RK + 1, RK), (RK + 3, RK + 2), (RIK + 1, RIK))

            def rot(eng, tiles, buf, name):
                eng.wait_ge(s_trig, 1)
                for t in tiles:
                    for a, b in ((0, 8), (RK, RK + 1), (RK + 2, RK + 3), (RI, RIK + 1)):
                        rotate(eng, t, a, b, cos, sin, buf[:, 0], buf[:, 1])
                    for dst, src in MAPS:
                        eng.tensor_copy(R[:, t, dst * 64:(dst + 1) * 64], R[:, t, src * 64:(src + 1) * 64])
                    eng.drain().then_inc(s_rot if name == "dve" else pools, 1)

            def rot_tensor(pe):
                pe.wait_ge(s_rot, 2)
                pe.wait_ge(pools, 2)
                for c in range(SLOTS // 2):
                    if c >= 8:
                        pe.wait_ge(s_copied2, c - 7)
                    for t in range(NT):
                        mm = nc.tensor.transpose(ps[:, c % 8, t * P:(t + 1) * P], R[:, t, c * P:(c + 1) * P],
                                                 core.ident)
                    mm.then_inc(s_turned, 1)

            def rot_scalar(act):
                act.wait_ge(s_ang, 1)
                act.activation(sin.rearrange("p t n -> p (t n)"), sin.rearrange("p t n -> p (t n)"), ACT.Sin)
                act.activation(cos.rearrange("p t n -> p (t n)"), cos.rearrange("p t n -> p (t n)"), ACT.Sin)
                act.drain().then_inc(s_trig, 1)
                for c in range(SLOTS // 2):
                    act.wait_ge(s_turned, c + 1)
                    act.activation(F[:, c, :], ps[:, c % 8, :], ACT.Copy).then_inc(s_copied2, 1)
            yield dict(act=rot_scalar, pe=rot_tensor, dve=lambda e: rot(e, (0, 1), tmp, "dve"),
                       pool=lambda e: rot(e, (2, 3), tmp2, "pool"))

            core.top = base
            bias = core.take(NT, T)
            score = core.take(NT, T)
            relu = core.take(2, T)
            best = core.take(8)
            assert core.top <= base + NT * SLOTS * 64
            qF, kF, iqF, ikF = F[:, 0:4], F[:, 4:6], F[:, 6:10], F[:, 10]
            i_scored, i_relu, i_used, i_picked = (sem(f"index_{n}") for n in ("scored", "rectified", "added", "picked"))
            FOUND = -3e38
            IU = [(t, h) for t in range(NT) for h in range(IH)]

            def index_tensor(pe):
                for n, (t, h) in enumerate(IU):
                    p0 = 64 * (h % 2)
                    if n >= 2:
                        pe.wait_ge(i_relu, n - 1)
                    nc.tensor.matmul(ps[:, n % 2, 0:(t + 1) * P], iqF[p0:p0 + 64, h // 2, t * P:(t + 1) * P],
                                     ikF[p0:p0 + 64, 0:(t + 1) * P], start=True, stop=True).then_inc(i_scored, 1)

            def index_scalar(act):
                for n, (t, h) in enumerate(IU):
                    act.wait_ge(i_scored, n + 1)
                    if n >= 2:
                        act.wait_ge(i_used, n - 1)
                    act.activation(relu[:, n % 2, 0:(t + 1) * P], ps[:, n % 2, 0:(t + 1) * P], ACT.Relu)\
                        .then_inc(i_relu, 1)

            def index_vector(dve):
                for n, (t, h) in enumerate(IU):
                    k = (t + 1) * P
                    sc = score[:, t, 0:k]
                    dve.wait_ge(i_relu, n + 1)
                    if h == 0:
                        dve.tensor_scalar(sc, relu[:, n % 2, 0:k], iw[:, t, 0:1], None, ALU.mult).then_inc(i_used, 1)
                    else:
                        dve.drain()
                        dve.scalar_tensor_tensor(out=sc, in0=relu[:, n % 2, 0:k], scalar=iw[:, t, h:h + 1], in1=sc,
                                                 op0=ALU.mult, op1=ALU.add).then_inc(i_used, 1)
                    if h < IH - 1:
                        continue
                    dve.drain()
                    dve.memset(score[0:CAUSAL, t, k - CAUSAL:k], NEG)
                    dve.drain()
                    if k <= TOPK:
                        dve.tensor_scalar(bias[:, t, 0:k], sc, NEG / 2, NEG, ALU.is_le, ALU.mult)
                        continue
                    for _ in range(TOPK // 8):
                        dve.max(best, sc)
                        dve.drain()
                        dve.match_replace(out=sc, in_to_replace=best, in_values=sc, imm_value=FOUND)
                        dve.drain()
                    dve.tensor_scalar(bias[:, t, 0:k], sc, FOUND / 2, NEG, ALU.is_gt, ALU.mult)
            yield dict(pe=index_tensor, act=index_scalar, dve=index_vector)

            core.top = base + NT * T
            s, pr, pt = core.take(2, T), core.take(2, T), core.take(2, T)
            U = BH * NT
            shift, total, den = (core.take(U) for _ in range(3))
            assert core.top <= base + NT * SLOTS * 64
            core.top = base + NT * SLOTS * 64 + SLOTS // 2 * T
            o = core.take(NT, BH * 64)
            (scores_ready, scores_read, shift_ready, probs_ready, probs_turned, turned_copied, out_ready,
             out_stored) = mix_sems
            U0 = (HEADS + X_HEADS) * NT
            units = [(t, h) for t in range(NT) for h in range(BH)]

            def tensor(pe):
                for u in range(U + 2):
                    if u < U:
                        t, h = units[u]
                        p0 = 64 * (h % 2)
                        if u >= 2:
                            pe.wait_ge(scores_read, U0 + u - 1)
                        nc.tensor.matmul(ps[:, u % 2, 0:(t + 1) * P], qF[p0:p0 + 64, h // 2, t * P:(t + 1) * P],
                                         kF[p0:p0 + 64, h // 4, 0:(t + 1) * P], start=True, stop=True)\
                            .then_inc(scores_ready, 1)
                    if 1 <= u <= U:
                        n = u - 1
                        t, h = units[n]
                        pe.wait_ge(probs_ready, U0 + n + 1)
                        if n >= 2:
                            pe.wait_ge(turned_copied, U0 + n - 1)
                        for k in range(t + 1):
                            mm = nc.tensor.transpose(ps[:, 2 + n % 2, k * P:(k + 1) * P],
                                                     pr[:, n % 2, k * P:(k + 1) * P], core.ident)
                        mm.then_inc(probs_turned, 1)
                    if u >= 2:
                        n = u - 2
                        t, h = units[n]
                        pe.wait_ge(turned_copied, U0 + n + 1)
                        if n >= 2:
                            pe.wait_ge(out_stored, U0 + n - 1)
                        for k in range(t + 1):
                            mm = nc.tensor.matmul(ps[:, 4 + n % 2, 0:64], pt[:, n % 2, k * P:(k + 1) * P],
                                                  v[:, k, (h // 4) * 64:(h // 4 + 1) * 64],
                                                  start=k == 0, stop=k == t)
                        mm.then_inc(out_ready, 1)

            def vector(dve):
                for u in range(U + 2):
                    if u < U:
                        t, h = units[u]
                        n = (t + 1) * P
                        dve.wait_ge(scores_ready, U0 + u + 1)
                        if u >= 2:
                            dve.wait_ge(probs_ready, U0 + u - 1)
                        dve.scalar_tensor_tensor(out=s[:, u % 2, 0:n], in0=ps[:, u % 2, 0:n], scalar=64 ** -0.5,
                                                 in1=bias[:, t, 0:n], op0=ALU.mult, op1=ALU.add)\
                            .then_inc(scores_read, 1)
                        dve.drain()
                        dve.tensor_reduce(shift[:, u:u + 1], s[:, u % 2, 0:n], AX.X, ALU.max, negate=True)\
                            .then_inc(shift_ready, 1)
                    if u >= 2:
                        n = u - 2
                        t, h = units[n]
                        dve.wait_ge(probs_ready, U0 + n + 1)
                        dve.reciprocal(den[:, n:n + 1], total[:, n:n + 1])
                        dve.drain()
                        dve.wait_ge(out_ready, U0 + n + 1)
                        dve.tensor_scalar(o[:, t, h * 64:(h + 1) * 64], ps[:, 4 + n % 2, 0:64], den[:, n:n + 1],
                                          None, ALU.mult).then_inc(out_stored, 1)

            def scalar(act):
                for u in range(U + 1):
                    if u < U:
                        t, h = units[u]
                        n = (t + 1) * P
                        act.wait_ge(shift_ready, U0 + u + 1)
                        if u >= 2:
                            act.wait_ge(probs_turned, U0 + u - 1)
                        act.activation(pr[:, u % 2, 0:n], s[:, u % 2, 0:n], ACT.Exp, bias=shift[:, u:u + 1],
                                       accum_out=total[:, u:u + 1]).then_inc(probs_ready, 1)
                    if u >= 1:
                        n = u - 1
                        t, h = units[n]
                        act.wait_ge(probs_turned, U0 + n + 1)
                        if n >= 2:
                            act.wait_ge(out_ready, U0 + n - 1)
                        act.activation(pt[:, n % 2, 0:(t + 1) * P], ps[:, 2 + n % 2, 0:(t + 1) * P], ACT.Copy)\
                            .then_inc(turned_copied, 1)
            yield dict(pe=tensor, dve=vector, act=scalar)
            core.top = base
            oT = core.take(4, T)
            gate = core.take(DC, T)
            yield turn(o, oT, 4)
            scratch = core.take(2, T)
            yield project([
                Job("features", columns_of(w2, DC, 256, OFF2["gate_b"]), None, DC, 256, 4,
                         gate_store(gate, col["b_gate_2"][:, 8:16]), source=hT),
                Job("features", columns_of(IN["w_proj_b_2"][0], 4, 512), None, 4, 512, 2,
                         add_times_store(gated, gate, scratch, 4), on="dve", source=oT),
                Job("features", columns_of(IN["w_out_2"][0], DC, 256), None, DC, 256, 4, add_store(xT),
                         on="dve", source=gated, needs=True)])
            core.top = mark

        def stages_moe():
            mark = core.top
            yield feature_norm(core, 0, xT, col["norm2_g_2"], hT)
            core.top = mark
            LG = EG + EXPERTS
            share = core.take(EXPERTS, T)
            above = core.top
            logit = core.take(NT, LG)
            rb = core.take(LG)
            comb = core.take(NT, EXPERTS)
            combT = core.take(T)
            pick = core.take(EXPERTS, P)
            g4, e4, one1, one2, rem, tmp = (core.take(NT, EG) for _ in range(6))
            el16, mm1, mm2, sm = core.take(NT, EXPERTS), core.take(NT), core.take(NT), core.take(NT)
            s_rb, s_arg, s_exp, s_comb, s_ct, s_ctc, s_sh, s_shc = (
                sem(f"router_{n}") for n in ("bias_landed", "logits_shifted", "exponentials", "weights_made",
                                             "weights_turned", "weights_copied", "shares_made",
                                             "shares_stored"))
            wg = IN["w_router_group_2"][0].rearrange("(k p) n -> p k n", p=P)
            we = IN["w_router_expert_2"][0].rearrange("(k p) n -> p k n", p=P)
            first = project([
                Job("tokens", lambda i, r: wg, None, DC, EG, 1,
                         lambda eng, i, u, acc, r: eng.activation(logit[:, u, 0:EG], acc[:, 0:EG], ACT.Copy),
                         source=hT),
                Job("tokens", lambda i, r: we, None, DC, EXPERTS, 1,
                         lambda eng, i, u, acc, r: eng.activation(logit[:, u, EG:LG], acc[:, 0:EXPERTS], ACT.Copy),
                         source=hT)])
            first_sp = first["sp"]
            before = len(stages)

            def sync(sp):
                core.begin(sp, before)
                sp.dma_start(rb[:, 0:EG], broadcast(IN["b_router_group_2"], EG)).then_inc(s_rb, 16)
                sp.dma_start(rb[:, EG:LG], broadcast(IN["b_router_expert_2"], EXPERTS)).then_inc(s_rb, 16)
                first_sp(sp)
            first["sp"] = sync
            yield first

            def row_max(dve, dst, src):
                dve.tensor_reduce(dst, src, AX.X, ALU.max)
                dve.drain()

            def along(t):
                return t.unsqueeze(2).to_broadcast([P, NT, EG])

            def first_of(dve, one, src, top):
                dve.tensor_tensor(one, src, along(top), ALU.is_equal)
                dve.memset(rem[:, :, 0], 1.0)
                dve.drain()
                for j in range(EG):
                    if j:
                        dve.tensor_tensor(rem[:, :, 0], rem[:, :, 0], one[:, :, j - 1], ALU.subtract)
                        dve.drain()
                        dve.tensor_tensor(one[:, :, j], one[:, :, j], rem[:, :, 0], ALU.mult)
                        dve.drain()

            def router_vector(dve):
                dve.wait_ge(s_rb, 32)
                dve.tensor_tensor(logit, logit, rb.unsqueeze(1).to_broadcast([P, NT, LG]), ALU.add)
                dve.drain()
                dve.tensor_copy(g4, logit[:, :, 0:EG])
                dve.drain()
                row_max(dve, mm1, g4)
                first_of(dve, one1, g4, mm1)
                dve.tensor_tensor(g4, g4, along(mm1), ALU.subtract)
                dve.tensor_tensor(el16.rearrange("p t (g k) -> p t g k", g=EG),
                                  logit[:, :, EG:LG].rearrange("p t (g k) -> p t g k", g=EG),
                                  one1.unsqueeze(3).to_broadcast([P, NT, EG, EG]), ALU.mult)
                dve.drain()
                dve.tensor_reduce(e4, el16.rearrange("p t (g k) -> p t k g", g=EG), AX.X, ALU.add)
                dve.drain()
                row_max(dve, mm2, e4)
                dve.tensor_tensor(e4, e4, along(mm2), ALU.subtract)
                dve.drain().then_inc(s_arg, 1)
                dve.wait_ge(s_exp, 1)
                dve.tensor_reduce(mm1, g4, AX.X, ALU.add)
                dve.tensor_reduce(mm2, e4, AX.X, ALU.add)
                dve.drain()
                dve.reciprocal(mm1, mm1)
                dve.reciprocal(mm2, mm2)
                dve.drain()
                dve.tensor_tensor(e4, e4, along(mm2), ALU.mult)
                dve.drain()
                row_max(dve, sm, e4)
                first_of(dve, g4, e4, sm)
                dve.scalar_tensor_tensor(out=tmp, in0=g4, scalar=-2.0, in1=e4, op0=ALU.mult, op1=ALU.add)
                dve.drain()
                row_max(dve, sm, tmp)
                first_of(dve, one2, tmp, sm)
                dve.tensor_tensor(one2, one2, g4, ALU.add)
                dve.drain()
                dve.tensor_tensor(e4, e4, one2, ALU.mult)
                dve.drain()
                dve.tensor_reduce(sm, e4, AX.X, ALU.add)
                dve.drain()
                dve.reciprocal(sm, sm)
                dve.drain()
                dve.tensor_tensor(sm, sm, mm1, ALU.mult)
                dve.drain()
                dve.tensor_tensor(e4, e4, along(sm), ALU.mult)
                dve.drain()
                for gi in range(EG):
                    dve.tensor_tensor(comb[:, :, gi * EG:(gi + 1) * EG], e4,
                                      one1[:, :, gi:gi + 1].to_broadcast([P, NT, EG]), ALU.mult)
                dve.drain().then_inc(s_comb, 1)
                dve.wait_ge(s_ct, 1)
                dve.tensor_copy(combT[0:EXPERTS, :], ps[0:EXPERTS, 4, :]).then_inc(s_ctc, 1)

            def router_scalar(act):
                act.wait_ge(s_arg, 1)
                act.activation(g4, g4, ACT.Exp)
                act.activation(e4, e4, ACT.Exp)
                act.drain().then_inc(s_exp, 1)

            def router_tensor(pe):
                pe.wait_ge(s_comb, 1)
                for t in range(NT):
                    mm = nc.tensor.transpose(ps[0:EXPERTS, 4, t * P:(t + 1) * P], comb[:, t, :], core.ident)
                mm.then_inc(s_ct, 1)

            def router_pool(gp):
                gp.memset(pick, 1.0)
                gp.drain()
                gp.affine_select(out=pick, in_=pick, compare_op=ALU.is_equal, fill=0.0, base=0,
                                 pattern=[[-1, EXPERTS], [0, P]], channel_multiplier=1)
            yield dict(dve=router_vector, act=router_scalar, pe=router_tensor, pool=router_pool)
            def share_tensor(pe):
                for e in range(EXPERTS):
                    if e >= 4:
                        pe.wait_ge(s_shc, e - 3)
                    nc.tensor.matmul(ps[:, 4 + e % 4, :], pick[0:EXPERTS, e, :], combT[0:EXPERTS, :],
                                     start=True, stop=True).then_inc(s_sh, 1)

            def share_vector(dve):
                for e in range(EXPERTS):
                    dve.wait_ge(s_sh, e + 1)
                    dve.tensor_copy(share[:, e, :], ps[:, 4 + e % 4, :]).then_inc(s_shc, 1)
            yield dict(pe=share_tensor, dve=share_vector)

            core.top = above
            expT, hP, weights = core.take_pair(DC, T), core.take_pair(DC, T), core.take_pair(2, Project.SLOT)
            core.top = mark
            silu = hT[:, 0:4, :].rearrange("p (s c) t -> p s c t", s=2)
            made = hT[:, 4:6, :]
            PER = EXPERTS // ROUNDS
            w1v = IN["w_exp_gate_2"][0].rearrange("(r e) (k p) n -> r e p k n", p=P, r=ROUNDS)
            w3v = IN["w_exp_up_2"][0].rearrange("(r e) (k p) n -> r e p k n", p=P, r=ROUNDS)

            def expert(e):
                def weights_of(v):
                    return lambda i, r: v[bass.ds(r, 1), e].rearrange("a p k n -> (a p) k n")

                def silu_store(eng, i, u, acc, r):
                    return eng.activation(silu[:, e % 2, u, :], acc, ACT.Silu)

                def up_store(eng, i, u, acc, r):
                    c = 2 * e + u
                    eng.tensor_tensor(made[:, u, :], acc, silu[:, e % 2, u, :], ALU.mult)
                    eng.drain()
                    one = share[:, bass.ds(r * PER + e, 1), :].rearrange("p a n -> p (a n)")
                    eng.tensor_tensor(made[:, u, :], made[:, u, :], one, ALU.mult)
                    eng.drain()
                    eng.tensor_copy(expT.hi[:, c, :], made[:, u, :])
                    eng.drain()
                    return eng.tensor_tensor(expT.lo[:, c, :], made[:, u, :], expT.hi[:, c, :].bitcast(F32),
                                             ALU.subtract)
                return [Job("features", weights_of(w1v), hP, DC, DE, 1, silu_store),
                        Job("features", weights_of(w3v), hP, DC, DE, 1, up_store, on="dve",
                                 with_last=True)]
            yield Project(core, weights, [j for e in range(PER) for j in expert(e)] +
                               [down(IN["w_exp_down_2"][0].rearrange("e f n -> (e f) n"), expT)],
                               repeat=ROUNDS, start=(hP, hT, DC)).programs()

        def stages_store():
            mark = core.top
            yield feature_norm(core, 0, xT, col["final_norm_g_2"], hT)
            core.top = mark
            final = core.take(NT, D)
            f_turned, f_copied = sem("result_turned"), sem("result_copied")

            def tensor(pe):
                for c in range(DC):
                    for t in range(NT):
                        mm = nc.tensor.transpose(ps[:, c, t * P:(t + 1) * P], hT[:, c, t * P:(t + 1) * P], core.ident)
                    mm.then_inc(f_turned, 1)

            def vector(dve):
                for c in range(0, DC, 2):
                    dve.wait_ge(f_turned, c + 1)
                    dve.tensor_copy(final[:, :, c * P:(c + 1) * P], ps[:, c, :].rearrange("p (t n) -> p t n", t=NT))

            def scalar(act):
                for c in range(1, DC, 2):
                    act.wait_ge(f_turned, c + 1)
                    act.activation(final[:, :, c * P:(c + 1) * P], ps[:, c, :].rearrange("p (t n) -> p t n", t=NT),
                                   ACT.Copy)
            yield dict(pe=tensor, dve=vector, act=scalar)
            before = len(stages)

            def sync(sp):
                core.begin(sp, before)
                for t in range(NT):
                    sp.dma_start(out[0, t * P:(t + 1) * P, :], final[:, t, :]).then_inc(s_out, 16)
                sp.wait_ge(s_out, 16 * NT)
            yield dict(sp=sync)

        stages = []
        run = stages.append
        run(stage_load())
        run(feature_norm(core, 1, xT, col["norm_mix"], hT))
        merged = core.take(DC, T)
        mark2 = core.top
        proj_qkv, attention, attn = stage_attention()
        run(proj_qkv)
        run(attention)
        mark = core.top
        attnT = core.take(DC, T)
        gate = core.take(DC, T)
        run(turn(attn, attnT, DC))
        w1 = IN["w_in"][0]
        run(project([
            Job("features", columns_of(w1, DC, 256, OFF_GATE), None, DC, 256, 4, gate_store(gate), source=hT),
            Job("features", columns_of(IN["w_attn_branch"][0], DC, 256), None, DC, 256, 4,
                     times_store(merged, gate), on="dve", source=attnT)]))
        core.top = mark2
        for st in stages_ssd():
            run(st)
        core.top = mark2 = core.top - DC * T
        for st in stages_cross():
            run(st)
        for st in stages_ffn():
            run(st)
        run(feature_norm(core, 0, xT, col["norm1_g_2"], hT))
        merged2 = core.take(DC, T)
        for st in stages_delta(merged2):
            run(st)
        for st in stages_sparse(merged2):
            run(st)
        core.top = mark2
        for st in stages_moe():
            run(st)
        core.top = mark2
        for st in stages_store():
            run(st)

        if debug:
            dbg = sem("debug_stored")
            def dump(sp):
                n = 0
                for name, buf in dict(merged=merged, hT=hT, xT=xT, merged2=merged2).items():
                    if name in debug:
                        sp.dma_start(debug[name].rearrange("(c p) t -> p c t", p=P), buf).then_inc(dbg, 16)
                        n += 1
                sp.wait_ge(dbg, 16 * n)

        def program(eng, name):
            for n, st in enumerate(stages):
                if name != "sp":
                    core.begin(eng, n)
                if name in st:
                    st[name](eng)
                if name != "sp":
                    core.finish(eng, name)

        with nc.Block() as block:
            @block.sync
            def _(sp):
                program(sp, "sp")
                core.begin(sp, len(stages))
                if debug:
                    dump(sp)

            @block.tensor
            def _(pe):
                program(pe, "pe")

            @block.vector
            def _(dve):
                program(dve, "dve")

            @block.scalar
            def _(act):
                program(act, "act")

            @block.gpsimd
            def _(gp):
                program(gp, "pool")


_DEBUG = {}


def kernel(**inputs):
    from concourse import bacc
    from concourse.bass_utils import run_bass_kernel_spmd

    nc = bacc.Bacc("TRN2", target_bir_lowering=False, num_devices=1)
    arrays, IN = {}, {}
    for name, value in inputs.items():
        a = np.ascontiguousarray(value)
        arrays[f"in_{name}"] = a
        IN[name] = nc.dram_tensor(f"in_{name}", a.shape, mybir.dt.from_np(a.dtype), kind="ExternalInput").ap()
    out = nc.dram_tensor("out", (1, T, D), F32, kind="ExternalOutput").ap()
    debug = {n: nc.dram_tensor(f"debug_{n}", shape, F32, kind="ExternalOutput").ap() for n, shape in _DEBUG.items()}
    mixer_kernel(nc, IN, out, debug)
    r = run_bass_kernel_spmd(nc, [arrays], core_ids=[0])
    got = r.results[0]["out"]
    if _DEBUG:
        return (got,) + tuple(r.results[0][f"debug_{n}"] for n in _DEBUG)
    return got
```

```python
from contextlib import ExitStack

import numpy as np
import concourse.bass as bass
from concourse import mybir

ALU = mybir.AluOpType
ACT = mybir.ActivationFunctionType
F32 = mybir.dt.float32
I32 = mybir.dt.int32
F32R = mybir.dt.float32r
AX = mybir.AxisListType

P = 128
T = 512
NT = T // P
D = 1024
DC = D // P
BANK = 512
EPS = 1e-6
WIDE = 256
NEG = -1e30

MEM = 256
HEADS, KV_HEADS, HD = 16, 4, 64
D_INNER, SSD_HEADS, GROUPS, D_STATE, TAPS = 2048, 32, 8, 128, 5
GH = SSD_HEADS // GROUPS
GW = D_INNER // GROUPS
X_HEADS, XD = 4, 128
D_FF = 4096
OFF_K = HEADS * HD
OFF_V = OFF_K + KV_HEADS * HD
OFF_Z = OFF_V + KV_HEADS * HD
OFF_XBC = OFF_Z + D_INNER
OFF_DT = OFF_XBC + D_INNER + 2 * GROUPS * D_STATE
OFF_GATE = OFF_DT + 2 * SSD_HEADS

AH, AD, TAPS_2 = 8, 64, 4
BH, BKV = 8, 2
IH = 8
TOPK = min(256, T // 4)
CAUSAL = 64
EXPERTS, EG, DE = 16, 4, 256
OFF2 = {}
_at = 0
for _name, _n in (("a_q", 512), ("a_k", 512), ("a_v", 512), ("a_z", 512), ("a_beta", 8), ("a_alpha", 8),
                  ("b_q", 512), ("b_k", 128), ("b_v", 128), ("i_q", 512), ("i_k", 64), ("i_w", 8),
                  ("gate_a", 1024), ("gate_b", 1024)):
    OFF2[_name] = _at
    _at += _n
ROPE_INV = (10000.0 ** (-np.arange(32) / 32)).astype(np.float32)


class Pair:

    def __init__(self, tensor):
        self.hi, self.lo = tensor[:, 0], tensor[:, 1]

    def shaped(self, chunks, n):
        part = Pair.__new__(Pair)
        part.hi, part.lo = (t.rearrange("p a b -> p (a b)")[:, 0:chunks * n].rearrange("p (a b) -> p a b", a=chunks)
                            for t in (self.hi, self.lo))
        return part


class Core:

    def __init__(self, nc, ctx):
        self.nc, self.ctx = nc, ctx
        self.ps = ctx.enter_context(nc.psum_tensor("ps", [P, 8, BANK], F32))
        self.ring = ctx.enter_context(nc.sbuf_tensor("ring", [P, 2, 4096], F32))
        self.arena_size = 44800
        self.arena = ctx.enter_context(nc.sbuf_tensor("arena", [P, self.arena_size], F32))
        self.arena_at = nc.sbuf_base - 4 * self.arena_size
        self.top = 0
        self.pairs = 0
        self.landed = [self.semaphore(f"raw_weights_landed_{s}") for s in range(Project.RAW)]
        self.raw_count = [0] * Project.RAW
        self.hi_made = self.semaphore("weights_hi_made")
        self.split = self.semaphore("weights_split")
        self.pair_hi = self.semaphore("activation_hi_made")
        self.pair_made = self.semaphore("activation_split")
        self.unit_ready = self.semaphore("product_ready")
        self.unit_stored = {e: self.semaphore(f"product_stored_{e}") for e in ("act", "dve")}
        self.followed = self.semaphore("product_followed")
        self.slots = self.units = self.chunks = self.follows = 0
        self.stored = {"act": 0, "dve": 0}
        self.fence = {e: self.semaphore(f"stage_done_{e}") for e in ("pe", "act", "dve", "pool")}

    def semaphore(self, name):
        return self.ctx.enter_context(self.nc.semaphore(name))

    def take_pair(self, chunks, n):
        size = 2 * chunks * n
        self.top = -(-self.top // 8) * 8
        assert self.top + size <= self.arena_size, (self.top, size)
        t = self.nc.alloc_sbuf_tensor_at(f"pair_{self.pairs}", [P, 2, chunks, n], F32R,
                                         offset=self.arena_at + 4 * self.top)
        self.pairs += 1
        self.top += size
        return Pair(t)

    def take(self, *shape):
        n = int(np.prod(shape))
        assert self.top + n <= self.arena_size, (self.top, n)
        v = self.arena[:, self.top:self.top + n]
        self.top += n
        if len(shape) == 2:
            v = v.rearrange("p (a b) -> p a b", a=shape[0])
        elif len(shape) == 3:
            v = v.rearrange("p (a b c) -> p a b c", a=shape[0], b=shape[1])
        elif len(shape) == 4:
            v = v.rearrange("p (a b c d) -> p a b c d", a=shape[0], b=shape[1], c=shape[2])
        return v

    def finish(self, eng, name):
        eng.drain().then_inc(self.fence[name], 1)

    def begin(self, eng, stage):
        if stage:
            for other in self.fence.values():
                eng.wait_ge(other, stage)


def product(nc, out, lhs, rhs, start, stop):
    nc.tensor.matmul(out, lhs[1], rhs[0], start=start, stop=False)
    nc.tensor.matmul(out, lhs[0], rhs[1], start=False, stop=False)
    return nc.tensor.matmul(out, lhs[0], rhs[0], start=False, stop=stop)


class Job:

    def __init__(self, kind, weights, act, kc, cols, slots, store, on="act", nt=T, needs=False, source=None,
                 follow=None, with_last=False):
        self.kind, self.weights, self.act, self.kc, self.cols = kind, weights, act, kc, cols
        self.slots, self.store, self.on, self.nt, self.needs = slots, store, on, nt, needs
        self.source, self.follow, self.with_last = source, follow, with_last
        self.per_slot = -(-cols // P) if kind == "features" else nt // P
        assert kc * cols <= Project.SLOT
        assert not follow or on == "act"


class Project:

    BANKS = 4
    SLOT = 2048
    RAW = 4

    def __init__(self, core, weights, jobs, repeat=1, start=None, params=None):
        self.core, self.repeat, self.pair, self.start = core, repeat, weights, start
        self.plan, self.units = [], []
        self.params = params
        count = {"act": 0, "dve": 0}
        chunks = follows = 0
        self.slot0, self.unit0, self.stored0 = core.slots, core.units, dict(core.stored)
        if start:
            core.chunks += start[2]
        self.chunk0, self.follow0, self.landed0 = core.chunks, core.follows, list(core.raw_count)
        for j in jobs:
            for i in range(j.slots):
                first = len(self.units)
                step = dict(j=j, i=i, first=first, needs=dict(count) if j.needs and i == 0 else None,
                            follows=follows, chunks=chunks, source=j.source is not None and i == 0)
                if step["source"]:
                    chunks += j.kc
                step["chunks_after"] = chunks
                for u in range(j.per_slot):
                    count[j.on] += 1
                    follows += j.follow is not None
                    self.units.append((j.on, count[j.on], follows if j.follow else 0))
                self.plan.append(step)
        self.count, self.chunks, self.follows = count, chunks, follows
        self.n = len(self.plan)
        self.extra = 2 if repeat > 1 else 0
        for k in range(repeat * self.n + self.extra):
            core.raw_count[k % self.RAW] += 16
        core.slots += repeat * self.n + self.extra
        core.units += repeat * len(self.units)
        core.chunks += repeat * chunks
        core.follows += repeat * follows
        for e in count:
            core.stored[e] += repeat * count[e]
        assert repeat == 1 or (self.n % self.RAW == 0 and len(self.units) % self.BANKS == 0)

    def rounds(self, eng, body):
        if self.repeat == 1:
            return body(0)
        with eng.Fori(0, self.repeat) as r:
            body(r)

    def raw(self, k):
        par = k % self.RAW
        half = self.core.ring[:, par // 2, :]
        return half[:, (par % 2) * self.SLOT:(par % 2 + 1) * self.SLOT]

    def sync(self, sp):
        core = self.core
        if self.slot0:
            sp.wait_ge(core.split, self.slot0)
        if self.repeat == 1:
            for k in range(self.n):
                if k == self.RAW and self.params:
                    self.params(sp)
                self.load(sp, k, 0)
            if self.n <= self.RAW and self.params:
                self.params(sp)
        else:
            self.rounds(sp, lambda r: [self.load(sp, k, r) for k in range(self.n)])
        for k in range(self.extra):
            self.load(sp, k, self.repeat)

    def load(self, sp, k, r):
        j, i = self.plan[k]["j"], self.plan[k]["i"]
        if k >= self.RAW or self.repeat > 1:
            assert self.slot0 + k - (self.RAW - 1) > 0
            sp.wait_ge(self.core.split, self.slot0 + k - (self.RAW - 1) + r * self.n)
        view = self.raw(k)[:, 0:j.kc * j.cols].rearrange("p (k n) -> p k n", k=j.kc)
        w = j.weights(i, 0 if isinstance(r, int) else r)
        self.core.nc.sync.dma_start(view, w).then_inc(self.core.landed[k % self.RAW], 16)

    def width(self, k):
        j = self.plan[k % self.n]["j"]
        return j.kc * j.cols

    def split_hi(self, act, k, r):
        core, n = self.core, self.width(k)
        par = k % self.RAW
        act.wait_ge(core.landed[par], self.landed0[par] + 16 * (k // self.RAW + 1) + 16 // self.RAW * self.n * r)
        act.activation(self.pair.hi[:, k % 2, 0:n], self.raw(k)[:, 0:n], ACT.Copy).then_inc(core.hi_made, 1)

    def split_lo(self, dve, k, r):
        core, n = self.core, self.width(k)
        dve.wait_ge(core.hi_made, self.slot0 + k + 1 + r * self.n)
        dve.tensor_tensor(self.pair.lo[:, k % 2, 0:n], self.raw(k)[:, 0:n],
                          self.pair.hi[:, k % 2, 0:n].bitcast(F32), ALU.subtract).then_inc(core.split, 1)

    def wait_needs(self, eng, step, r):
        if step["needs"]:
            for e, c in step["needs"].items():
                if c:
                    eng.wait_ge(self.core.unit_stored[e], self.stored0[e] + c + r * self.count[e])
            if step["follows"]:
                eng.wait_ge(self.core.followed, self.follow0 + step["follows"] + r * self.follows)

    def start_hi(self, act):
        if self.start:
            pair, source, kc = self.start
            for c in range(kc):
                act.activation(pair.hi[:, c, :], source[:, c, :], ACT.Copy).then_inc(self.core.pair_hi, 1)

    def start_lo(self, dve):
        if self.start:
            pair, source, kc = self.start
            for c in range(kc):
                dve.wait_ge(self.core.pair_hi, self.chunk0 - kc + c + 1)
                dve.tensor_tensor(pair.lo[:, c, :], source[:, c, :], pair.hi[:, c, :].bitcast(F32),
                                  ALU.subtract).then_inc(self.core.pair_made, 1)

    def source_hi(self, act, k, r):
        if k < self.n and self.plan[k]["source"]:
            step = self.plan[k]
            j = step["j"]
            self.wait_needs(act, step, r)
            for c in range(j.kc):
                act.activation(j.act.hi[:, c, 0:j.nt], j.source[:, c, 0:j.nt], ACT.Copy).then_inc(self.core.pair_hi, 1)

    def source_lo(self, dve, k, r):
        if k < self.n and self.plan[k]["source"]:
            step = self.plan[k]
            j = step["j"]
            for c in range(j.kc):
                dve.wait_ge(self.core.pair_hi, self.chunk0 + step["chunks"] + c + 1 + r * self.chunks)
                dve.tensor_tensor(j.act.lo[:, c, 0:j.nt], j.source[:, c, 0:j.nt],
                                  j.act.hi[:, c, 0:j.nt].bitcast(F32), ALU.subtract).then_inc(self.core.pair_made, 1)

    def multiply(self, pe, k, r):
        core, nc = self.core, self.core.nc
        step = self.plan[k]
        j, first = step["j"], step["first"]
        pe.wait_ge(core.split, self.slot0 + k + 1 + r * self.n)
        self.wait_needs(pe, step, r)
        w = [t[:, k % 2, 0:j.kc * j.cols].rearrange("p (k n) -> p k n", k=j.kc) for t in (self.pair.hi, self.pair.lo)]
        a = (j.act.hi, j.act.lo)
        for u in range(j.per_slot):
            m = first + u
            bank = m % self.BANKS
            if m >= self.BANKS or self.repeat > 1:
                e, c, f = self.units[m - self.BANKS]
                if m < self.BANKS:
                    c, f = c - self.count[e], f and f - self.follows
                assert self.stored0[e] + c > 0
                pe.wait_ge(core.unit_stored[e], self.stored0[e] + c + r * self.count[e])
                if f > 0:
                    pe.wait_ge(core.followed, self.follow0 + f + r * self.follows)
                else:
                    assert not self.units[m - self.BANKS][2] or m < self.BANKS and self.repeat == 1
            for c in range(j.kc):
                if step["source"] and u == 0:
                    pe.wait_ge(core.pair_made, self.chunk0 + step["chunks"] + c + 1 + r * self.chunks)
                flags = dict(start=c == 0, stop=c == j.kc - 1)
                if j.kind == "features":
                    width = min(P, j.cols - u * P)
                    mm = product(nc, core.ps[0:width, bank, 0:j.nt], [x[:, c, u * P:u * P + width] for x in w],
                                 [x[:, c, 0:j.nt] for x in a], **flags)
                else:
                    mm = product(nc, core.ps[:, bank, 0:j.cols], [x[:, c, u * P:(u + 1) * P] for x in a],
                                 [x[:, c, :] for x in w], **flags)
            mm.then_inc(core.unit_ready, 1)

    def put(self, eng, name, k, r):
        core, step = self.core, self.plan[k]
        j, i, first = step["j"], step["i"], step["first"]
        for u in range(j.per_slot):
            m = first + u
            if j.on == name:
                eng.wait_ge(core.unit_ready, self.unit0 + m + 1 + r * len(self.units))
                if j.with_last:
                    e, c, _ = self.units[m - j.per_slot]
                    eng.wait_ge(core.unit_stored[e], self.stored0[e] + c + r * self.count[e])
                j.store(eng, i, u, core.ps[:, m % self.BANKS, :], r).then_inc(core.unit_stored[name], 1)
            elif j.follow:
                eng.wait_ge(core.unit_stored["act"], self.stored0["act"] + self.units[m][1] + r * self.count["act"])
                j.follow(eng, i, u, r).then_inc(core.followed, 1)
        if k + 2 < self.n or self.repeat > 1:
            if name == "act":
                eng.wait_ge(core.unit_ready, self.unit0 + first + j.per_slot + r * len(self.units))
                self.split_hi(eng, k + 2, r)
            else:
                self.split_lo(eng, k + 2, r)
        if k + 1 < self.n and self.plan[k + 1]["source"]:
            if name == "act":
                eng.wait_ge(core.unit_ready, self.unit0 + first + j.per_slot + r * len(self.units))
                self.source_hi(eng, k + 1, r)
            else:
                self.source_lo(eng, k + 1, r)

    def scalar(self, act):
        self.split_hi(act, 0, 0)
        assert not (self.plan[0]["source"] and self.repeat > 1)
        self.start_hi(act)
        self.source_hi(act, 0, 0)
        if self.n > 1:
            self.split_hi(act, 1, 0)
        self.rounds(act, lambda r: [self.put(act, "act", k, r) for k in range(self.n)])

    def vector(self, dve):
        self.split_lo(dve, 0, 0)
        self.start_lo(dve)
        self.source_lo(dve, 0, 0)
        if self.n > 1:
            self.split_lo(dve, 1, 0)
        self.rounds(dve, lambda r: [self.put(dve, "dve", k, r) for k in range(self.n)])

    def tensor(self, pe):
        if self.start:
            pe.wait_ge(self.core.pair_made, self.chunk0)
        self.rounds(pe, lambda r: [self.multiply(pe, k, r) for k in range(self.n)])

    def programs(self):
        return dict(sp=self.sync, pe=self.tensor, act=self.scalar, dve=self.vector)


def columns_of(w, kc, width, base=0, row0=0):
    view = w.rearrange("(k p) n -> p k n", p=P)
    return lambda i, r: view[:, row0:row0 + kc, base + i * width:base + (i + 1) * width]


def feature_norm(core, stage, src, gain, dst, nt=T):
    nc, ps = core.nc, core.ps
    mark = core.top
    sq = core.take(DC, nt)
    v, r, a = core.take(nt), core.take(nt), core.take(nt)
    core.top = mark
    squares, summed, var_ready, root_ready = core.norm_sems
    k = core.norms
    core.norms += 1

    def scalar(act):
        for c in range(DC):
            act.activation(sq[:, c, :], src[:, c, :], ACT.Square).then_inc(squares, 1)
        act.wait_ge(var_ready, k + 1)
        act.activation(r, v, ACT.Sqrt).then_inc(root_ready, 1)

    def tensor(pe):
        for c in range(DC):
            pe.wait_ge(squares, DC * k + c + 1)
            mm = nc.tensor.matmul(ps[:, 4, 0:nt], core.ones, sq[:, c, :], start=c == 0, stop=c == DC - 1)
        mm.then_inc(summed, 1)

    def vector(dve):
        dve.wait_ge(summed, k + 1)
        dve.tensor_scalar(v, ps[:, 4, 0:nt], 1.0 / D, EPS, ALU.mult, ALU.add).then_inc(var_ready, 1)
        dve.wait_ge(root_ready, k + 1)
        newton_rsqrt(core, dve, v, r, a)
        for c in range(DC):
            dve.scalar_tensor_tensor(out=dst[:, c, :], in0=src[:, c, :], scalar=gain[:, c:c + 1], in1=r,
                                     op0=ALU.mult, op1=ALU.mult)

    return dict(act=scalar, pe=tensor, dve=vector)


def newton_rsqrt(core, dve, v, r, a):
    dve.reciprocal(r, r)
    dve.drain()
    dve.tensor_tensor(a, r, r, ALU.mult)
    dve.drain()
    dve.tensor_tensor(a, a, v, ALU.mult)
    dve.drain()
    dve.tensor_scalar(a, a, -0.5, 1.5, ALU.mult, ALU.add)
    dve.drain()
    dve.tensor_tensor(r, r, a, ALU.mult)
    dve.drain()


def mixer_kernel(nc, IN, out, debug):
    with ExitStack() as ctx:
        core = Core(nc, ctx)
        ps = core.ps
        sem = core.semaphore
        core.norm_sems = [core.semaphore(n) for n in ("squares_ready", "squares_summed", "variance_ready", "root_ready")]
        core.norms = 0

        core.ident = core.take(P)
        core.ones = core.take(P)
        LE, GT, LT, GE = (core.take(P) for _ in range(4))
        PROWS = 3
        rows = core.take(PROWS, P)
        cols = core.take(PROWS * P)
        col = {}
        pieces, at = [], 0
        for name, n in (("norm_mix", 8), ("norm_cross", 8), ("norm_mem", 8), ("norm_ffn", 8), ("norm_final", 8),
                        ("ssd_norm", 16), ("conv_b", 32), ("conv_w", 160), ("norm1_g_2", 8), ("norm2_g_2", 8),
                        ("b_gate_2", 16), ("conv_w_2", 48), ("final_norm_g_2", 8)):
            flat = IN[name]
            flat = {1: lambda a: a.rearrange("(r c) -> r c", c=P),
                    2: lambda a: a.rearrange("a (r c) -> (a r) c", c=P),
                    3: lambda a: a.rearrange("a t (r c) -> (a t r) c", c=P)}[len(flat.shape)](flat)
            col[name] = cols[:, at:at + n]
            done = 0
            while done < n:
                m = min(n - done, P - at % P)
                pieces.append((rows[at % P:at % P + m, at // P, :], flat[done:done + m, :]))
                done, at = done + m, at + m
        assert at <= PROWS * P
        x_at = core.top
        xT = core.take(DC, T)
        hT = core.take(DC, T)
        floor = core.top

        s_small = sem("parameters_landed")
        s_x = sem("x_landed")
        s_made = sem("constants_made")
        s_prow = sem("parameter_rows_zeroed")
        s_turned = sem("chunks_turned")
        s_out = sem("output_stored")
        s_copied = sem("chunks_copied")

        def stage_load():
            mark = core.top
            xt = core.take(NT, D)
            core.top = mark

            def sync(sp):
                for t in range(NT):
                    sp.dma_start(xt[:, t, :], IN["x"][0, t * P:(t + 1) * P, :]).then_inc(s_x, 16)
                sp.wait_ge(s_prow, 1)
                for dst, src in pieces:
                    sp.dma_start(dst, src).then_inc(s_small, 16)

            def pool(gp):
                gp.memset(core.ident, 0.0)
                gp.memset(core.ones, 1.0)
                for m in (LE, GT, LT, GE):
                    gp.memset(m, 1.0)
                gp.drain()
                gp.affine_select(out=core.ident, in_=core.ident, compare_op=ALU.not_equal, fill=1.0, base=0,
                                 pattern=[[-1, P]], channel_multiplier=1)
                for m, cmp, mult in ((LE, ALU.is_ge, -1), (GT, ALU.is_gt, 1), (LT, ALU.is_gt, -1), (GE, ALU.is_ge, 1)):
                    gp.affine_select(out=m, in_=m, compare_op=cmp, fill=0.0, base=0,
                                     pattern=[[-mult, P]], channel_multiplier=mult)

            def vector(dve):
                dve.memset(rows, 0.0).then_inc(s_prow, 1)
                for c in range(DC // 2):
                    dve.wait_ge(s_turned, c + 1)
                    dve.tensor_copy(xT[:, c, :], ps[:, c, :]).then_inc(s_copied, 1)
                dve.wait_ge(s_turned, DC + 1)
                dve.tensor_copy(cols, ps[:, 0, 0:PROWS * P]).then_inc(s_made, 1)

            def scalar(act):
                for c in range(DC // 2, DC):
                    act.wait_ge(s_turned, c + 1)
                    act.activation(xT[:, c, :], ps[:, c, :], ACT.Copy)

            def tensor(pe):
                pe.wait_ge(core.fence["pool"], 1)
                pe.wait_ge(s_x, 16 * NT)
                for c in range(DC):
                    for t in range(NT):
                        mm = nc.tensor.transpose(ps[:, c, t * P:(t + 1) * P], xt[:, t, c * P:(c + 1) * P], core.ident)
                    mm.then_inc(s_turned, 1)
                pe.wait_ge(s_small, 16 * len(pieces))
                pe.wait_ge(s_copied, 1)
                for t in range(PROWS):
                    mm = nc.tensor.transpose(ps[:, 0, t * P:(t + 1) * P], rows[:, t, :], core.ident)
                mm.then_inc(s_turned, 1)
            return dict(sp=sync, pool=pool, dve=vector, act=scalar, pe=tensor)


        s_turned_to = sem("activations_turned")
        turns = [0]

        def turn(src, dst, chunks, nt=T):
            base = turns[0]
            turns[0] += chunks

            def tensor(pe):
                for c in range(chunks):
                    for t in range(nt // P):
                        mm = nc.tensor.transpose(ps[:, c, t * P:(t + 1) * P], src[:, t, c * P:(c + 1) * P], core.ident)
                    mm.then_inc(s_turned_to, 1)

            def vector(dve):
                for c in range(chunks):
                    dve.wait_ge(s_turned_to, base + c + 1)
                    dve.tensor_copy(dst[:, c, :], ps[:, c, 0:nt])
            return dict(pe=tensor, dve=vector)

        def project(jobs, params=None):
            mark = core.top
            n = max(j.source.shape[1] * j.source.shape[2] for j in jobs)
            act, weights = core.take_pair(1, n), core.take_pair(2, Project.SLOT)
            core.top = mark
            last = None
            for j in jobs:
                same = j.source is last
                last = j.source
                j.act = act.shaped(j.kc, j.nt)
                if same:
                    j.source = None
            return Project(core, weights, jobs, params=params).programs()

        def copy_store(dst, scale=1.0, per_slot=2):
            return lambda eng, i, u, acc, r: eng.activation(dst[:, i * per_slot + u, :], acc, ACT.Copy, scale=scale)

        def add_store(dst, per_slot=2):
            return lambda eng, i, u, acc, r: eng.tensor_tensor(dst[:, i * per_slot + u, :], acc,
                                                               dst[:, i * per_slot + u, :], ALU.add)

        def gate_store(dst, bias=None):
            def store(eng, i, u, acc, r):
                m = i * 2 + u
                return eng.activation(dst[:, m, :], acc, ACT.Sigmoid, bias=0.0 if bias is None else bias[:, m:m + 1])
            return store

        def times_store(dst, gate, per_slot=2):
            def store(eng, i, u, acc, r):
                m = i * per_slot + u
                return eng.tensor_tensor(dst[:, m, :], acc, gate[:, m, :], ALU.mult)
            return store

        def add_times_store(dst, gate, scratch, per_slot=2, wait=None):
            def store(eng, i, u, acc, r):
                m = i * per_slot + u
                if wait:
                    eng.wait_ge(*wait)
                eng.tensor_tensor(scratch[:, u % 2, :], acc, gate[:, m, :], ALU.mult)
                eng.drain()
                return eng.tensor_tensor(dst[:, m, :], dst[:, m, :], scratch[:, u % 2, :], ALU.add)
            return store

        def broadcast(src, n):
            return bass.AP(src.tensor, src.offset, [[0, P], [1, n]])

        mix_sems = [sem(f"attention_{n}") for n in ("scores_ready", "scores_read", "shift_ready", "probs_ready",
                                                    "probs_turned", "turned_copied", "mix_ready", "mix_stored")]

        def stage_attention():
            mark = core.top
            qT = core.take(DC, T)
            kd = core.take(KV_HEADS, T)
            v = core.take(NT, KV_HEADS * HD)
            W = 3 * P
            dist = core.take(W)
            dist2 = core.take(W)
            sink = core.take(HEADS)
            above = core.top
            attn = core.take(NT, D)
            s, pr, pt = core.take(3, W), core.take(3, W), core.take(2, W)
            U = HEADS * NT
            top, shift, total, esink, den = (core.take(U) for _ in range(5))
            core.top = above
            w = IN["w_in"][0]

            def k_store(eng, i, u, acc, r):
                for half in range(2):
                    for copy in range(2):
                        ins = eng.activation(kd[64 * copy:64 * copy + 64, 2 * u + half, :],
                                             acc[64 * half:64 * half + 64, :], ACT.Copy)
                return ins

            def dt_store(eng, i, u, acc, r):
                n = 2 * SSD_HEADS
                return eng.activation(dt_raw[:, u * n:(u + 1) * n], acc[:, 0:n], ACT.Copy)

            jobs = [Job("features", columns_of(w, DC, 256), None, DC, 256, 4, copy_store(qT, HD ** -0.5),
                             source=hT),
                    Job("features", columns_of(w, DC, 256, OFF_K), None, DC, 256, 1, k_store, source=hT),
                    Job("tokens", columns_of(w, DC, 256, OFF_V), None, DC, 256, 1,
                             lambda eng, i, u, acc, r: eng.activation(v[:, u, :], acc[:, 0:256], ACT.Copy),
                             source=hT),
                    Job("tokens", columns_of(w, DC, WIDE, OFF_DT), None, DC, WIDE, 1, dt_store,
                        source=hT)]
            first = project(jobs)
            core.top = mark
            s_sink, s_dist, sum_ready = sem("sink_landed"), sem("distances_made"), sem("sums_ready")
            (scores_ready, scores_read, shift_ready, probs_ready, probs_turned, turned_copied, out_ready,
             out_stored) = mix_sems
            first_sp = first["sp"]

            def sync(sp):
                sp.dma_start(sink, broadcast(IN["attn_sink"], HEADS)).then_inc(s_sink, 16)
                first_sp(sp)
            first["sp"] = sync

            def pool(gp):
                gp.iota(dist, pattern=[[-1, W]], base=P, channel_multiplier=1, allow_small_or_imprecise_dtypes=True)
                gp.drain()
                gp.tensor_scalar(dist2, dist, -1.0, None, ALU.mult)
                gp.drain()
                gp.affine_select(out=dist, in_=dist, compare_op=ALU.is_ge, fill=1e32, base=0,
                                 pattern=[[1, W]], channel_multiplier=-1)
                gp.affine_select(out=dist2, in_=dist2, compare_op=ALU.is_ge, fill=1e32, base=2 * P,
                                 pattern=[[-1, W]], channel_multiplier=1)
                gp.drain().then_inc(s_dist, 1)
            first["pool"] = pool

            units = [(h, b, max(0, b - 1), min(NT, b + 2)) for h in range(HEADS) for b in range(NT)]

            def tensor(pe):
                for u in range(U + 3):
                    if u < U:
                        h, b, k0, k1 = units[u]
                        r = 64 * (h % 2)
                        if u >= 3:
                            pe.wait_ge(scores_read, u - 2)
                        nc.tensor.matmul(ps[:, u % 3, 0:(k1 - k0) * P], qT[r:r + 64, h // 2, b * P:(b + 1) * P],
                                         kd[r:r + 64, h // 4, k0 * P:k1 * P], start=True, stop=True)\
                            .then_inc(scores_ready, 1)
                    if 2 <= u <= U + 1:
                        n = u - 2
                        h, b, k0, k1 = units[n]
                        pe.wait_ge(probs_ready, n + 1)
                        if n >= 2:
                            pe.wait_ge(turned_copied, n - 1)
                        for k in range(k1 - k0):
                            mm = nc.tensor.transpose(ps[:, 3 + n % 2, k * P:(k + 1) * P],
                                                     pr[:, n % 3, k * P:(k + 1) * P], core.ident)
                        mm.then_inc(probs_turned, 1)
                    if u >= 3:
                        n = u - 3
                        h, b, k0, k1 = units[n]
                        pe.wait_ge(turned_copied, n + 1)
                        if n >= 2:
                            pe.wait_ge(out_stored, n - 1)
                        for k in range(k1 - k0):
                            mm = nc.tensor.matmul(ps[:, 5 + n % 2, 0:HD], pt[:, n % 2, k * P:(k + 1) * P],
                                                  v[:, k0 + k, (h // 4) * HD:(h // 4 + 1) * HD],
                                                  start=k == 0, stop=k == k1 - k0 - 1)
                        mm.then_inc(out_ready, 1)

            def vector(dve):
                dve.wait_ge(s_dist, 1)
                dve.tensor_tensor(dist, dist, dist2, ALU.max)
                dve.drain()
                dve.wait_ge(s_sink, 16)
                for u in range(U + 3):
                    if u < U:
                        h, b, k0, k1 = units[u]
                        n = (k1 - k0) * P
                        w0 = (k0 - b + 1) * P
                        dve.wait_ge(scores_ready, u + 1)
                        if u >= 3:
                            dve.wait_ge(probs_ready, u - 2)
                        dve.scalar_tensor_tensor(out=s[:, u % 3, 0:n], in0=dist[:, w0:w0 + n],
                                                 scalar=-(2.0 ** (-8.0 * (h + 1) / HEADS)),
                                                 in1=ps[:, u % 3, 0:n], op0=ALU.mult, op1=ALU.add)\
                            .then_inc(scores_read, 1)
                        dve.drain()
                        dve.tensor_reduce(top[:, u:u + 1], s[:, u % 3, 0:n], AX.X, ALU.max)
                        dve.drain()
                        dve.tensor_scalar(shift[:, u:u + 1], top[:, u:u + 1], sink[:, h:h + 1], -1.0,
                                          ALU.max, ALU.mult).then_inc(shift_ready, 1)
                    if u >= 3:
                        n = u - 3
                        h, b = units[n][:2]
                        dve.wait_ge(sum_ready, n + 1)
                        dve.tensor_tensor(den[:, n:n + 1], total[:, n:n + 1], esink[:, n:n + 1], ALU.add)
                        dve.drain()
                        dve.reciprocal(den[:, n:n + 1], den[:, n:n + 1])
                        dve.drain()
                        dve.wait_ge(out_ready, n + 1)
                        dve.tensor_scalar(attn[:, b, h * HD:(h + 1) * HD], ps[:, 5 + n % 2, 0:HD],
                                          den[:, n:n + 1], None, ALU.mult).then_inc(out_stored, 1)

            def scalar(act):
                act.wait_ge(s_sink, 16)
                for u in range(U + 2):
                    if u < U:
                        h, b, k0, k1 = units[u]
                        n = (k1 - k0) * P
                        act.wait_ge(shift_ready, u + 1)
                        if u >= 3:
                            act.wait_ge(probs_turned, u - 2)
                        act.activation(pr[:, u % 3, 0:n], s[:, u % 3, 0:n], ACT.Exp, bias=shift[:, u:u + 1],
                                       accum_out=total[:, u:u + 1]).then_inc(probs_ready, 1)
                        act.activation(esink[:, u:u + 1], sink[:, h:h + 1], ACT.Exp, bias=shift[:, u:u + 1])\
                            .then_inc(sum_ready, 1)
                    if u >= 2:
                        n = u - 2
                        h, b, k0, k1 = units[n]
                        act.wait_ge(probs_turned, n + 1)
                        if n >= 2:
                            act.wait_ge(out_ready, n - 1)
                        act.activation(pt[:, n % 2, 0:(k1 - k0) * P], ps[:, 3 + n % 2, 0:(k1 - k0) * P], ACT.Copy)\
                            .then_inc(turned_copied, 1)
            return first, dict(pe=tensor, dve=vector, act=scalar), attn

        def softplus(x, u, a, b, ready, base, act_too):
            r0, r1 = ready

            def vector(dve):
                dve.tensor_scalar(a, x, -1.0, None, ALU.mult)
                dve.drain()
                dve.tensor_tensor(u, a, x, ALU.min).then_inc(r0, 1)
                dve.wait_ge(r1, base + 1)
                dve.tensor_scalar(a, u, 2.0, None, ALU.add)
                dve.drain()
                dve.reciprocal(a, a)
                dve.drain()
                dve.tensor_tensor(u, u, a, ALU.mult)
                dve.drain()
                dve.tensor_tensor(a, u, u, ALU.mult)
                dve.drain()
                dve.tensor_scalar(b, a, 2.0 / 17, 2.0 / 15, ALU.mult, ALU.add)
                for k in (13, 11, 9, 7, 5, 3, 1):
                    dve.drain()
                    dve.tensor_tensor(b, b, a, ALU.mult)
                    dve.drain()
                    dve.tensor_scalar(b, b, 2.0 / k, None, ALU.add)
                dve.drain()
                dve.tensor_tensor(b, b, u, ALU.mult)
                dve.drain()
                dve.scalar_tensor_tensor(out=x, in0=x, scalar=0.0, in1=b, op0=ALU.max, op1=ALU.add)
                dve.drain()

            def scalar(act):
                act.wait_ge(r0, base + 1)
                act.activation(u, u, ACT.Exp).then_inc(r1, 1)
            return vector, scalar

        ssdT = None

        def stages_ssd():
            mark = core.top
            w = IN["w_in"][0]
            ssdT = core.take(2 * GROUPS, T)
            inner = core.top
            H = SSD_HEADS
            dt = core.take(2, NT, H)
            a = core.take(2, NT, H)
            into = core.take(2, NT, H)
            wst = core.take(2, NT, H)
            whole = core.take(2, NT, H)
            bias, alog = core.take(2, H), core.take(2, H)
            dskip = core.take(H)
            after_dt = core.top
            raw = dt_raw
            u_, a_, b_ = (core.take(NT * 2 * H) for _ in range(3))
            core.top = after_dt
            raw4 = raw.rearrange("p (c d h) -> p c d h", c=NT, d=2)
            s_par, sp0, sp1, s_a, s_exp, s_a_ready, s_sums = (
                sem(n) for n in ("ssd_parameters_landed", "softplus_arg", "softplus_exp", "a_log_exp", "decay_exp",
                                 "log_decays_ready", "decay_sums_ready"))

            before = len(stages)
            parked = nc.dram_tensor("parked", (2, P, DC, T), F32, kind="Internal").ap()
            s_parked, s_unparked, s_h_hi = sem("streams_parked"), sem("streams_back"), sem("ssd_input_hi_made")
            here = core.top
            core.top = x_at
            hP = core.take_pair(DC, T)
            core.top = merged_at
            wP = core.take_pair(2, DC * P)
            core.top = here

            def sync(sp):
                core.begin(sp, before)
                sp.dma_start(bias.rearrange("p d h -> p (d h)"), broadcast(IN["dt_bias"], 2 * H)).then_inc(s_par, 16)
                sp.dma_start(alog.rearrange("p d h -> p (d h)"), broadcast(IN["a_log"], 2 * H)).then_inc(s_par, 16)
                sp.dma_start(dskip, broadcast(IN["d_skip"], H)).then_inc(s_par, 16)
                sp.dma_start(parked[0], xT).then_inc(s_parked, 16)
                sp.dma_start(parked[1], merged).then_inc(s_parked, 16)
            soft_v, soft_a = softplus(raw, u_, a_, b_, (sp0, sp1), 0, None)

            def decay_vector(dve):
                dve.wait_ge(s_par, 48)
                for c in range(NT):
                    dve.tensor_tensor(raw4[:, c], raw4[:, c], bias, ALU.add)
                dve.drain()
                soft_v(dve)
                for d in range(2):
                    dve.tensor_copy(dt[:, d], raw4[:, :, d, :])
                dve.drain()
                dve.wait_ge(s_a, 1)
                for d in range(2):
                    for c in range(NT):
                        ins = dve.scalar_tensor_tensor(out=a[:, d, c, :], in0=dt[:, d, c, :], scalar=-1.0,
                                                       in1=alog[:, d, :], op0=ALU.mult, op1=ALU.mult)
                ins.then_inc(s_a_ready, 1)
                dve.wait_ge(s_exp, 1)
                dve.tensor_tensor(wst, wst, dt, ALU.mult)
                for c in range(DC):
                    dve.wait_ge(s_h_hi, c + 1)
                    dve.tensor_tensor(hP.lo[:, c, :], hT[:, c, :], hP.hi[:, c, :].bitcast(F32), ALU.subtract)

            def decay_scalar(act):
                act.wait_ge(s_par, 48)
                act.activation(alog, alog, ACT.Exp).then_inc(s_a, 1)
                soft_a(act)
                act.wait_ge(s_sums, 1)
                flat = lambda t: t.rearrange("p d c h -> p (d c h)")
                act.activation(flat(into), ps[:, 0, 0:2 * NT * H], ACT.Exp)
                act.activation(flat(whole), ps[:, 1, 0:2 * NT * H], ACT.Exp)
                act.activation(flat(wst), ps[:, 2, 0:2 * NT * H], ACT.Exp).then_inc(s_exp, 1)
                act.wait_ge(s_parked, 32)
                for c in range(DC):
                    act.activation(hP.hi[:, c, :], hT[:, c, :], ACT.Copy).then_inc(s_h_hi, 1)

            def decay_tensor(pe):
                pe.wait_ge(s_a_ready, 1)
                n = NT * H
                for bank, masks in ((0, (LE, GE)), (1, (core.ones, core.ones)), (2, (GT, LT))):
                    for d in range(2):
                        mm = nc.tensor.matmul(ps[:, bank, d * n:(d + 1) * n], masks[d],
                                              a[:, d].rearrange("p c h -> p (c h)"), start=True, stop=True)
                mm.then_inc(s_sums, 1)

            PAD = TAPS // 2
            up = core.take(4, T + 2 * PAD)
            cv = core.take(4, T)
            fT = core.take(4, T)
            xt = core.take(NT, GW)
            Bt = core.take(NT, D_STATE)
            xw = core.take(4, NT, GW)
            xd = core.take(NT, GW)
            prev = core.take(2, NT, GW)
            cb = core.take(2, NT, P)
            am = core.take(4, GH, P)
            ex = core.take(2, GH * P)
            M = xw[:, 2:4].rearrange("p a c n -> p (a c n)").rearrange("p (a n) -> p a n", a=4)
            off = core.take(2, GW)
            junk = core.take(NT, GW)
            ss, vv, rr, aa = (core.take(NT) for _ in range(4))
            core.top = mark
            zt, y = (core.ring[:, 1, DC * GW + i * NT * GW:DC * GW + (i + 1) * NT * GW]
                     .rearrange("p (c n) -> p c n", c=NT) for i in range(2))
            (w_landed0, w_landed1, u_ready, u_copied, z_ready, z_stored, conv_ready, feat_ready, turned,
             tok_ready, xw_ready, st_ready, prev_ready, cb_ready, cb_read, am_ready, diff_ready, ex_ready, m_ready,
             y_ready, y_read, y_done, ss_ready, v_ready, root_ready, y_final, y_turned, y_stored, diag_done, pads_zeroed) = (
                sem(f"ssd_{n}") for n in (
                    "xbc_weights_landed", "z_weights_landed", "xbc_ready", "xbc_copied", "z_ready",
                    "z_stored", "conv_ready", "features_ready", "turned", "tokens_ready", "weighted_ready",
                    "chunk_states_ready", "states_ready", "cb_ready", "cb_read", "steps_ready", "sums_ready",
                    "decays_ready", "mixers_ready", "y_ready", "y_read", "y_gated", "squares_ready", "variance_ready",
                    "root_ready", "y_normed", "y_turned", "y_stored", "diagonal_made", "pads_zeroed"))
            split_before = core.slots
            w_hi, w_split = sem("ssd_weights_hi_made"), sem("ssd_weights_split")
            wv = w.rearrange("(k p) n -> p k n", p=P)
            slot0 = core.ring[:, 0, :].rearrange("p (k n) -> p k n", k=DC)
            slot1 = core.ring[:, 1, 0:DC * GW].rearrange("p (k n) -> p k n", k=DC)
            OFF_B = OFF_XBC + D_INNER
            OFF_C = OFF_B + GROUPS * D_STATE
            cw = col["conv_w"].rearrange("p (t c) -> p t c", t=TAPS)
            ORDER = (2, 3, 0, 1)
            BANKS_X = (3, 0, 1, 2)
            SUMS = (4, 6)

            def chunk_of(g, j):
                return (2 * g, 2 * g + 1, g + 2 * GROUPS, g + 3 * GROUPS)[j]

            def after(eng, s, value):
                if not isinstance(value, int) or value > 0:
                    eng.wait_ge(s, value)

            def columns(at, n):
                return slice(at, at + n) if isinstance(at, int) else bass.ds(at, n)

            def chunk(t, m):
                return t[:, columns(m, 1)]

            def looped(eng, first, middle, last):
                first()
                with eng.Fori(0, GROUPS - 1) as g:
                    middle(g)
                last(GROUPS - 1)

            def chunk_slot(t, n):
                return t[:, n % 2, :].rearrange("p (k n) -> p k n", k=DC)

            def z_slot(t):
                return t.rearrange("p a n -> p (a n)").rearrange("p (k n) -> p k n", k=DC)

            def weights_of(n):
                if n == 4:
                    return slot1, z_slot(wP.hi), z_slot(wP.lo)
                j = ORDER[n]
                return slot0[:, :, j * P:(j + 1) * P], chunk_slot(wP.hi, n), chunk_slot(wP.lo, n)

            def ssd_sync(sp):
                def load(g):
                    after(sp, w_split, g * 5 - 1)
                    for c, n, at in ((0, GW, OFF_XBC + g * GW), (GW, D_STATE, OFF_B + g * D_STATE),
                                     (GW + D_STATE, D_STATE, OFF_C + g * D_STATE)):
                        sp.dma_start(slot0[:, :, c:c + n], wv[:, :, columns(at, n)]).then_inc(w_landed0, 16)
                    after(sp, w_split, g * 5)
                    sp.dma_start(slot1, wv[:, :, columns(OFF_Z + g * GW, GW)]).then_inc(w_landed1, 16)
                sp.wait_ge(core.split, split_before)
                looped(sp, lambda: load(0), lambda g: load(g + 1), lambda g: None)
                sp.wait_ge(z_ready, NT * GROUPS)
                sp.wait_ge(y_turned, 2 * GROUPS)

            def ssd_tensor(pe):
                def features(g, n):
                    bank = BANKS_X[n]
                    pe.wait_ge(w_split, g * 5 + (n + 1))
                    if n == 0:
                        after(pe, cb_read, g)
                    if n == 1:
                        after(pe, prev_ready, g)
                    wt = [chunk_slot(t, n) for t in (wP.hi, wP.lo)]
                    for k in range(DC):
                        mm = product(nc, ps[:, bank, :], [t[:, k, :] for t in wt], [hP.hi[:, k, :], hP.lo[:, k, :]],
                                     start=k == 0, stop=k == DC - 1)
                    mm.then_inc(u_ready, 1)

                def sums(g, n):
                    pe.wait_ge(am_ready, g * 8 + (n + 1))
                    if n == 0:
                        pe.wait_ge(z_stored, g * 4 + 4)
                    if n == 1:
                        after(pe, y_stored, g * 2)
                    after(pe, ex_ready, g * 8 + (n - 1))
                    for r in range(GH):
                        mm = nc.tensor.matmul(ps[:, SUMS[n % 2], r * P:(r + 1) * P], am[:, n % 4, r, :],
                                              (LE, GE)[n % 2], start=True, stop=True)
                    mm.then_inc(diff_ready, 1)

                def turn_y(g):
                    pe.wait_ge(y_final, g + 1)
                    for j in range(2):
                        for t in range(NT):
                            mm = nc.tensor.transpose(ps[:, 6 + j, t * P:(t + 1) * P], y[:, t, j * P:(j + 1) * P],
                                                     core.ident)
                        mm.then_inc(y_turned, 1)

                def front(g, turn_last):
                    pe.wait_ge(feat_ready, g * 4 + 2)
                    pe.wait_ge(u_copied, g * 4 + 4)
                    for c in range(NT):
                        t = slice(c * P, (c + 1) * P)
                        mm = nc.tensor.matmul(ps[:, 3, t], fT[:, 2, t], fT[:, 3, t], start=True, stop=True)
                    mm.then_inc(cb_ready, 1)
                    pe.wait_ge(feat_ready, g * 4 + 4)
                    for j in range(3):
                        for t in range(NT):
                            mm = nc.tensor.transpose(ps[:, j, t * P:(t + 1) * P], fT[:, j, t * P:(t + 1) * P],
                                                     core.ident)
                        mm.then_inc(turned, 1)
                    pe.wait_ge(w_split, g * 5 + 5)
                    after(pe, y_read, g * 4)
                    for t in range(NT):
                        for k in range(DC):
                            mm = product(nc, ps[:, 4 + t // 2, t % 2 * GW:(t % 2 + 1) * GW],
                                         [x[:, k, t * P:(t + 1) * P] for x in (hP.hi, hP.lo)],
                                         [z_slot(x)[:, k, :] for x in (wP.hi, wP.lo)],
                                         start=k == 0, stop=k == DC - 1)
                        mm.then_inc(z_ready, 1)
                    turn_last()
                    pe.wait_ge(xw_ready, g * 4 + 2)
                    pe.wait_ge(tok_ready, g * 3 + 3)
                    n = 0
                    for d, chunks in ((0, (0, 1, 2)), (1, (3, 2, 1))):
                        for c in chunks:
                            mm = nc.tensor.matmul(ps[:, n // 2, (n % 2) * GW:(n % 2 + 1) * GW], Bt[:, c, :],
                                                  xw[:, 2 + d, c, :], start=True, stop=True)
                            n += 1
                    mm.then_inc(st_ready, 1)
                    sums(g, 0)
                    sums(g, 1)

                def back(g, between):
                    for c in range(NT):
                        if c:
                            between(c)
                        if c + 1 < NT:
                            sums(g, 2 * c + 2)
                            sums(g, 2 * c + 3)
                        if c == 0:
                            between(c)
                        t = slice(c * P, (c + 1) * P)
                        if c == 0:
                            pe.wait_ge(prev_ready, g + 1)
                            pe.wait_ge(xw_ready, g * 4 + 4)
                        else:
                            pe.wait_ge(y_read, g * 4 + c)
                        if c > 0:
                            nc.tensor.matmul(ps[:, 5, 0:GW], fT[:, 3, t], prev[:, 0, c, :], start=True, stop=True)
                        if c < NT - 1:
                            nc.tensor.matmul(ps[:, 5, GW:2 * GW], fT[:, 3, t], prev[:, 1, c, :], start=True, stop=True)
                        pe.wait_ge(m_ready, g * 8 + (2 * c + 2))
                        for r in range(GH):
                            for d in range(2):
                                mm = nc.tensor.matmul(ps[:, 7, r * 64:(r + 1) * 64],
                                                      M[:, (2 * c + d) % 4, r * P:(r + 1) * P],
                                                      xw[:, d, c, r * 64:(r + 1) * 64], start=d == 0, stop=d == 1)
                        mm.then_inc(y_ready, 1)

                def first():
                    for n in range(4):
                        features(0, n)
                    front(0, lambda: None)

                def middle(g):
                    back(g, lambda n: features(g + 1, n))
                    front(g + 1, lambda: turn_y(g))

                def last(g):
                    back(g, lambda n: None)
                    turn_y(g)
                looped(pe, first, middle, last)

            def ssd_scalar(act):
                def weights_hi(g, n):
                    src, hi, _ = weights_of(n)
                    if n == 0:
                        act.wait_ge(w_landed0, g * 48 + 48)
                    if n == 4:
                        act.wait_ge(w_landed1, g * 16 + 16)
                    after(act, z_ready if n < 2 else u_ready, g * 4 + (0, 0, 1, 2, 4)[n])
                    act.activation(hi, src, ACT.Copy).then_inc(w_hi, 1)

                def next_weights(g, n):
                    if n != 2:
                        weights_hi(g, min(n + 2, 4))

                def copy_up(g, n):
                    act.wait_ge(u_ready, g * 4 + (n + 1))
                    after(act, conv_ready, g * 4)
                    act.activation(up[:, ORDER[n], PAD:PAD + T], ps[:, BANKS_X[n], :], ACT.Copy).then_inc(u_copied, 1)

                def silus(g):
                    after(act, y_ready, g * 4)
                    for n, j in enumerate(ORDER):
                        act.wait_ge(conv_ready, g * 4 + (n + 1))
                        act.activation(fT[:, j, :], cv[:, j, :], ACT.Silu,
                                       bias=chunk(col["conv_b"], chunk_of(g, j))).then_inc(feat_ready, 1)

                def to_tokens(g):
                    for j in range(3):
                        act.wait_ge(turned, g * 3 + (j + 1))
                        src = ps[:, j, :].rearrange("p (t n) -> p t n", t=NT)
                        dst = xt[:, :, j * P:(j + 1) * P] if j < 2 else Bt
                        act.activation(dst, src, ACT.Copy).then_inc(tok_ready, 1)

                def silu_z(g):
                    for t in range(NT):
                        act.wait_ge(z_ready, g * 4 + (t // 2 * 2 + 2))
                        act.activation(zt[:, t, :], ps[:, 4 + t // 2, t % 2 * GW:(t % 2 + 1) * GW],
                                       ACT.Silu).then_inc(z_stored, 1)

                def decay(g, n):
                    act.wait_ge(diff_ready, g * 8 + (n + 1))
                    after(act, m_ready, g * 8 + (n - 1))
                    act.activation(ex[:, n % 2, :], ps[:, SUMS[n % 2], :], ACT.Exp).then_inc(ex_ready, 1)

                def square(g, c):
                    act.wait_ge(y_done, g * 4 + (c + 1))
                    act.activation(junk[:, c, :], y[:, c, :], ACT.Square, accum_out=ss[:, c:c + 1]).then_inc(ss_ready, 1)

                def back(g, between):
                    for c in range(NT):
                        if c:
                            between(c)
                        if c + 1 < NT:
                            decay(g, 2 * c + 2)
                            decay(g, 2 * c + 3)
                        if c == 0:
                            between(c)
                        if c:
                            square(g, c - 1)
                    square(g, NT - 1)

                def root(g):
                    act.wait_ge(v_ready, g + 1)
                    act.activation(rr, vv, ACT.Sqrt).then_inc(root_ready, 1)

                def store_y(g):
                    for j in range(2):
                        act.wait_ge(y_turned, g * 2 + (j + 1))
                        act.activation(chunk(ssdT, 2 * g + j).rearrange("p a t -> p (a t)"), ps[:, 6 + j, :], ACT.Copy,
                                       scale=chunk(col["ssd_norm"], 2 * g + j)).then_inc(y_stored, 1)

                def first():
                    act.wait_ge(pads_zeroed, 1)
                    weights_hi(0, 0)
                    weights_hi(0, 1)
                    for n in range(4):
                        copy_up(0, n)
                        next_weights(0, n)
                    silus(0)
                    to_tokens(0)
                    silu_z(0)
                    decay(0, 0)
                    decay(0, 1)

                def middle(g):
                    weights_hi(g + 1, 0)
                    weights_hi(g + 1, 1)
                    back(g, lambda n: (copy_up(g + 1, n), next_weights(g + 1, n)))
                    silus(g + 1)
                    root(g)
                    to_tokens(g + 1)
                    silu_z(g + 1)
                    store_y(g)
                    decay(g + 1, 0)
                    decay(g + 1, 1)

                def last(g):
                    back(g, lambda n: None)
                    root(g)
                    store_y(g)
                looped(act, first, middle, last)

            def per_head(t, g, d, c=None):
                if c is None:
                    return t[:, d, :, columns(g * GH, GH)].unsqueeze(3).to_broadcast([P, NT, GH, 64])
                return t[:, d, c, columns(g * GH, GH)].unsqueeze(2).to_broadcast([P, GH, 64])

            heads = lambda t: t.rearrange("p (r n) -> p r n", r=GH)

            def ssd_vector(dve):
                def weights_lo(g, n):
                    src, hi, lo = weights_of(n)
                    dve.wait_ge(w_hi, g * 5 + (n + 1))
                    dve.tensor_tensor(lo, src, hi.bitcast(F32), ALU.subtract).then_inc(w_split, 1)

                def next_weights(g, n):
                    if n != 2:
                        weights_lo(g, min(n + 2, 4))

                def conv(g, n):
                    j, m = ORDER[n], chunk_of(g, ORDER[n])
                    dve.wait_ge(u_copied, g * 4 + (n + 1))
                    after(dve, feat_ready, g * 4)
                    dve.tensor_scalar(cv[:, j, :], up[:, j, 0:T], chunk(cw[:, 0, :], m), None, ALU.mult)
                    for k in range(1, TAPS):
                        dve.drain()
                        ins = dve.scalar_tensor_tensor(out=cv[:, j, :], in0=up[:, j, k:k + T],
                                                       scalar=chunk(cw[:, k, :], m), in1=cv[:, j, :],
                                                       op0=ALU.mult, op1=ALU.add)
                    ins.then_inc(conv_ready, 1)

                def states(g):
                    dve.wait_ge(cb_ready, g + 1)
                    for d, mask in enumerate((LE, GE)):
                        ins = dve.tensor_tensor(cb[:, d], ps[:, 3, :].rearrange("p (c n) -> p c n", c=NT),
                                                mask.unsqueeze(1).to_broadcast([P, NT, P]), ALU.mult)
                    ins.then_inc(cb_read, 1)
                    dve.drain()
                    dve.wait_ge(st_ready, g + 1)
                    adds = {}
                    for n in range(6):
                        adds[n // 3, n % 3] = ps[:, n // 2, (n % 2) * GW:(n % 2 + 1) * GW]
                    for d in range(2):
                        dve.tensor_copy(prev[:, d, (1, 2)[d], :], adds[d, 0])
                    for i in (1, 2):
                        steps = [(d, (i, 3 - i)[d], (i + 1, 2 - i)[d]) for d in range(2)]
                        dve.drain()
                        for d, c, to in steps:
                            dve.tensor_tensor(heads(prev[:, d, to, :]), heads(prev[:, d, c, :]),
                                              per_head(whole, g, d, c), ALU.mult)
                        dve.drain()
                        for d, c, to in steps:
                            dve.tensor_tensor(prev[:, d, to, :], adds[d, i], prev[:, d, to, :], ALU.add)
                    dve.drain().then_inc(prev_ready, 1)

                def mixers(g, n):
                    c, d = n // 2, n % 2
                    dve.wait_ge(ex_ready, g * 8 + (n + 1))
                    if n >= 4:
                        dve.wait_ge(y_ready, g * 4 + (n // 2 - 1))
                    dve.tensor_tensor(heads(M[:, n % 4, :]), heads(ex[:, n % 2, :]),
                                      cb[:, d, c, :].unsqueeze(1).to_broadcast([P, GH, P]), ALU.mult)\
                        .then_inc(m_ready, 1)

                def back(g, between):
                    mixers(g, 0)
                    mixers(g, 1)
                    for c in range(NT):
                        if c + 1 < NT:
                            mixers(g, 2 * c + 2)
                            mixers(g, 2 * c + 3)
                        dve.wait_ge(y_ready, g * 4 + (c + 1))
                        dve.wait_ge(diag_done, g + 1)
                        if c > 0:
                            dve.tensor_tensor(heads(off[:, 0, :]), heads(ps[:, 5, 0:GW]), per_head(into, g, 0, c),
                                              ALU.mult)
                        if c < NT - 1:
                            dve.tensor_tensor(heads(off[:, 1, :]), heads(ps[:, 5, GW:2 * GW]),
                                              per_head(into, g, 1, c), ALU.mult)
                        dve.tensor_tensor(y[:, c, :], ps[:, 7, 0:GW], xd[:, c, :], ALU.add).then_inc(y_read, 1)
                        dve.drain()
                        if c > 0:
                            dve.tensor_tensor(y[:, c, :], y[:, c, :], off[:, 0, :], ALU.add)
                            dve.drain()
                        if c < NT - 1:
                            dve.tensor_tensor(y[:, c, :], y[:, c, :], off[:, 1, :], ALU.add)
                            dve.drain()
                        dve.tensor_tensor(y[:, c, :], y[:, c, :], zt[:, c, :], ALU.mult).then_inc(y_done, 1)
                        between(c)

                def norm(g):
                    dve.wait_ge(ss_ready, g * 4 + 4)
                    dve.tensor_scalar(vv, ss, 1.0 / GW, EPS, ALU.mult, ALU.add).then_inc(v_ready, 1)
                    dve.wait_ge(root_ready, g + 1)
                    newton_rsqrt(core, dve, vv, rr, aa)
                    for c in range(NT):
                        ins = dve.tensor_scalar(y[:, c, :], y[:, c, :], rr[:, c:c + 1], None, ALU.mult)
                    ins.then_inc(y_final, 1)

                def first():
                    dve.memset(up, 0.0).then_inc(pads_zeroed, 1)
                    weights_lo(0, 0)
                    weights_lo(0, 1)
                    for n in range(4):
                        conv(0, n)
                        next_weights(0, n)
                    states(0)

                def middle(g):
                    weights_lo(g + 1, 0)
                    weights_lo(g + 1, 1)
                    back(g, lambda n: (conv(g + 1, n), next_weights(g + 1, n)))
                    norm(g)
                    states(g + 1)

                def last(g):
                    back(g, lambda n: None)
                    norm(g)
                looped(dve, first, middle, last)

            def ssd_pool(gp):
                with gp.Fori(0, GROUPS) as g:
                    def steps(n):
                        c, d = n // 2, n % 2
                        if n >= 4:
                            gp.wait_ge(diff_ready, g * 8 + (n - 3))
                        gp.tensor_tensor(am[:, n % 4], (GT, LT)[d].unsqueeze(1).to_broadcast([P, GH, P]),
                                         a[:, d, c, bass.ds(g * GH, GH)].unsqueeze(2).to_broadcast([P, GH, P]),
                                         ALU.mult).then_inc(am_ready, 1)
                    gp.wait_ge(tok_ready, g * 3 + 2)
                    for n, t in ((2, wst), (3, wst)):
                        for c in range(NT):
                            ins = gp.tensor_tensor(heads(xw[:, n, c, :]), heads(xt[:, c, :]),
                                                   per_head(t, g, n % 2, c), ALU.mult)
                        ins.then_inc(xw_ready, 1)
                    for n in range(4):
                        steps(n)
                    for n, t in ((0, dt), (1, dt)):
                        for c in range(NT):
                            ins = gp.tensor_tensor(heads(xw[:, n, c, :]), heads(xt[:, c, :]),
                                                   per_head(t, g, n % 2, c), ALU.mult)
                        ins.then_inc(xw_ready, 1)
                    for c in range(NT):
                        ins = gp.tensor_tensor(heads(xd[:, c, :]), heads(xt[:, c, :]),
                                               dskip[:, bass.ds(g * GH, GH)].unsqueeze(2).to_broadcast([P, GH, 64]),
                                               ALU.mult)
                    ins.then_inc(diag_done, 1)
                    for n in range(4, 8):
                        steps(n)

            ssd = dict(sp=ssd_sync, pe=ssd_tensor, act=ssd_scalar, dve=ssd_vector, pool=ssd_pool)
            def whole_again(dve):
                for c in range(DC):
                    dve.tensor_tensor(hT[:, c, :], hP.hi[:, c, :].bitcast(F32), hP.lo[:, c, :].bitcast(F32), ALU.add)

            def unpark(sp):
                core.begin(sp, before + 3)
                sp.dma_start(merged, parked[1]).then_inc(s_unparked, 16)
                sp.dma_start(xT, parked[0]).then_inc(s_unparked, 16)

            gate = core.arena[:, inner:inner + DC * T].rearrange("p (a b) -> p a b", a=DC)
            core.top = inner + DC * T
            scratch = core.take(2, T)
            w_branch = IN["w_ssd_branch"][0]
            join = project(
                [Job("features", columns_of(w, DC, 256, OFF_GATE + D), None, DC, 256, 4, gate_store(gate),
                          source=hT)] +
                [Job("features", columns_of(w_branch, DC, 256, row0=c), None, DC, 256, 4,
                     add_times_store(merged, gate, scratch, wait=(s_unparked, 32)), on="dve",
                     source=ssdT[:, c:c + DC, :])
                 for c in (0, DC)] +
                [Job("features", columns_of(IN["w_out"][0], DC, 256), None, DC, 256, 4, add_store(xT),
                          on="dve", source=merged, needs=True)],
                params=unpark)
            core.top = mark
            return dict(sp=sync, pe=decay_tensor, act=decay_scalar, dve=decay_vector), ssd, dict(dve=whole_again), join

        def stages_cross():
            mark = core.top
            MT = MEM // P
            memT = core.take(DC, MEM)
            kx = core.take(X_HEADS, MEM)
            vx = core.take(MT, X_HEADS * XD)
            qx = core.take(X_HEADS, T)
            ox = core.take(X_HEADS, T)
            pr, pt = core.take(3, MEM), core.take(2, MEM)
            U = X_HEADS * NT
            shift, total, den = (core.take(U) for _ in range(3))
            above = core.top
            mt = core.take(MT, D)
            s_mem, normed = sem("memory_landed"), sem("cross_probs_normed")
            (scores_ready, scores_read, shift_ready, probs_ready, probs_turned, turned_copied, out_ready,
             out_stored) = mix_sems
            U0 = HEADS * NT
            before = len(stages)
            load = turn(mt, memT, DC, nt=MEM)
            turn_pe = load["pe"]

            def sync(sp):
                core.begin(sp, before)
                for t in range(MT):
                    sp.dma_start(mt[:, t, :], IN["mem"][0, t * P:(t + 1) * P, :]).then_inc(s_mem, 16)
            load["sp"] = sync

            def wait_turn(pe):
                pe.wait_ge(s_mem, 16 * MT)
                turn_pe(pe)
            load["pe"] = wait_turn
            yield load
            yield feature_norm(core, 0, memT, col["norm_mem"], memT, nt=MEM)
            yield feature_norm(core, 0, xT, col["norm_cross"], hT)
            core.top = mark
            wkv = IN["w_xkv"][0]
            core.top = above
            yield project([
                Job("features", columns_of(IN["w_xq"][0], DC, 256), None, DC, 256, 2,
                         copy_store(qx, XD ** -0.5), source=hT),
                Job("features", columns_of(wkv, DC, 256), None, DC, 256, 2,
                         lambda eng, i, u, acc, r: eng.activation(kx[:, 2 * i + u, :], acc[:, 0:MEM], ACT.Copy),
                         nt=MEM, source=memT),
                Job("tokens", columns_of(wkv, DC, 256, 512), None, DC, 256, 2,
                         lambda eng, i, u, acc, r: eng.activation(vx[:, u, i * 256:(i + 1) * 256], acc[:, 0:256],
                                                                  ACT.Copy), nt=MEM, source=memT)])
            core.top = mark
            units = [(h, b) for h in range(X_HEADS) for b in range(NT)]

            def tensor(pe):
                for u in range(U + 3):
                    if u < U:
                        h, b = units[u]
                        if u >= 3:
                            pe.wait_ge(scores_read, U0 + u - 2)
                        nc.tensor.matmul(ps[:, u % 3, 0:MEM], qx[:, h, b * P:(b + 1) * P], kx[:, h, :],
                                         start=True, stop=True).then_inc(scores_ready, 1)
                    if 2 <= u <= U + 1:
                        n = u - 2
                        pe.wait_ge(normed, n + 1)
                        if n >= 2:
                            pe.wait_ge(turned_copied, U0 + n - 1)
                        for k in range(MT):
                            mm = nc.tensor.transpose(ps[:, 3 + n % 2, k * P:(k + 1) * P],
                                                     pr[:, n % 3, k * P:(k + 1) * P], core.ident)
                        mm.then_inc(probs_turned, 1)
                    if u >= 3:
                        n = u - 3
                        h, b = units[n]
                        pe.wait_ge(turned_copied, U0 + n + 1)
                        if n >= 2:
                            pe.wait_ge(out_stored, U0 + n - 1)
                        for k in range(MT):
                            mm = nc.tensor.matmul(ps[:, 5 + n % 2, 0:P], vx[:, k, h * XD:(h + 1) * XD],
                                                  pt[:, n % 2, k * P:(k + 1) * P], start=k == 0, stop=k == MT - 1)
                        mm.then_inc(out_ready, 1)

            def vector(dve):
                for u in range(U + 3):
                    if u < U:
                        dve.wait_ge(scores_ready, U0 + u + 1)
                        dve.tensor_reduce(shift[:, u:u + 1], ps[:, u % 3, 0:MEM], AX.X, ALU.max, negate=True)\
                            .then_inc(shift_ready, 1)
                    if 1 <= u <= U:
                        n = u - 1
                        dve.wait_ge(probs_ready, U0 + n + 1)
                        dve.reciprocal(den[:, n:n + 1], total[:, n:n + 1])
                        dve.drain()
                        dve.tensor_scalar(pr[:, n % 3, :], pr[:, n % 3, :], den[:, n:n + 1], None, ALU.mult)\
                            .then_inc(normed, 1)
                    if u >= 3:
                        n = u - 3
                        h, b = units[n]
                        dve.wait_ge(out_ready, U0 + n + 1)
                        dve.tensor_copy(ox[:, h, b * P:(b + 1) * P], ps[:, 5 + n % 2, 0:P]).then_inc(out_stored, 1)

            def scalar(act):
                for u in range(U + 2):
                    if u < U:
                        act.wait_ge(shift_ready, U0 + u + 1)
                        if u >= 3:
                            act.wait_ge(probs_turned, U0 + u - 2)
                        act.activation(pr[:, u % 3, :], ps[:, u % 3, 0:MEM], ACT.Exp, bias=shift[:, u:u + 1],
                                       accum_out=total[:, u:u + 1]).then_inc(probs_ready, 1)
                        act.wait_ge(probs_ready, U0 + u + 1)
                        act.drain().then_inc(scores_read, 1)
                    if u >= 2:
                        n = u - 2
                        act.wait_ge(probs_turned, U0 + n + 1)
                        if n >= 2:
                            act.wait_ge(out_ready, U0 + n - 1)
                        act.activation(pt[:, n % 2, :], ps[:, 3 + n % 2, 0:MEM], ACT.Copy).then_inc(turned_copied, 1)
            yield dict(pe=tensor, dve=vector, act=scalar)
            core.top = above
            yield project([Job("features", columns_of(IN["w_xo"][0], X_HEADS, 512), None, X_HEADS, 512,
                                          2, add_store(xT, 4), on="dve", source=ox)])
            core.top = mark

        ROUNDS = 4

        def hidden(w, r):
            return w.rearrange("(r k p) n -> r p k n", p=P, k=DC)[bass.ds(r, 1)].rearrange("a p k n -> (a p) k n")

        def down(w, act):
            return Job("features", lambda i, r: hidden(w, r)[:, :, i * 256:(i + 1) * 256], act, DC, 256, 4,
                            add_store(xT), on="dve", needs=True)

        def stages_ffn():
            mark = core.top
            yield feature_norm(core, 0, xT, col["norm_ffn"], hT)
            up = core.take(4, T)
            upT, hP, weights = core.take_pair(DC, T), core.take_pair(DC, T), core.take_pair(2, Project.SLOT)
            core.top = mark
            w_up = IN["w_up"][0].rearrange("(k p) (r n) -> r p k n", p=P, r=ROUNDS)

            def relu2_store(eng, i, u, acc, r):
                eng.activation(up[:, i % 2 * 2 + u, :], acc, ACT.Relu)
                eng.drain()
                eng.activation(up[:, i % 2 * 2 + u, :], up[:, i % 2 * 2 + u, :], ACT.Square)
                eng.drain()
                return eng.activation(upT.hi[:, i * 2 + u, :], up[:, i % 2 * 2 + u, :], ACT.Copy)

            def relu2_low(dve, i, u, r):
                c = i * 2 + u
                return dve.tensor_tensor(upT.lo[:, c, :], up[:, i % 2 * 2 + u, :], upT.hi[:, c, :].bitcast(F32), ALU.subtract)
            yield Project(core, weights, [
                Job("features", lambda i, r: w_up[bass.ds(r, 1)].rearrange("a p k n -> (a p) k n")
                         [:, :, i * 256:(i + 1) * 256], hP, DC, 256, 4, relu2_store, follow=relu2_low),
                down(IN["w_down"][0], upT)], repeat=ROUNDS, start=(hP, hT, DC)).programs()
            yield feature_norm(core, 0, xT, col["norm_final"], xT)

        w2 = IN["w_in_2"][0]

        def stages_delta(gated):
            mark = core.top
            QKV = 3 * AH * AD
            tok = core.take(NT, QKV)
            zt = core.take(NT, AH * AD)
            beta = core.take(NT, AH)
            g = core.take(NT, AH)
            into, whole, onward = core.take(NT, AH), core.take(NT, AH), core.take(NT, AH)
            alog, bias = core.take(AH), core.take(AH)
            ngain = core.take(AD)
            soft = [core.take(NT * AH) for _ in range(3)]
            norm_r = [core.take(NT * 2 * AH) for _ in range(3)]
            base = core.top
            PAD = TAPS_2 - 1
            up = core.take(12, T + PAD)
            cv = core.take(12, T)
            core.top = base
            (s_par, sp0, sp1, s_a, s_g, s_sums, s_exp, pads, conv_ready, feat_ready, s_turned, tok_ready, sq_ready,
             v_ready, root_ready, s_beta) = (
                sem(f"delta_{n}") for n in ("parameters_landed", "softplus_arg", "softplus_exp", "a_log_exp",
                                            "log_decays_ready", "decay_sums_ready", "decays_ready", "pads_zeroed",
                                            "conv_ready", "features_ready", "turned", "tokens_ready",
                                            "squares_ready", "variance_ready", "root_ready", "beta_ready"))
            wv = w2.rearrange("(k p) n -> p k n", p=P)
            al = OFF2["a_beta"]

            def ba_store(eng, i, u, acc, r):
                eng.activation(beta[:, u, :], acc[:, 0:AH], ACT.Sigmoid)
                return eng.activation(g[:, u, :], acc[:, AH:2 * AH], ACT.Copy)
            core.top = mark - DC * T
            weights = core.take_pair(2, Project.SLOT)
            core.top = base + 12 * (T + PAD)
            hP = core.take_pair(DC, T)
            core.top = base
            before = len(stages)

            def params(sp):
                core.begin(sp, before)
                for dst, src, n in ((alog, "a_log_2", AH), (bias, "dt_bias_2", AH), (ngain, "a_norm_g_2", AD)):
                    sp.dma_start(dst, broadcast(IN[src], n)).then_inc(s_par, 16)

            first = Project(core, weights, [
                Job("features", columns_of(w2, DC, 256), hP, DC, 256, 6,
                         lambda eng, i, u, acc, r: eng.activation(up[:, i * 2 + u, PAD:PAD + T], acc, ACT.Copy),
                         source=hT),
                Job("tokens", columns_of(w2, DC, 256, OFF2["a_z"]), hP, DC, 256, 2,
                         lambda eng, i, u, acc, r: eng.activation(zt[:, u, i * 256:(i + 1) * 256], acc[:, 0:256],
                                                                  ACT.Silu)),
                Job("tokens", columns_of(w2, DC, WIDE, al), hP, DC, WIDE, 1, ba_store)], params=params).programs()
            first_act = first["act"]

            def scalar(act):
                act.wait_ge(pads, 1)
                first_act(act)
            first["act"] = scalar
            first_dve = first["dve"]

            def vector(dve):
                dve.memset(up[:, :, 0:PAD], 0.0).then_inc(pads, 1)
                first_dve(dve)
            first["dve"] = vector
            yield first

            gf = g.rearrange("p c h -> p (c h)")
            soft_v, soft_a = softplus(gf, soft[0], soft[1], soft[2], (sp0, sp1), 0, None)
            cw = col["conv_w_2"].rearrange("p (t c) -> p t c", t=TAPS_2)

            def conv_vector(dve):
                dve.wait_ge(s_par, 48)
                dve.tensor_tensor(g, g, bias.unsqueeze(1).to_broadcast([P, NT, AH]), ALU.add)
                dve.drain()
                soft_v(dve)
                dve.wait_ge(s_a, 1)
                dve.scalar_tensor_tensor(out=g, in0=g, scalar=-1.0, in1=alog.unsqueeze(1).to_broadcast([P, NT, AH]),
                                         op0=ALU.mult, op1=ALU.mult).then_inc(s_g, 1)
                for group in (range(0, 4), range(4, 8), range(8, 12)):
                    for c in group:
                        dve.tensor_scalar(cv[:, c, :], up[:, c, 0:T], cw[:, 0, c:c + 1], None, ALU.mult)
                    for k in range(1, TAPS_2):
                        dve.drain()
                        for c in group:
                            ins = dve.scalar_tensor_tensor(out=cv[:, c, :], in0=up[:, c, k:k + T],
                                                           scalar=cw[:, k, c:c + 1], in1=cv[:, c, :],
                                                           op0=ALU.mult, op1=ALU.add)
                            if k == TAPS_2 - 1:
                                ins.then_inc(conv_ready, 1)
                v, r, a = norm_r
                dve.wait_ge(sq_ready, NT)
                for t in range(NT):
                    dve.tensor_reduce(v[:, t * 2 * AH:(t + 1) * 2 * AH],
                                      squares[:, t, :].rearrange("p (h n) -> p h n", n=AD), AX.X, ALU.add)
                dve.drain()
                dve.tensor_scalar(v, v, EPS, None, ALU.add).then_inc(v_ready, 1)
                dve.wait_ge(root_ready, 1)
                newton_rsqrt(core, dve, v, r, a)
                r3 = r.rearrange("p (t h) -> p t h", t=NT)
                dve.tensor_scalar(r3[:, :, 0:AH], r3[:, :, 0:AH], AD ** -0.5, None, ALU.mult)
                dve.drain()
                for t in range(NT):
                    x = tok[:, t, 0:2 * AH * AD].rearrange("p (h n) -> p h n", n=AD)
                    dve.tensor_tensor(x, x, r3[:, t, :].unsqueeze(2).to_broadcast([P, 2 * AH, AD]), ALU.mult)

            squares = up.rearrange("p a b -> p (a b)")[:, 0:NT * 2 * AH * AD].rearrange("p (t n) -> p t n", t=NT)

            def conv_scalar(act):
                act.wait_ge(s_par, 48)
                act.activation(alog, alog, ACT.Exp).then_inc(s_a, 1)
                soft_a(act)
                act.wait_ge(s_sums, 1)
                for n, dst in enumerate((into, whole, onward)):
                    act.activation(dst.rearrange("p c h -> p (c h)"), ps[:, 7, n * 32:(n + 1) * 32], ACT.Exp)
                for n in range(12 + 4):
                    if n < 12:
                        act.wait_ge(conv_ready, n + 1)
                        act.activation(cv[:, n, :], cv[:, n, :], ACT.Silu).then_inc(feat_ready, 1)
                    if n >= 4:
                        c = n - 4
                        act.wait_ge(s_turned, c + 1)
                        act.activation(tok[:, :, c * P:(c + 1) * P],
                                       ps[:, c % 6, :].rearrange("p (t n) -> p t n", t=NT),
                                       ACT.Copy).then_inc(tok_ready, 1)
                act.wait_ge(tok_ready, 12)
                for t in range(NT):
                    act.activation(squares[:, t, :], tok[:, t, 0:2 * AH * AD], ACT.Square).then_inc(sq_ready, 1)
                act.wait_ge(v_ready, 1)
                act.activation(norm_r[1], norm_r[0], ACT.Sqrt).then_inc(root_ready, 1)

            def conv_tensor(pe):
                pe.wait_ge(s_g, 1)
                for n, mask in enumerate((LE, core.ones, GT)):
                    mm = nc.tensor.matmul(ps[:, 7, n * 32:(n + 1) * 32], mask, gf, start=True, stop=True)
                mm.then_inc(s_sums, 1)
                for c in range(12):
                    pe.wait_ge(feat_ready, c + 1)
                    if c >= 6:
                        pe.wait_ge(tok_ready, c - 5)
                    for t in range(NT):
                        mm = nc.tensor.transpose(ps[:, c % 6, t * P:(t + 1) * P], cv[:, c, t * P:(t + 1) * P],
                                                 core.ident)
                    mm.then_inc(s_turned, 1)
            yield dict(pe=conv_tensor, act=conv_scalar, dve=conv_vector)

            core.top = base
            qkT = core.take(8, T)
            qdT = core.take(4, T)
            kb = core.take(NT, AH * AD)
            vb = core.take(NT, AH * AD)
            kd = core.take(NT, AH * AD)
            after = core.top
            qd = core.take(NT, AH * AD)
            (made, t_turned, t_copied) = (sem(f"delta_{n}") for n in ("decayed_made", "qk_turned", "qk_copied"))
            hd = lambda t: t.rearrange("p (h n) -> p h n", n=AD)
            spread = lambda t: t.unsqueeze(2).to_broadcast([P, AH, AD])

            def prep_pool(gp):
                for c in range(NT):
                    q = tok[:, c, 0:512]
                    gp.tensor_tensor(hd(qd[:, c, :]), hd(q), spread(into[:, c, :]), ALU.mult).then_inc(made, 1)
                for c in range(NT):
                    k = tok[:, c, 512:1024]
                    gp.tensor_tensor(hd(kd[:, c, :]), hd(k), spread(onward[:, c, :]), ALU.mult)

            def prep_vector(dve):
                for c in range(NT):
                    k, v = (tok[:, c, n * 512:(n + 1) * 512] for n in (1, 2))
                    dve.tensor_tensor(hd(kb[:, c, :]), hd(k), spread(beta[:, c, :]), ALU.mult)
                    dve.tensor_tensor(hd(vb[:, c, :]), hd(v), spread(beta[:, c, :]), ALU.mult)
                dve.drain()
                for c in range(NT):
                    dve.tensor_tensor(hd(kb[:, c, :]), hd(kb[:, c, :]), spread(into[:, c, :]), ALU.mult)

            def prep_tensor(pe):
                for c in range(12):
                    if c >= 8:
                        pe.wait_ge(made, NT)
                        pe.wait_ge(t_copied, c - 7)
                    src = tok[:, :, c * P:(c + 1) * P] if c < 8 else qd[:, :, (c - 8) * P:(c - 7) * P]
                    for t in range(NT):
                        mm = nc.tensor.transpose(ps[:, c % 8, t * P:(t + 1) * P], src[:, t, :], core.ident)
                    mm.then_inc(t_turned, 1)

            def prep_scalar(act):
                for c in range(12):
                    act.wait_ge(t_turned, c + 1)
                    act.activation(qkT[:, c, :] if c < 8 else qdT[:, c - 8, :], ps[:, c % 8, :], ACT.Copy)\
                        .then_inc(t_copied, 1)
            yield dict(pe=prep_tensor, act=prep_scalar, pool=prep_pool, dve=prep_vector)

            core.top = after
            B4 = 4
            LEVELS = 7
            levels = core.take(LEVELS, P)
            levelsT = core.take(LEVELS, P)
            gm = [core.take(2, B4, P) for h in range(2)]
            ring = core.ring.rearrange("p a b -> p (a b)").rearrange("p (n r k) -> p n r k", n=16, r=B4)
            N, NTr, NL, X, XT, Y = ([ring[:, 2 * i + h] for h in range(2)] for i in range(6))
            E = [ring[:, 12 + 2 * h:14 + 2 * h].rearrange("p d r k -> p d (r k)") for h in range(2)]
            QK = core.take(2, B4, P)
            U = core.take(2, B4 * AD)
            WT = core.take(4, P)
            V = core.take(2, B4 * AD)
            S = core.take(4, AD)
            O = tok
            core.top = mark + 0
            b4 = lambda t: t.rearrange("p (r n) -> p r n", r=B4)
            wide = lambda t: t.rearrange("p r n -> p (r n)")
            over = lambda m: m.unsqueeze(1).to_broadcast([P, B4, P])
            names = ("masks_made", "steps_made", "sums_ready", "decays_ready", "products_ready", "n_made", "n_turned",
                     "nt_copied", "level_masked", "y_made", "y_copied", "z_made", "x_updated", "uw_ready", "uw_copied",
                     "ws_ready", "v_ready", "out_made", "out_stored", "state_updated", "qk_made", "x_started")
            (masks, steps, sums, decays, prods, n_made, n_turned, nt_copied, lmasked, y_made, y_copied, z_made, x_up,
             uw_ready, uw_copied, ws_ready, v_made, out_made, out_stored, state_up, qk_made, x_start) = (
                sem(f"delta_{n}_") for n in names)

            def mask_pool(gp):
                for tile, lower in ((levels, True), (levelsT, False)):
                    gp.memset(tile, 0.0)
                gp.drain()
                for l in range(LEVELS):
                    b = 1 << l
                    nb = P // (2 * b)
                    v = levels[:, l, :].rearrange("p (n a b) -> p n a b", a=2, b=b)[:, :, 0, :]
                    vT = levelsT[:, l, :].rearrange("p (n a b) -> p n a b", a=2, b=b)[:, :, 1, :]
                    gp.memset(v, 1.0)
                    gp.memset(vT, 1.0)
                gp.drain()
                for l in range(LEVELS):
                    b = 1 << l
                    nb = P // (2 * b)
                    v = levels[:, l, :].rearrange("p (n a b) -> p n a b", a=2, b=b)[:, :, 0, :]
                    vT = levelsT[:, l, :].rearrange("p (n a b) -> p n a b", a=2, b=b)[:, :, 1, :]
                    gp.affine_select(out=v, in_=v, compare_op=ALU.is_ge, fill=0.0, base=-b,
                                     pattern=[[-2 * b, nb], [0, b]], channel_multiplier=1)
                    gp.affine_select(out=vT, in_=vT, compare_op=ALU.is_ge, fill=0.0, base=0,
                                     pattern=[[-2 * b, nb], [0, b]], channel_multiplier=1)
                gp.drain()
                for l in range(LEVELS):
                    b = 1 << l
                    nb = P // (2 * b)
                    v = levels[:, l, :].rearrange("p (n a b) -> p n a b", a=2, b=b)[:, :, 0, :]
                    vT = levelsT[:, l, :].rearrange("p (n a b) -> p n a b", a=2, b=b)[:, :, 1, :]
                    gp.affine_select(out=v, in_=v, compare_op=ALU.is_ge, fill=0.0, base=2 * b - 1,
                                     pattern=[[2 * b, nb], [0, b]], channel_multiplier=-1)
                    gp.affine_select(out=vT, in_=vT, compare_op=ALU.is_ge, fill=0.0, base=b - 1,
                                     pattern=[[2 * b, nb], [0, b]], channel_multiplier=-1)
                gp.drain().then_inc(masks, 1)

            def of_batch(t, c, h):
                return t[:, c, :].rearrange("p (r b) -> p r b", b=2)[:, :, h]

            def bank(h, i):
                return ps[:, 4 * h + i]

            def level_count(c, l, h):
                return 2 * ((LEVELS - 1) * c + (l - 1)) + h + 1

            def delta_pool(gp):
                mask_pool(gp)
                for c in range(NT):
                    for h in range(2):
                        n = 2 * c + h
                        if c:
                            gp.wait_ge(sums, 2 * (n - 2) + 2)
                        gb = of_batch(g, c, h).unsqueeze(2).to_broadcast([P, B4, P])
                        gp.tensor_tensor(gm[h][:, 0], over(LE), gb, ALU.mult).then_inc(steps, 1)
                        gp.tensor_tensor(gm[h][:, 1], over(GT), gb, ALU.mult).then_inc(steps, 1)
                    for l in range(1, LEVELS):
                        for h in range(2):
                            if l == 1:
                                gp.wait_ge(nt_copied, 2 * c + h + 1)
                            if l > 1:
                                gp.wait_ge(y_made, level_count(c, l - 1, h))
                            elif c:
                                gp.wait_ge(y_made, level_count(c - 1, LEVELS - 1, h))
                            gp.tensor_tensor(NL[h], NTr[h], over(levelsT[:, l, :]), ALU.mult).then_inc(lmasked, 1)

            def pair(t, head, c):
                p0 = 64 * (head % 2)
                return t[p0:p0 + 64, head // 2, c * P:(c + 1) * P]

            def delta_tensor(pe):
                def start(c, h):
                    n, hs = 2 * c + h, range(h, AH, 2)
                    if c:
                        pe.wait_ge(state_up, n - 1)
                    for d, (m1, m2) in enumerate(((LE, GT), (GT, LE))):
                        pe.wait_ge(steps, 2 * n + d + 1)
                        for r in range(B4):
                            mm = nc.tensor.matmul(bank(h, d)[:, r * P:(r + 1) * P], gm[h][:, d, r, :], m2,
                                                  start=True, stop=True)
                        mm.then_inc(sums, 1)
                    for r, head in enumerate(hs):
                        kk = pair(qkT[:, 4:8], head, c)
                        nc.tensor.matmul(bank(h, 2)[:, r * P:(r + 1) * P], kk, kk, start=True, stop=True)
                    for r, head in enumerate(hs):
                        mm = nc.tensor.matmul(bank(h, 3)[:, r * P:(r + 1) * P], pair(qkT[:, 4:8], head, c),
                                              pair(qkT, head, c), start=True, stop=True)
                    mm.then_inc(prods, 1)

                def level_y(c, l, h):
                    k = level_count(c, l, h)
                    pe.wait_ge(lmasked, k)
                    if l > 1:
                        pe.wait_ge(x_up, 2 * (k - 2))
                    for r in range(B4):
                        mm = nc.tensor.matmul(bank(h, 0)[:, r * P:(r + 1) * P], NL[h][:, r, :], X[h][:, r, :],
                                              start=True, stop=True)
                    mm.then_inc(y_made, 1)

                def level_z(c, l, h):
                    pe.wait_ge(y_copied, level_count(c, l, h))
                    for r in range(B4):
                        mm = nc.tensor.matmul(bank(h, 1)[:, r * P:(r + 1) * P], XT[h][:, r, :], Y[h][:, r, :],
                                              start=True, stop=True)
                    mm.then_inc(z_made, 1)
                    for r in range(B4):
                        mm = nc.tensor.matmul(bank(h, 2)[:, r * P:(r + 1) * P], Y[h][:, r, :], XT[h][:, r, :],
                                              start=True, stop=True)
                    mm.then_inc(z_made, 1)

                def uw(c, h):
                    p0, hs = 64 * h, range(h, AH, 2)
                    pe.wait_ge(x_up, 2 * level_count(c, LEVELS - 1, h))
                    for r, head in enumerate(hs):
                        mm = nc.tensor.matmul(bank(h, 3)[:, r * AD:(r + 1) * AD], XT[h][:, r, :],
                                              vb[:, c, head * AD:(head + 1) * AD], start=True, stop=True)
                    mm.then_inc(uw_ready, 1)
                    for r, head in enumerate(hs):
                        mm = nc.tensor.matmul(bank(h, 1)[p0:p0 + 64, r * P:(r + 1) * P],
                                              kb[:, c, head * AD:(head + 1) * AD], XT[h][:, r, :],
                                              start=True, stop=True)
                    mm.then_inc(uw_ready, 1)

                def w_state(c, h):
                    n, p0 = 2 * c + h, 64 * h
                    pe.wait_ge(uw_copied, 2 * (n + 1))
                    if c:
                        pe.wait_ge(state_up, n - 1)
                    for r in range(B4):
                        mm = nc.tensor.matmul(bank(h, 3)[:, r * AD:(r + 1) * AD],
                                              WT[p0:p0 + 64, r, :], S[p0:p0 + 64, r, :],
                                              start=True, stop=True)
                    mm.then_inc(ws_ready, 1)

                def outputs(c, h):
                    n, p0, hs = 2 * c + h, 64 * h, range(h, AH, 2)
                    pe.wait_ge(v_made, n + 1)
                    pe.wait_ge(qk_made, n + 1)
                    for r, head in enumerate(hs):
                        o = bank(h, 0)[:, r * AD:(r + 1) * AD]
                        nc.tensor.matmul(o, pair(qdT, head, c), S[p0:p0 + 64, r, :], start=True, stop=False)
                        mm = nc.tensor.matmul(o, QK[:, h, r, :], V[:, h, r * AD:(r + 1) * AD],
                                              start=False, stop=True)
                    mm.then_inc(out_made, 1)
                    for r, head in enumerate(hs):
                        mm = nc.tensor.matmul(bank(h, 2)[p0:p0 + 64, r * AD:(r + 1) * AD],
                                              kd[:, c, head * AD:(head + 1) * AD],
                                              V[:, h, r * AD:(r + 1) * AD], start=True, stop=True)
                    mm.then_inc(out_made, 1)

                for c in range(NT):
                    for h in range(2):
                        start(c, h)
                    for h in range(2):
                        pe.wait_ge(n_made, 2 * c + h + 1)
                        for r in range(B4):
                            mm = nc.tensor.transpose(bank(h, 0)[:, r * P:(r + 1) * P], N[h][:, r, :], core.ident)
                        mm.then_inc(n_turned, 1)
                    for l in range(1, LEVELS):
                        for h in range(2):
                            if l == 1:
                                pe.wait_ge(x_start, 2 * c + h + 1)
                            level_y(c, l, h)
                        for h in range(2):
                            level_z(c, l, h)
                    for h in range(2):
                        uw(c, h)
                    for h in range(2):
                        w_state(c, h)
                    for h in range(2):
                        outputs(c, h)

            def delta_scalar(act):
                for c in range(NT):
                    for h in range(2):
                        n = 2 * c + h
                        if c:
                            act.wait_ge(n_made, n - 1)
                            act.wait_ge(qk_made, n - 1)
                        for d in range(2):
                            act.wait_ge(sums, 2 * n + d + 1)
                            act.activation(E[h][:, d, :], bank(h, d), ACT.Exp).then_inc(decays, 1)
                    for h in range(2):
                        act.wait_ge(n_turned, 2 * c + h + 1)
                        if c:
                            act.wait_ge(lmasked, level_count(c - 1, LEVELS - 1, h))
                        act.activation(wide(NTr[h]), bank(h, 0), ACT.Copy).then_inc(nt_copied, 1)
                    for l in range(1, LEVELS):
                        for h in range(2):
                            k = level_count(c, l, h)
                            act.wait_ge(y_made, k)
                            if l > 1:
                                act.wait_ge(z_made, 2 * (k - 2))
                            act.activation(wide(Y[h]), bank(h, 0), ACT.Copy).then_inc(y_copied, 1)
                    for h in range(2):
                        n = 2 * c + h
                        act.wait_ge(uw_ready, 2 * n + 1)
                        if c:
                            act.wait_ge(v_made, n - 1)
                        act.activation(U[:, h, :], bank(h, 3)[:, 0:B4 * AD], ACT.Copy).then_inc(uw_copied, 1)
                        act.wait_ge(uw_ready, 2 * n + 2)
                        if c:
                            act.wait_ge(ws_ready, n - 1)
                        q = slice(64 * h, 64 * h + 64)
                        act.activation(wide(WT[q]), bank(h, 1)[q], ACT.Copy).then_inc(uw_copied, 1)

            def delta_vector(dve):
                dve.memset(S, 0.0)
                dve.wait_ge(masks, 1)
                dve.drain()
                for c in range(NT):
                    for h in range(2):
                        n = 2 * c + h
                        bb = of_batch(beta, c, h).unsqueeze(2).to_broadcast([P, B4, P])
                        dve.wait_ge(prods, n + 1)
                        dve.tensor_tensor(N[h], b4(bank(h, 2)), over(GT), ALU.mult)
                        dve.tensor_tensor(QK[:, h], b4(bank(h, 3)), over(LE), ALU.mult)
                        dve.drain()
                        dve.wait_ge(decays, 2 * n + 1)
                        dve.tensor_tensor(N[h], N[h], b4(E[h][:, 0, :]), ALU.mult)
                        dve.wait_ge(decays, 2 * n + 2)
                        dve.tensor_tensor(QK[:, h], QK[:, h], b4(E[h][:, 1, :]), ALU.mult).then_inc(qk_made, 1)
                        dve.drain()
                        dve.tensor_tensor(N[h], N[h], bb, ALU.mult).then_inc(n_made, 1)
                    for h in range(2):
                        dve.drain()
                        dve.tensor_tensor(X[h], N[h], over(levels[:, 0, :]), ALU.mult)
                        dve.drain()
                        dve.tensor_tensor(X[h], over(core.ident), X[h], ALU.subtract)
                        dve.wait_ge(nt_copied, 2 * c + h + 1)
                        dve.tensor_tensor(XT[h], NTr[h], over(levelsT[:, 0, :]), ALU.mult)
                        dve.drain()
                        dve.tensor_tensor(XT[h], over(core.ident), XT[h], ALU.subtract).then_inc(x_start, 1)
                    for l in range(1, LEVELS):
                        for h in range(2):
                            k = level_count(c, l, h)
                            dve.wait_ge(z_made, 2 * k - 1)
                            dve.tensor_tensor(wide(X[h]), wide(X[h]), bank(h, 1), ALU.subtract).then_inc(x_up, 1)
                            dve.wait_ge(z_made, 2 * k)
                            dve.tensor_tensor(wide(XT[h]), wide(XT[h]), bank(h, 2), ALU.subtract).then_inc(x_up, 1)
                        dve.drain()
                    for h in range(2):
                        dve.wait_ge(ws_ready, 2 * c + h + 1)
                        dve.tensor_tensor(V[:, h, :], U[:, h, :], bank(h, 3)[:, 0:B4 * AD], ALU.subtract)\
                            .then_inc(v_made, 1)
                    for h in range(2):
                        n = 2 * c + h
                        dve.wait_ge(out_made, 2 * n + 2)
                        q = slice(64 * h, 64 * h + 64)
                        dve.tensor_tensor(S[q], S[q], of_batch(whole, c, h)[q].unsqueeze(2).to_broadcast([64, B4, AD]),
                                          ALU.mult)
                        dve.tensor_copy(O[:, c, 0:512].rearrange("p (r b n) -> p r b n", b=2, n=AD)[:, :, h, :],
                                        bank(h, 0)[:, 0:B4 * AD].rearrange("p (r n) -> p r n", r=B4))
                        dve.drain()
                        dve.tensor_tensor(wide(S[q]), wide(S[q]), bank(h, 2)[q, 0:B4 * AD], ALU.add)\
                            .then_inc(state_up, 1)
            yield dict(pool=delta_pool, pe=delta_tensor, act=delta_scalar, dve=delta_vector)
            delta_end = len(stages)

            core.top = base
            oT = core.take(4, T)
            sqs = core.take(NT, AH * AD)
            osq, ov, oroot, ogain = (sem(f"delta_out_{n}") for n in (
                "squares_ready", "variance_ready", "root_ready", "gained"))
            v, r, a = (t[:, 0:NT * AH] for t in norm_r)
            oturn = turn(O[:, :, 0:512], oT, 4)

            def out_scalar(act):
                act.activation(sqs, O[:, :, 0:512], ACT.Square).then_inc(osq, 1)
                act.wait_ge(ov, 1)
                act.activation(r, v, ACT.Sqrt).then_inc(oroot, 1)

            def out_vector(dve):
                dve.wait_ge(osq, 1)
                for t in range(NT):
                    dve.tensor_reduce(v[:, t * AH:(t + 1) * AH], hd(sqs[:, t, :]), AX.X, ALU.add)
                dve.drain()
                dve.tensor_scalar(v, v, 1.0 / AD, EPS, ALU.mult, ALU.add).then_inc(ov, 1)
                dve.wait_ge(oroot, 1)
                newton_rsqrt(core, dve, v, r, a)
                for t in range(NT):
                    o = hd(O[:, t, 0:512])
                    dve.tensor_tensor(o, o, spread(r[:, t * AH:(t + 1) * AH]), ALU.mult)
                    dve.drain()
                    dve.tensor_tensor(o, o, ngain.unsqueeze(1).to_broadcast([P, AH, AD]), ALU.mult)
                    dve.drain()
                    ins = dve.tensor_tensor(O[:, t, 0:512], O[:, t, 0:512], zt[:, t, :], ALU.mult)
                ins.then_inc(ogain, 1)
                oturn["dve"](dve)

            def out_tensor(pe):
                pe.wait_ge(ogain, 1)
                oturn["pe"](pe)
            yield dict(act=out_scalar, dve=out_vector, pe=out_tensor)
            core.top = mark
            gate = core.take(DC, T)
            core.top = base + 4 * T
            join = project([
                Job("features", columns_of(w2, DC, 256, OFF2["gate_a"]), None, DC, 256, 4,
                         gate_store(gate, col["b_gate_2"][:, 0:8]), source=hT),
                Job("features", columns_of(IN["w_proj_a_2"][0], 4, 512), None, 4, 512, 2,
                         times_store(gated, gate, 4), on="dve", source=oT)])
            join_sp = join["sp"]

            def join_sync(sp):
                core.begin(sp, delta_end)
                join_sp(sp)
            join["sp"] = join_sync
            yield join
            core.top = mark

        def stages_sparse(gated):
            mark = core.top
            SLOTS = 22
            RK, RI, RIK = 8, 12, 20
            v = core.take(NT, BKV * 64)
            iw = core.take(NT, IH)
            inv = core.take(32)
            pos_f = core.take(NT)
            pos_i = core.take(NT)
            sin, cos = core.take(NT, 32), core.take(NT, 32)
            ang, kk, t1 = core.take(NT, 32), core.take(NT, 32), core.take(NT, 32)
            base = core.top
            R = core.take(NT, SLOTS * 64)
            F = core.take(SLOTS // 2, T)
            tmp = core.take(2, 20 * 32)
            heads_of = lambda t, a, b: R[:, t, a * 64:b * 64].rearrange("p (h n) -> p h n", n=64)
            s_pos, s_inv, s_ang, s_trig, pools, s_rot, s_turned, s_copied2 = (
                sem(f"sparse_{n}") for n in ("positions_landed", "frequencies_made", "angles_ready", "sines_ready",
                                             "rotated_part", "rotated", "turned", "copied"))

            def bk_store(eng, i, u, acc, r):
                for h in range(BKV):
                    eng.activation(heads_of(u, RK + 2 * h, RK + 2 * h + 1), acc[:, h * 64:(h + 1) * 64].unsqueeze(1),
                                   ACT.Copy)
                return eng.activation(v[:, u, :], acc[:, 128:256], ACT.Copy)

            def ik_store(eng, i, u, acc, r):
                eng.activation(R[:, u, RIK * 64:(RIK + 1) * 64], acc[:, 0:64], ACT.Copy)
                return eng.activation(iw[:, u, :], acc[:, 64:72], ACT.Copy, scale=float((IH * 64) ** -0.5))
            core.top = base + NT * SLOTS * 64

            before = len(stages)

            def params(sp):
                core.begin(sp, before)
                sp.dma_start(pos_i.bitcast(I32), IN["positions_2"][0].rearrange("(t p) -> p t", p=P),
                             allow_slow_non_contiguous=True).then_inc(s_pos, 16)

            def to_R(column):
                return lambda eng, i, u, acc, r: eng.activation(R[:, u, column + i * 256:column + (i + 1) * 256],
                                                                acc[:, 0:256], ACT.Copy)
            first = project([
                Job("tokens", columns_of(w2, DC, 256, OFF2["b_q"]), None, DC, 256, 2, to_R(0), source=hT),
                Job("tokens", columns_of(w2, DC, 256, OFF2["b_k"]), None, DC, 256, 1, bk_store, source=hT),
                Job("tokens", columns_of(w2, DC, 256, OFF2["i_q"]), None, DC, 256, 2, to_R(RI * 64),
                         source=hT),
                Job("tokens", columns_of(w2, DC, WIDE, OFF2["i_k"]), None, DC, WIDE, 1, ik_store, source=hT)], params)
            core.top = base + NT * SLOTS * 64 + SLOTS // 2 * T + 2 * 20 * 32
            first_dve = first["dve"]
            def freq_pool(gp):
                for i in range(32):
                    gp.memset(inv[:, i:i + 1], float(ROPE_INV[i]))
                gp.drain().then_inc(s_inv, 1)

            def angle_vector(dve):
                dve.wait_ge(s_pos, 16)
                dve.tensor_copy(pos_f, pos_i.bitcast(I32))
                dve.wait_ge(s_inv, 1)
                dve.drain()
                for t in range(NT):
                    dve.tensor_scalar(ang[:, t, :], inv, pos_f[:, t:t + 1], None, ALU.mult)
                dve.drain()
                TWO_PI = 2 * np.pi
                c1 = float(np.float32(6.28125))
                c2 = float(np.float32(TWO_PI - c1))
                c2 = float(np.array(c2, np.float32).view(np.uint32).__and__(0xFFFFF000).astype(np.uint32).view(np.float32))
                c3 = float(np.float32(TWO_PI - c1 - c2))
                MAGIC = 1.5 * 2.0 ** 23
                for dst, shift, edge in ((sin, 0.0, 0.0), (cos, 0.25, np.pi / 2)):
                    dve.tensor_scalar(kk, ang, 1.0 / TWO_PI, shift, ALU.mult, ALU.add)
                    dve.drain()
                    dve.tensor_scalar(kk, kk, MAGIC, None, ALU.add)
                    dve.drain()
                    dve.tensor_scalar(kk, kk, -MAGIC, None, ALU.add)
                    dve.drain()
                    dve.scalar_tensor_tensor(out=dst, in0=kk, scalar=-c1, in1=ang, op0=ALU.mult, op1=ALU.add)
                    dve.drain()
                    dve.scalar_tensor_tensor(out=dst, in0=kk, scalar=-c2, in1=dst, op0=ALU.mult, op1=ALU.add)
                    dve.drain()
                    dve.scalar_tensor_tensor(out=dst, in0=kk, scalar=-c3, in1=dst, op0=ALU.mult, op1=ALU.add)
                    dve.drain()
                    if edge:
                        dve.tensor_scalar(dst, dst, edge, None, ALU.add)
                        dve.drain()
                    dve.tensor_scalar(dst, dst, float(np.float32(3.1415925)), -float(np.float32(3.1415925)),
                                      ALU.min, ALU.max)
                dve.drain().then_inc(s_ang, 1)

            def vector(dve):
                first_dve(dve)
                angle_vector(dve)
            first.update(pool=freq_pool, dve=vector)
            yield first

            def rotate(eng, t, a, b, c, s_, x, y):
                n = b - a
                h = heads_of(t, a, b)
                x1, x2 = h[:, :, 0:32], h[:, :, 32:64]
                cb_ = cos[:, t, :].unsqueeze(1).to_broadcast([P, n, 32])
                sb_ = sin[:, t, :].unsqueeze(1).to_broadcast([P, n, 32])
                xx = x[:, 0:n * 32].rearrange("p (h n) -> p h n", n=32)
                yy = y[:, 0:n * 32].rearrange("p (h n) -> p h n", n=32)
                eng.tensor_tensor(xx, x2, sb_, ALU.mult)
                eng.tensor_tensor(yy, x1, sb_, ALU.mult)
                eng.drain()
                eng.tensor_tensor(x1, x1, cb_, ALU.mult)
                eng.tensor_tensor(x2, x2, cb_, ALU.mult)
                eng.drain()
                eng.tensor_tensor(x1, x1, xx, ALU.subtract)
                eng.tensor_tensor(x2, x2, yy, ALU.add)
                eng.drain()

            tmp2 = core.take(2, 20 * 32)
            MAPS = ((RK + 1, RK), (RK + 3, RK + 2), (RIK + 1, RIK))

            def rot(eng, tiles, buf, name):
                eng.wait_ge(s_trig, 1)
                for t in tiles:
                    for a, b in ((0, 8), (RK, RK + 1), (RK + 2, RK + 3), (RI, RIK + 1)):
                        rotate(eng, t, a, b, cos, sin, buf[:, 0], buf[:, 1])
                    for dst, src in MAPS:
                        eng.tensor_copy(R[:, t, dst * 64:(dst + 1) * 64], R[:, t, src * 64:(src + 1) * 64])
                    eng.drain().then_inc(s_rot if name == "dve" else pools, 1)

            def rot_tensor(pe):
                pe.wait_ge(s_rot, 3)
                pe.wait_ge(pools, 1)
                for c in range(SLOTS // 2):
                    if c >= 8:
                        pe.wait_ge(s_copied2, c - 7)
                    for t in range(NT):
                        mm = nc.tensor.transpose(ps[:, c % 8, t * P:(t + 1) * P], R[:, t, c * P:(c + 1) * P],
                                                 core.ident)
                    mm.then_inc(s_turned, 1)

            def rot_scalar(act):
                act.wait_ge(s_ang, 1)
                act.activation(sin.rearrange("p t n -> p (t n)"), sin.rearrange("p t n -> p (t n)"), ACT.Sin)
                act.activation(cos.rearrange("p t n -> p (t n)"), cos.rearrange("p t n -> p (t n)"), ACT.Sin)
                act.drain().then_inc(s_trig, 1)
                for c in range(SLOTS // 2):
                    act.wait_ge(s_turned, c + 1)
                    act.activation(F[:, c, :], ps[:, c % 8, :], ACT.Copy).then_inc(s_copied2, 1)
            yield dict(act=rot_scalar, pe=rot_tensor, dve=lambda e: rot(e, (0, 1, 2), tmp, "dve"),
                       pool=lambda e: rot(e, (3,), tmp2, "pool"))

            core.top = base
            bias = core.take(NT, T)
            score = core.take(NT, T)
            relu = core.take(2, T)
            best = core.take(8)
            assert core.top <= base + NT * SLOTS * 64
            qF, kF, iqF, ikF = F[:, 0:4], F[:, 4:6], F[:, 6:10], F[:, 10]
            i_scored, i_relu, i_used, i_picked = (sem(f"index_{n}") for n in ("scored", "rectified", "added", "picked"))
            FOUND = -3e38
            IU = [(t, h) for t in range(NT) for h in range(IH)]

            def index_tensor(pe):
                for n, (t, h) in enumerate(IU):
                    p0 = 64 * (h % 2)
                    if n >= 2:
                        pe.wait_ge(i_relu, n - 1)
                    nc.tensor.matmul(ps[:, n % 2, 0:(t + 1) * P], iqF[p0:p0 + 64, h // 2, t * P:(t + 1) * P],
                                     ikF[p0:p0 + 64, 0:(t + 1) * P], start=True, stop=True).then_inc(i_scored, 1)

            def index_scalar(act):
                for n, (t, h) in enumerate(IU):
                    act.wait_ge(i_scored, n + 1)
                    if n >= 2:
                        act.wait_ge(i_used, n - 1)
                    act.activation(relu[:, n % 2, 0:(t + 1) * P], ps[:, n % 2, 0:(t + 1) * P], ACT.Relu)\
                        .then_inc(i_relu, 1)

            def index_vector(dve):
                for n, (t, h) in enumerate(IU):
                    k = (t + 1) * P
                    sc = score[:, t, 0:k]
                    dve.wait_ge(i_relu, n + 1)
                    if h == 0:
                        dve.tensor_scalar(sc, relu[:, n % 2, 0:k], iw[:, t, 0:1], None, ALU.mult).then_inc(i_used, 1)
                    else:
                        dve.drain()
                        dve.scalar_tensor_tensor(out=sc, in0=relu[:, n % 2, 0:k], scalar=iw[:, t, h:h + 1], in1=sc,
                                                 op0=ALU.mult, op1=ALU.add).then_inc(i_used, 1)
                    if h < IH - 1:
                        continue
                    dve.drain()
                    dve.memset(score[0:CAUSAL, t, k - CAUSAL:k], NEG)
                    dve.drain()
                    if k <= TOPK:
                        dve.tensor_scalar(bias[:, t, 0:k], sc, NEG / 2, NEG, ALU.is_le, ALU.mult)
                        continue
                    for _ in range(TOPK // 8):
                        dve.max(best, sc)
                        dve.drain()
                        dve.match_replace(out=sc, in_to_replace=best, in_values=sc, imm_value=FOUND)
                        dve.drain()
                    dve.tensor_scalar(bias[:, t, 0:k], sc, FOUND / 2, NEG, ALU.is_gt, ALU.mult)
            yield dict(pe=index_tensor, act=index_scalar, dve=index_vector)

            U = BH * NT
            core.top = base + NT * SLOTS * 64 + SLOTS // 2 * T
            o = core.take(NT, BH * 64)
            s, pr, pt = core.take(3, T), core.take(3, T), core.take(2, T)
            shift, total, den = (core.take(U) for _ in range(3))
            (scores_ready, scores_read, shift_ready, probs_ready, probs_turned, turned_copied, out_ready,
             out_stored) = mix_sems
            U0 = (HEADS + X_HEADS) * NT
            units = [(t, h) for t in range(NT) for h in range(BH)]

            def tensor(pe):
                for u in range(U + 3):
                    if u < U:
                        t, h = units[u]
                        p0 = 64 * (h % 2)
                        if u >= 3:
                            pe.wait_ge(scores_read, U0 + u - 2)
                        nc.tensor.matmul(ps[:, u % 3, 0:(t + 1) * P], qF[p0:p0 + 64, h // 2, t * P:(t + 1) * P],
                                         kF[p0:p0 + 64, h // 4, 0:(t + 1) * P], start=True, stop=True)\
                            .then_inc(scores_ready, 1)
                    if 2 <= u <= U + 1:
                        n = u - 2
                        t, h = units[n]
                        pe.wait_ge(probs_ready, U0 + n + 1)
                        if n >= 2:
                            pe.wait_ge(turned_copied, U0 + n - 1)
                        for k in range(t + 1):
                            mm = nc.tensor.transpose(ps[:, 3 + n % 2, k * P:(k + 1) * P],
                                                     pr[:, n % 3, k * P:(k + 1) * P], core.ident)
                        mm.then_inc(probs_turned, 1)
                    if u >= 3:
                        n = u - 3
                        t, h = units[n]
                        pe.wait_ge(turned_copied, U0 + n + 1)
                        if n >= 2:
                            pe.wait_ge(out_stored, U0 + n - 1)
                        for k in range(t + 1):
                            mm = nc.tensor.matmul(ps[:, 5 + n % 2, 0:64], pt[:, n % 2, k * P:(k + 1) * P],
                                                  v[:, k, (h // 4) * 64:(h // 4 + 1) * 64],
                                                  start=k == 0, stop=k == t)
                        mm.then_inc(out_ready, 1)

            def vector(dve):
                for u in range(U + 3):
                    if u < U:
                        t, h = units[u]
                        n = (t + 1) * P
                        dve.wait_ge(scores_ready, U0 + u + 1)
                        if u >= 3:
                            dve.wait_ge(probs_ready, U0 + u - 2)
                        dve.scalar_tensor_tensor(out=s[:, u % 3, 0:n], in0=ps[:, u % 3, 0:n], scalar=64 ** -0.5,
                                                 in1=bias[:, t, 0:n], op0=ALU.mult, op1=ALU.add)\
                            .then_inc(scores_read, 1)
                        dve.drain()
                        dve.tensor_reduce(shift[:, u:u + 1], s[:, u % 3, 0:n], AX.X, ALU.max, negate=True)\
                            .then_inc(shift_ready, 1)
                    if u >= 3:
                        n = u - 3
                        t, h = units[n]
                        dve.wait_ge(probs_ready, U0 + n + 1)
                        dve.reciprocal(den[:, n:n + 1], total[:, n:n + 1])
                        dve.drain()
                        dve.wait_ge(out_ready, U0 + n + 1)
                        dve.tensor_scalar(o[:, t, h * 64:(h + 1) * 64], ps[:, 5 + n % 2, 0:64], den[:, n:n + 1],
                                          None, ALU.mult).then_inc(out_stored, 1)

            def scalar(act):
                for u in range(U + 2):
                    if u < U:
                        t, h = units[u]
                        n = (t + 1) * P
                        act.wait_ge(shift_ready, U0 + u + 1)
                        if u >= 3:
                            act.wait_ge(probs_turned, U0 + u - 2)
                        act.activation(pr[:, u % 3, 0:n], s[:, u % 3, 0:n], ACT.Exp, bias=shift[:, u:u + 1],
                                       accum_out=total[:, u:u + 1]).then_inc(probs_ready, 1)
                    if u >= 2:
                        n = u - 2
                        t, h = units[n]
                        act.wait_ge(probs_turned, U0 + n + 1)
                        if n >= 2:
                            act.wait_ge(out_ready, U0 + n - 1)
                        act.activation(pt[:, n % 2, 0:(t + 1) * P], ps[:, 3 + n % 2, 0:(t + 1) * P], ACT.Copy)\
                            .then_inc(turned_copied, 1)
            yield dict(pe=tensor, dve=vector, act=scalar)
            core.top = base
            oT = core.take(4, T)
            gate = core.take(DC, T)
            yield turn(o, oT, 4)
            scratch = core.take(2, T)
            yield project([
                Job("features", columns_of(w2, DC, 256, OFF2["gate_b"]), None, DC, 256, 4,
                         gate_store(gate, col["b_gate_2"][:, 8:16]), source=hT),
                Job("features", columns_of(IN["w_proj_b_2"][0], 4, 512), None, 4, 512, 2,
                         add_times_store(gated, gate, scratch, 4), on="dve", source=oT),
                Job("features", columns_of(IN["w_out_2"][0], DC, 256), None, DC, 256, 4, add_store(xT),
                         on="dve", source=gated, needs=True)])
            core.top = mark

        def stages_moe():
            mark = core.top
            yield feature_norm(core, 0, xT, col["norm2_g_2"], hT)
            core.top = mark
            LG = EG + EXPERTS
            share = core.take(EXPERTS, T)
            above = core.top
            groupT, expertT = core.take(T), core.take(T)
            logit = core.take(NT, LG)
            rb = core.take(LG)
            comb = core.take(NT, EXPERTS)
            pick = core.take(EXPERTS, P)
            pickR, combT = core.take_pair(EXPERTS // 2, P), core.take_pair(1, T)
            picked = sem("router_picks_made")
            g4, e4, one1, one2, rem, tmp = (core.take(NT, EG) for _ in range(6))
            el16, mm1, mm2, sm = core.take(NT, EXPERTS), core.take(NT), core.take(NT), core.take(NT)
            s_rb, s_arg, s_exp, s_comb, s_ct, s_ctc, s_sh, s_shc = (
                sem(f"router_{n}") for n in ("bias_landed", "logits_shifted", "exponentials", "weights_made",
                                             "weights_turned", "weights_copied", "shares_made",
                                             "shares_stored"))
            s_lt = sem("router_logits_turned")
            wg = IN["w_router_group_2"][0].rearrange("(k p) n -> p k n", p=P)
            we = IN["w_router_expert_2"][0].rearrange("(k p) n -> p k n", p=P)
            before = len(stages)

            def params(sp):
                core.begin(sp, before)
                sp.dma_start(rb[:, 0:EG], broadcast(IN["b_router_group_2"], EG)).then_inc(s_rb, 16)
                sp.dma_start(rb[:, EG:LG], broadcast(IN["b_router_expert_2"], EXPERTS)).then_inc(s_rb, 16)

            first = project([
                Job("features", lambda i, r: wg, None, DC, EG, 1,
                    lambda eng, i, u, acc, r: eng.activation(groupT[0:EG, :], acc[0:EG, :], ACT.Copy), source=hT),
                Job("features", lambda i, r: we, None, DC, EXPERTS, 1,
                    lambda eng, i, u, acc, r: eng.activation(expertT[0:EXPERTS, :], acc[0:EXPERTS, :], ACT.Copy),
                    source=hT)], params)
            yield first

            def row_max(dve, dst, src):
                dve.tensor_reduce(dst, src, AX.X, ALU.max)
                dve.drain()

            def along(t):
                return t.unsqueeze(2).to_broadcast([P, NT, EG])

            def first_of(dve, one, src, top):
                dve.tensor_tensor(one, src, along(top), ALU.is_equal)
                dve.memset(rem[:, :, 0], 1.0)
                dve.drain()
                for j in range(EG):
                    if j:
                        dve.tensor_tensor(rem[:, :, 0], rem[:, :, 0], one[:, :, j - 1], ALU.subtract)
                        dve.drain()
                        dve.tensor_tensor(one[:, :, j], one[:, :, j], rem[:, :, 0], ALU.mult)
                        dve.drain()

            def router_vector(dve):
                dve.wait_ge(s_rb, 32)
                dve.wait_ge(s_lt, 1)
                for t in range(NT):
                    dve.tensor_tensor(logit[:, t, 0:EG], ps[:, 5, t * P:t * P + EG], rb[:, 0:EG], ALU.add)
                    dve.tensor_tensor(logit[:, t, EG:LG], ps[:, 6, t * P:t * P + EXPERTS], rb[:, EG:LG], ALU.add)
                dve.drain()
                dve.tensor_copy(g4, logit[:, :, 0:EG])
                dve.drain()
                row_max(dve, mm1, g4)
                first_of(dve, one1, g4, mm1)
                dve.tensor_tensor(g4, g4, along(mm1), ALU.subtract)
                dve.tensor_tensor(el16.rearrange("p t (g k) -> p t g k", g=EG),
                                  logit[:, :, EG:LG].rearrange("p t (g k) -> p t g k", g=EG),
                                  one1.unsqueeze(3).to_broadcast([P, NT, EG, EG]), ALU.mult)
                dve.drain()
                dve.tensor_reduce(e4, el16.rearrange("p t (g k) -> p t k g", g=EG), AX.X, ALU.add)
                dve.drain()
                row_max(dve, mm2, e4)
                dve.tensor_tensor(e4, e4, along(mm2), ALU.subtract)
                dve.drain().then_inc(s_arg, 1)
                dve.wait_ge(picked, 1)
                half = EXPERTS // 2
                dve.tensor_copy(pickR.hi, pick[:, 0:half, :])
                dve.tensor_copy(pickR.lo, pick[:, half:, :])
                dve.wait_ge(s_exp, 1)
                dve.tensor_reduce(mm1, g4, AX.X, ALU.add)
                dve.tensor_reduce(mm2, e4, AX.X, ALU.add)
                dve.drain()
                dve.reciprocal(mm1, mm1)
                dve.reciprocal(mm2, mm2)
                dve.drain()
                dve.tensor_tensor(e4, e4, along(mm2), ALU.mult)
                dve.drain()
                row_max(dve, sm, e4)
                first_of(dve, g4, e4, sm)
                dve.scalar_tensor_tensor(out=tmp, in0=g4, scalar=-2.0, in1=e4, op0=ALU.mult, op1=ALU.add)
                dve.drain()
                row_max(dve, sm, tmp)
                first_of(dve, one2, tmp, sm)
                dve.tensor_tensor(one2, one2, g4, ALU.add)
                dve.drain()
                dve.tensor_tensor(e4, e4, one2, ALU.mult)
                dve.drain()
                dve.tensor_reduce(sm, e4, AX.X, ALU.add)
                dve.drain()
                dve.reciprocal(sm, sm)
                dve.drain()
                dve.tensor_tensor(sm, sm, mm1, ALU.mult)
                dve.drain()
                dve.tensor_tensor(e4, e4, along(sm), ALU.mult)
                dve.drain()
                for gi in range(EG):
                    dve.tensor_tensor(comb[:, :, gi * EG:(gi + 1) * EG], e4,
                                      one1[:, :, gi:gi + 1].to_broadcast([P, NT, EG]), ALU.mult)
                dve.drain().then_inc(s_comb, 1)
                dve.wait_ge(s_ct, 1)
                dve.tensor_copy(combT.hi[0:EXPERTS, 0, :], ps[0:EXPERTS, 4, :])
                dve.drain()
                dve.tensor_tensor(combT.lo[0:EXPERTS, 0, :], ps[0:EXPERTS, 4, :],
                                  combT.hi[0:EXPERTS, 0, :].bitcast(F32), ALU.subtract).then_inc(s_ctc, 1)

            def router_scalar(act):
                act.wait_ge(s_arg, 1)
                act.activation(g4, g4, ACT.Exp)
                act.activation(e4, e4, ACT.Exp)
                act.drain().then_inc(s_exp, 1)

            def router_tensor(pe):
                for t in range(NT):
                    nc.tensor.transpose(ps[:, 5, t * P:t * P + EG], groupT[0:EG, t * P:(t + 1) * P],
                                        core.ident[0:EG, 0:EG])
                    mm = nc.tensor.transpose(ps[:, 6, t * P:t * P + EXPERTS], expertT[0:EXPERTS, t * P:(t + 1) * P],
                                             core.ident[0:EXPERTS, 0:EXPERTS])
                mm.then_inc(s_lt, 1)
                pe.wait_ge(s_comb, 1)
                for t in range(NT):
                    mm = nc.tensor.transpose(ps[0:EXPERTS, 4, t * P:(t + 1) * P], comb[:, t, :], core.ident)
                mm.then_inc(s_ct, 1)

            def router_pool(gp):
                gp.memset(pick, 1.0)
                gp.drain()
                gp.affine_select(out=pick, in_=pick, compare_op=ALU.is_equal, fill=0.0, base=0,
                                 pattern=[[-1, EXPERTS], [0, P]], channel_multiplier=1).then_inc(picked, 1)
            yield dict(dve=router_vector, act=router_scalar, pe=router_tensor, pool=router_pool)
            def share_tensor(pe):
                for e in range(EXPERTS):
                    if e >= 4:
                        pe.wait_ge(s_shc, e - 3)
                    row_e = (pickR.hi, pickR.lo)[e // (EXPERTS // 2)][0:EXPERTS, e % (EXPERTS // 2), :]
                    nc.tensor.matmul(ps[:, 4 + e % 4, :], row_e, combT.lo[0:EXPERTS, 0, :], start=True, stop=False)
                    nc.tensor.matmul(ps[:, 4 + e % 4, :], row_e, combT.hi[0:EXPERTS, 0, :],
                                     start=False, stop=True).then_inc(s_sh, 1)

            def share_vector(dve):
                for e in range(EXPERTS):
                    dve.wait_ge(s_sh, e + 1)
                    dve.tensor_copy(share[:, e, :], ps[:, 4 + e % 4, :]).then_inc(s_shc, 1)
            yield dict(pe=share_tensor, dve=share_vector)

            core.top = above
            expT, hP, weights = core.take_pair(DC, T), core.take_pair(DC, T), core.take_pair(2, Project.SLOT)
            core.top = mark
            silu = hT[:, 0:4, :].rearrange("p (s c) t -> p s c t", s=2)
            made = hT[:, 4:6, :]
            PER = EXPERTS // ROUNDS
            w1v = IN["w_exp_gate_2"][0].rearrange("(r e) (k p) n -> r e p k n", p=P, r=ROUNDS)
            w3v = IN["w_exp_up_2"][0].rearrange("(r e) (k p) n -> r e p k n", p=P, r=ROUNDS)

            def expert(e):
                def weights_of(v):
                    return lambda i, r: v[bass.ds(r, 1), e].rearrange("a p k n -> (a p) k n")

                def silu_store(eng, i, u, acc, r):
                    return eng.activation(silu[:, e % 2, u, :], acc, ACT.Silu)

                def up_store(eng, i, u, acc, r):
                    c = 2 * e + u
                    eng.tensor_tensor(made[:, u, :], acc, silu[:, e % 2, u, :], ALU.mult)
                    eng.drain()
                    one = share[:, bass.ds(r * PER + e, 1), :].rearrange("p a n -> p (a n)")
                    eng.tensor_tensor(made[:, u, :], made[:, u, :], one, ALU.mult)
                    eng.drain()
                    eng.tensor_copy(expT.hi[:, c, :], made[:, u, :])
                    eng.drain()
                    return eng.tensor_tensor(expT.lo[:, c, :], made[:, u, :], expT.hi[:, c, :].bitcast(F32),
                                             ALU.subtract)
                return [Job("features", weights_of(w1v), hP, DC, DE, 1, silu_store),
                        Job("features", weights_of(w3v), hP, DC, DE, 1, up_store, on="dve",
                                 with_last=True)]
            yield Project(core, weights, [j for e in range(PER) for j in expert(e)] +
                               [down(IN["w_exp_down_2"][0].rearrange("e f n -> (e f) n"), expT)],
                               repeat=ROUNDS, start=(hP, hT, DC)).programs()

        def stages_store():
            mark = core.top
            yield feature_norm(core, 0, xT, col["final_norm_g_2"], hT)
            core.top = mark
            final = core.take(NT, D)
            f_turned, f_copied = sem("result_turned"), sem("result_copied")

            def tensor(pe):
                for c in range(DC):
                    for t in range(NT):
                        mm = nc.tensor.transpose(ps[:, c, t * P:(t + 1) * P], hT[:, c, t * P:(t + 1) * P], core.ident)
                    mm.then_inc(f_turned, 1)

            def vector(dve):
                for c in range(0, DC, 2):
                    dve.wait_ge(f_turned, c + 1)
                    dve.tensor_copy(final[:, :, c * P:(c + 1) * P], ps[:, c, :].rearrange("p (t n) -> p t n", t=NT))

            def scalar(act):
                for c in range(1, DC, 2):
                    act.wait_ge(f_turned, c + 1)
                    act.activation(final[:, :, c * P:(c + 1) * P], ps[:, c, :].rearrange("p (t n) -> p t n", t=NT),
                                   ACT.Copy)
            yield dict(pe=tensor, dve=vector, act=scalar)
            before = len(stages)

            def sync(sp):
                core.begin(sp, before)
                for t in range(NT):
                    sp.dma_start(out[0, t * P:(t + 1) * P, :], final[:, t, :]).then_inc(s_out, 16)
                sp.wait_ge(s_out, 16 * NT)
            yield dict(sp=sync)

        stages = []
        run = stages.append
        run(stage_load())
        run(feature_norm(core, 1, xT, col["norm_mix"], hT))
        dt_raw = core.take(NT * 2 * SSD_HEADS)
        merged_at = core.top
        merged = core.take(DC, T)
        mark2 = core.top
        proj_qkv, attention, attn = stage_attention()
        run(proj_qkv)
        run(attention)
        mark = core.top
        attnT = core.take(DC, T)
        gate = core.take(DC, T)
        run(turn(attn, attnT, DC))
        w1 = IN["w_in"][0]
        run(project([
            Job("features", columns_of(w1, DC, 256, OFF_GATE), None, DC, 256, 4, gate_store(gate), source=hT),
            Job("features", columns_of(IN["w_attn_branch"][0], DC, 256), None, DC, 256, 4,
                     times_store(merged, gate), on="dve", source=attnT)]))
        core.top = mark2
        for st in stages_ssd():
            run(st)
        core.top = mark2 = core.top - DC * T
        for st in stages_cross():
            run(st)
        for st in stages_ffn():
            run(st)
        run(feature_norm(core, 0, xT, col["norm1_g_2"], hT))
        merged2 = core.take(DC, T)
        for st in stages_delta(merged2):
            run(st)
        for st in stages_sparse(merged2):
            run(st)
        core.top = mark2
        for st in stages_moe():
            run(st)
        core.top = mark2
        for st in stages_store():
            run(st)

        if debug:
            dbg = sem("debug_stored")
            def dump(sp):
                n = 0
                for name, buf in dict(merged=merged, hT=hT, xT=xT, merged2=merged2).items():
                    if name in debug:
                        sp.dma_start(debug[name].rearrange("(c p) t -> p c t", p=P), buf).then_inc(dbg, 16)
                        n += 1
                sp.wait_ge(dbg, 16 * n)

        def program(eng, name):
            for n, st in enumerate(stages):
                if name != "sp":
                    core.begin(eng, n)
                if name in st:
                    st[name](eng)
                if name != "sp":
                    core.finish(eng, name)

        with nc.Block() as block:
            @block.sync
            def _(sp):
                program(sp, "sp")
                core.begin(sp, len(stages))
                if debug:
                    dump(sp)

            @block.tensor
            def _(pe):
                program(pe, "pe")

            @block.vector
            def _(dve):
                program(dve, "dve")

            @block.scalar
            def _(act):
                program(act, "act")

            @block.gpsimd
            def _(gp):
                program(gp, "pool")


_DEBUG = {}


def kernel(**inputs):
    from concourse import bacc
    from concourse.bass_utils import run_bass_kernel_spmd

    nc = bacc.Bacc("TRN2", target_bir_lowering=False, num_devices=1)
    arrays, IN = {}, {}
    for name, value in inputs.items():
        a = np.ascontiguousarray(value)
        arrays[f"in_{name}"] = a
        IN[name] = nc.dram_tensor(f"in_{name}", a.shape, mybir.dt.from_np(a.dtype), kind="ExternalInput").ap()
    out = nc.dram_tensor("out", (1, T, D), F32, kind="ExternalOutput").ap()
    debug = {n: nc.dram_tensor(f"debug_{n}", shape, F32, kind="ExternalOutput").ap() for n, shape in _DEBUG.items()}
    mixer_kernel(nc, IN, out, debug)
    r = run_bass_kernel_spmd(nc, [arrays], core_ids=[0])
    got = r.results[0]["out"]
    if _DEBUG:
        return (got,) + tuple(r.results[0][f"debug_{n}"] for n in _DEBUG)
    return got
```
